# Optimizing a Trainium2 kernel written in Bass

```python
import math
import jax
import jax.numpy as jnp
from jax import lax
import numpy as np

D_MODEL = 1024
BATCH = 1
SEQ = 128
DEPTH = 2
DEC_BATCH = 1
DEC_SEQ = 256
PAST_LEN = 128

GRID_W = 64
N_BRANCH = 4
BRANCH_W = D_MODEL // 4
HEAD_DIM = 64
Q_BLOCK = 128
NA_HEADS = BRANCH_W // HEAD_DIM
NA_WIN_R = 8
NA_WIN_C = 16
SWA_HEADS = BRANCH_W // HEAD_DIM
SWA_KV_HEADS = SWA_HEADS // 2
SWA_WINDOW = 128
SWA_BLOCK = 128
HY_WIDTH = BRANCH_W
HY_ORDER = 2
HY_FREQS = 16
HY_EMB = 1 + 2 * HY_FREQS
HY_HIDDEN = 64
HY_MIN_DECAY = 3.07
HY_MAX_DECAY = 15.35
DIFF_HD = 32
DIFF_HEADS = BRANCH_W // (2 * DIFF_HD)
D_FF = 128 * ((8 * D_MODEL // 3 + 127) // 128)
ROPE_BASE = 10000.0
EPS = 1e-6
NEG = -1e30
N_MOD = 9
NA_W = 3 * NA_HEADS * HEAD_DIM
SWA_QW = SWA_HEADS * HEAD_DIM
SWA_KVW = SWA_KV_HEADS * HEAD_DIM
SWA_W = SWA_QW + 2 * SWA_KVW
HY_IN_W = 3 * HY_WIDTH
DIFF_W = 3 * DIFF_HEADS * 2 * DIFF_HD
GATE_W = N_BRANCH * D_MODEL
SPLIT_IDX = (NA_W, NA_W + SWA_W, NA_W + SWA_W + HY_IN_W, NA_W + SWA_W + HY_IN_W + DIFF_W)
IN_W = SPLIT_IDX[-1] + GATE_W

kernel_name = 'hybrid_diffusion_trunk_step'

F32 = jnp.float32

def rmsnorm(x, g):
    xf = x.astype(F32)
    y = xf * lax.rsqrt(jnp.mean(xf * xf, axis=-1, keepdims=True) + EPS)
    return (y * g.astype(F32)).astype(x.dtype)

def swiglu(h, w1, w3, w2):
    return (jax.nn.silu(h @ w1) * (h @ w3)) @ w2

def to_heads(t, n):
    B, L, _ = t.shape
    return t.reshape(B, L, n, -1).transpose(0, 2, 1, 3)

def from_heads(t):
    B, H, L, d = t.shape
    return t.transpose(0, 2, 1, 3).reshape(B, L, H * d)

def expand_kv(t):
    return jnp.repeat(t, SWA_HEADS // SWA_KV_HEADS, axis=1)

def rope_tables(L, dh):
    nf = dh // 4
    t = jnp.arange(L)
    freqs = ROPE_BASE ** (-jnp.arange(nf, dtype=F32) / nf)
    ang_r = (t // GRID_W).astype(F32)[:, None] * freqs
    ang_c = (t % GRID_W).astype(F32)[:, None] * freqs
    return (jnp.cos(ang_r), jnp.sin(ang_r), jnp.cos(ang_c), jnp.sin(ang_c))

def apply_rope(x, tabs):
    cr, sr, cc, sc = tabs
    nf = x.shape[-1] // 4
    xf = x.astype(F32)

    def rot(xa, cos, sin):
        a, b = xa[..., :nf], xa[..., nf:]
        return jnp.concatenate([a * cos - b * sin, b * cos + a * sin], axis=-1)

    half = 2 * nf
    out = jnp.concatenate([rot(xf[..., :half], cr, sr), rot(xf[..., half:], cc, sc)], axis=-1)
    return out.astype(x.dtype)

def rope_pair(x, tabs):
    return jnp.concatenate([apply_rope(x[..., :DIFF_HD], tabs), apply_rope(x[..., DIFF_HD:], tabs)], axis=-1)

def dense_attention(q, k, v, sink):
    B, H, Lq, d = q.shape
    nb = Lq // Q_BLOCK
    scale = d ** -0.5
    qb = jnp.moveaxis(q.reshape(B, H, nb, Q_BLOCK, d), 2, 0)

    def block(qi):
        s = jnp.einsum('bhqd,bhkd->bhqk', qi, k).astype(F32) * scale
        if sink is None:
            p = jax.nn.softmax(s, axis=-1)
        else:
            s_sink = jnp.broadcast_to(sink.astype(F32)[None, :, None, None], s.shape[:-1] + (1,))
            p = jax.nn.softmax(jnp.concatenate([s, s_sink], axis=-1), axis=-1)[..., :-1]
        return jnp.einsum('bhqk,bhkd->bhqd', p.astype(v.dtype), v)

    o = lax.map(block, qb)
    return jnp.moveaxis(o, 0, 2).reshape(B, H, Lq, v.shape[-1])

def diff_attention(q, k, v, lam):
    B, H, Lq, _ = q.shape
    Lk = k.shape[2]
    nb = Lq // Q_BLOCK
    scale = DIFF_HD ** -0.5
    qb = jnp.moveaxis(q.reshape(B, H, nb, Q_BLOCK, 2, DIFF_HD), 2, 0)
    kk = k.reshape(B, H, Lk, 2, DIFF_HD)

    def block(qi):
        s = jnp.einsum('bhqmd,bhkmd->bhmqk', qi, kk).astype(F32) * scale
        p = jax.nn.softmax(s, axis=-1)
        a = p[:, :, 0] - lam * p[:, :, 1]
        return jnp.einsum('bhqk,bhkd->bhqd', a.astype(v.dtype), v)

    o = lax.map(block, qb)
    return jnp.moveaxis(o, 0, 2).reshape(B, H, Lq, v.shape[-1])

def neighbourhood_attention(q, k, v, kc, vc, rpb):
    B, H, L, d = q.shape
    R = L // GRID_W
    kh = min(NA_WIN_R, R)
    scale = d ** -0.5
    qg = q.reshape(B, H, R, GRID_W, d)
    r = jnp.arange(R)
    rows = jnp.clip(r - kh // 2, 0, R - kh)[:, None] + jnp.arange(kh)[None, :]
    k_win = k.reshape(B, H, R, GRID_W, d)[:, :, rows]
    v_win = v.reshape(B, H, R, GRID_W, d)[:, :, rows]
    col = jnp.arange(GRID_W)
    c0 = jnp.clip(col - NA_WIN_C // 2, 0, GRID_W - NA_WIN_C)
    col_ok = (col[None, :] >= c0[:, None]) & (col[None, :] < c0[:, None] + NA_WIN_C)
    d_row = rows - r[:, None] + (NA_WIN_R - 1)
    d_col = jnp.clip(col[None, :] - col[:, None] + (NA_WIN_C - 1), 0, 2 * NA_WIN_C - 2)
    bias = rpb.astype(F32)[:, d_row[:, None, :, None], d_col[None, :, None, :]]
    s = jnp.einsum('bhrqd,bhrjkd->bhrqjk', qg, k_win).astype(F32) * scale + bias[None]
    s = jnp.where(col_ok[:, None, :], s, NEG).reshape(B, H, R, GRID_W, kh * GRID_W)
    s_ctx = jnp.einsum('bhrqd,bhcd->bhrqc', qg, kc).astype(F32) * scale
    p = jax.nn.softmax(jnp.concatenate([s, s_ctx], axis=-1), axis=-1).astype(v.dtype)
    nw = kh * GRID_W
    p_win = p[..., :nw].reshape(B, H, R, GRID_W, kh, GRID_W)
    o = jnp.einsum('bhrqjk,bhrjkd->bhrqd', p_win, v_win) + jnp.einsum('bhrqc,bhcd->bhrqd', p[..., nw:], vc)
    return o.reshape(B, H, L, d)

def window_attention(q, k, v, kc, vc, sink):
    B, H, L, d = q.shape
    nb = L // SWA_BLOCK
    scale = d ** -0.5
    pad = ((0, 0), (0, 0), (SWA_BLOCK, SWA_BLOCK), (0, 0))

    def band(t):
        tb = jnp.pad(t, pad).reshape(B, H, nb + 2, SWA_BLOCK, d)
        return jnp.concatenate([tb[:, :, :-2], tb[:, :, 1:-1], tb[:, :, 2:]], axis=3)

    k_b, v_b = band(k), band(v)
    qb = q.reshape(B, H, nb, SWA_BLOCK, d)
    q_pos = jnp.arange(nb)[:, None] * SWA_BLOCK + jnp.arange(SWA_BLOCK)[None, :]
    k_pos = jnp.arange(nb)[:, None] * SWA_BLOCK - SWA_BLOCK + jnp.arange(3 * SWA_BLOCK)[None, :]
    kp = k_pos[:, None, :]
    ok = (kp >= 0) & (kp < L) & (jnp.abs(kp - q_pos[:, :, None]) <= SWA_WINDOW)
    s = jnp.einsum('bhnqd,bhnkd->bhnqk', qb, k_b).astype(F32) * scale
    s = jnp.where(ok, s, NEG)
    s_ctx = jnp.einsum('bhnqd,bhcd->bhnqc', qb, kc).astype(F32) * scale
    s_sink = jnp.broadcast_to(sink.astype(F32)[None, :, None, None, None], (B, H, nb, SWA_BLOCK, 1))
    p = jax.nn.softmax(jnp.concatenate([s, s_ctx, s_sink], axis=-1), axis=-1).astype(v.dtype)
    nk = 3 * SWA_BLOCK
    Lc = kc.shape[2]
    o = jnp.einsum('bhnqk,bhnkd->bhnqd', p[..., :nk], v_b) + jnp.einsum('bhnqc,bhcd->bhnqd', p[..., nk:nk + Lc], vc)
    return o.reshape(B, H, L, d)

def hyena_filters(L, lp):
    tn = jnp.arange(L, dtype=F32) / L
    ang = 2.0 * math.pi * tn[:, None] * jnp.arange(1, HY_FREQS + 1, dtype=F32)[None, :]
    z = jnp.concatenate([tn[:, None], jnp.cos(ang), jnp.sin(ang)], axis=-1)
    w = lp['hy_sin_freq'].astype(F32)
    g = jnp.sin(w * (z @ lp['hy_w1'].astype(F32) + lp['hy_b1'].astype(F32)))
    g = jnp.sin(w * (g @ lp['hy_w2'].astype(F32) + lp['hy_b2'].astype(F32)))
    hfil = (g @ lp['hy_w3'].astype(F32)).reshape(L, HY_ORDER, 2, HY_WIDTH)
    rate = jnp.exp(lp['hy_log_decay'].astype(F32)).reshape(HY_ORDER, 2, HY_WIDTH)
    hfil = hfil * jnp.exp(-rate[None] * tn[:, None, None, None])
    full = jnp.concatenate([hfil[:, :, 0], jnp.zeros((1, HY_ORDER, HY_WIDTH), F32), hfil[1:, :, 1][::-1]], axis=0)
    return full / (jnp.sum(jnp.abs(full), axis=0, keepdims=True) + EPS)

def hyena(u, lp):
    B, L, _ = u.shape
    w = lp['hy_short_w']
    up = jnp.pad(u, ((0, 0), (1, 1), (0, 0)))
    z = up[:, :L] * w[0] + up[:, 1:L + 1] * w[1] + up[:, 2:] * w[2] + lp['hy_short_b']
    v, x1, x2 = jnp.split(z, 3, axis=-1)
    filt_f = jnp.fft.rfft(hyena_filters(L, lp), axis=0)
    y = v.astype(F32)
    for o, gate in enumerate((x1, x2)):
        yf = jnp.fft.rfft(y, n=2 * L, axis=1)
        conv = jnp.fft.irfft(yf * filt_f[None, :, o], n=2 * L, axis=1)[:, :L]
        y = gate.astype(F32) * (conv + lp['hy_skip'][o].astype(F32) * y)
    return y.astype(u.dtype)

def token_mixing(h, lp, l, ctx_cache):
    B, L, _ = h.shape
    proj = h @ lp['w_in']
    na_in, swa_in, hy_in, diff_in, gate_in = jnp.split(proj, list(SPLIT_IDX), axis=-1)
    na_q, na_k, na_v = [to_heads(t, NA_HEADS) for t in jnp.split(na_in, 3, axis=-1)]
    swa_q = to_heads(swa_in[..., :SWA_QW], SWA_HEADS)
    swa_k = to_heads(swa_in[..., SWA_QW:SWA_QW + SWA_KVW], SWA_KV_HEADS)
    swa_v = to_heads(swa_in[..., SWA_QW + SWA_KVW:], SWA_KV_HEADS)
    d_q, d_k, d_v = [to_heads(t, DIFF_HEADS) for t in jnp.split(diff_in, 3, axis=-1)]
    lam_init = 0.8 - 0.6 * math.exp(-0.3 * l)
    lvec = lp['diff_lambda'].astype(F32)
    lam = jnp.exp(jnp.sum(lvec[0] * lvec[1])) - jnp.exp(jnp.sum(lvec[2] * lvec[3])) + lam_init
    sink = lp['swa_sink']
    if ctx_cache is None:
        a_o = dense_attention(na_q, na_k, na_v, None)
        b_o = dense_attention(swa_q, expand_kv(swa_k), expand_kv(swa_v), sink)
        d_o = diff_attention(d_q, d_k, d_v, lam)
        ctx_out = (na_k, na_v, swa_k, swa_v, d_k, d_v)
    else:
        ck_na, cv_na, ck_swa, cv_swa, ck_d, cv_d = ctx_cache
        a_o = neighbourhood_attention(na_q, na_k, na_v, ck_na, cv_na, lp['na_rpb'])
        tabs = rope_tables(L, HEAD_DIM)
        b_o = window_attention(apply_rope(swa_q, tabs), expand_kv(apply_rope(swa_k, tabs)), expand_kv(swa_v),
                               expand_kv(ck_swa), expand_kv(cv_swa), sink)
        tabs_d = rope_tables(L, DIFF_HD)
        d_o = diff_attention(rope_pair(d_q, tabs_d), jnp.concatenate([rope_pair(d_k, tabs_d), ck_d], axis=2),
                             jnp.concatenate([d_v, cv_d], axis=2), lam)
        ctx_out = None
    d_o = rmsnorm(d_o, lp['diff_subln']) * (1.0 - lam_init)
    c_o = hyena(hy_in, lp)
    branches = (from_heads(a_o), from_heads(b_o), c_o, from_heads(d_o))
    gates = jax.nn.sigmoid(gate_in.reshape(B, L, N_BRANCH, D_MODEL))
    merged = gates[:, :, 0] * (branches[0] @ lp['w_branch'][0])
    for i in range(1, N_BRANCH):
        merged = merged + gates[:, :, i] * (branches[i] @ lp['w_branch'][i])
    return merged @ lp['w_out'], ctx_out

def trunk_layer(x, cond, lp, l, ctx_cache):
    mod = jax.nn.silu(cond) @ lp['w_ada'] + lp['b_ada']
    mod = mod.reshape(mod.shape[0], 1, N_MOD, D_MODEL)
    sh1, sc1, g1, sh2, sc2, g2, sh3, sc3, g3 = [mod[:, :, i] for i in range(N_MOD)]
    h = rmsnorm(x, lp['norm_ffn1']) * (1 + sc1) + sh1
    x = x + 0.5 * g1 * swiglu(h, lp['ffn1_w1'], lp['ffn1_w3'], lp['ffn1_w2'])
    h = rmsnorm(x, lp['norm_mix']) * (1 + sc2) + sh2
    mix, ctx_out = token_mixing(h, lp, l, ctx_cache)
    x = x + g2 * mix
    h = rmsnorm(x, lp['norm_ffn2']) * (1 + sc3) + sh3
    x = x + 0.5 * g3 * swiglu(h, lp['ffn2_w1'], lp['ffn2_w3'], lp['ffn2_w2'])
    return x, ctx_out

def setup_inputs(seed: int = 0) -> dict:
    key = jax.random.key(seed)
    keys = iter(jax.random.split(key, 64))

    def nrm(shape, scale):
        return jax.random.normal(next(keys), shape, jnp.float32) * scale

    D = D_MODEL
    C = HY_WIDTH
    hy_rates = jnp.log(jnp.linspace(HY_MIN_DECAY, HY_MAX_DECAY, HY_ORDER * 2 * C, dtype=jnp.float32))
    return {
        'x_prompt': nrm((BATCH, SEQ, D), 1.0),
        'x_sample': nrm((DEC_BATCH, DEC_SEQ, D), 1.0),
        'cache_na_k': nrm((DEC_BATCH, DEPTH, NA_HEADS, PAST_LEN, HEAD_DIM), 1.0),
        'cache_na_v': nrm((DEC_BATCH, DEPTH, NA_HEADS, PAST_LEN, HEAD_DIM), 1.0),
        'cache_swa_k': nrm((DEC_BATCH, DEPTH, SWA_KV_HEADS, PAST_LEN, HEAD_DIM), 1.0),
        'cache_swa_v': nrm((DEC_BATCH, DEPTH, SWA_KV_HEADS, PAST_LEN, HEAD_DIM), 1.0),
        'cache_diff_k': nrm((DEC_BATCH, DEPTH, DIFF_HEADS, PAST_LEN, 2 * DIFF_HD), 1.0),
        'cache_diff_v': nrm((DEC_BATCH, DEPTH, DIFF_HEADS, PAST_LEN, 2 * DIFF_HD), 1.0),
        'c': nrm((DEC_BATCH, D), 1.0),
        'c_ctx': nrm((D,), 1.0),
        'w_ada': nrm((DEPTH, D, N_MOD * D), D ** -0.5),
        'b_ada': nrm((DEPTH, N_MOD * D), 0.02),
        'norm_ffn1': 1.0 + nrm((DEPTH, D), 0.02),
        'norm_mix': 1.0 + nrm((DEPTH, D), 0.02),
        'norm_ffn2': 1.0 + nrm((DEPTH, D), 0.02),
        'final_norm': 1.0 + nrm((D,), 0.02),
        'ffn1_w1': nrm((DEPTH, D, D_FF), D ** -0.5),
        'ffn1_w3': nrm((DEPTH, D, D_FF), D ** -0.5),
        'ffn1_w2': nrm((DEPTH, D_FF, D), D_FF ** -0.5),
        'ffn2_w1': nrm((DEPTH, D, D_FF), D ** -0.5),
        'ffn2_w3': nrm((DEPTH, D, D_FF), D ** -0.5),
        'ffn2_w2': nrm((DEPTH, D_FF, D), D_FF ** -0.5),
        'w_in': nrm((DEPTH, D, IN_W), D ** -0.5),
        'w_branch': nrm((DEPTH, N_BRANCH, BRANCH_W, D), BRANCH_W ** -0.5),
        'w_out': nrm((DEPTH, D, D), D ** -0.5),
        'na_rpb': nrm((DEPTH, NA_HEADS, 2 * NA_WIN_R - 1, 2 * NA_WIN_C - 1), 0.1),
        'swa_sink': nrm((DEPTH, SWA_HEADS), 0.5),
        'hy_short_w': nrm((DEPTH, 3, HY_IN_W), 3 ** -0.5),
        'hy_short_b': nrm((DEPTH, HY_IN_W), 0.02),
        'hy_w1': nrm((DEPTH, HY_EMB, HY_HIDDEN), HY_EMB ** -0.5),
        'hy_b1': nrm((DEPTH, HY_HIDDEN), 0.1),
        'hy_w2': nrm((DEPTH, HY_HIDDEN, HY_HIDDEN), HY_HIDDEN ** -0.5),
        'hy_b2': nrm((DEPTH, HY_HIDDEN), 0.1),
        'hy_w3': nrm((DEPTH, HY_HIDDEN, HY_ORDER * 2 * C), HY_HIDDEN ** -0.5),
        'hy_sin_freq': 1.0 + nrm((DEPTH, HY_HIDDEN), 0.05),
        'hy_log_decay': hy_rates[None, :] + nrm((DEPTH, HY_ORDER * 2 * C), 0.05),
        'hy_skip': nrm((DEPTH, HY_ORDER, C), 0.5),
        'diff_lambda': nrm((DEPTH, 4, DIFF_HD), 0.1),
        'diff_subln': 1.0 + nrm((DEPTH, 2 * DIFF_HD), 0.02),
    }

def reference(x_prompt, x_sample, cache_na_k, cache_na_v, cache_swa_k, cache_swa_v, cache_diff_k, cache_diff_v,
              c, c_ctx, w_ada, b_ada, norm_ffn1, norm_mix, norm_ffn2, final_norm,
              ffn1_w1, ffn1_w3, ffn1_w2, ffn2_w1, ffn2_w3, ffn2_w2, w_in, w_branch, w_out,
              na_rpb, swa_sink, hy_short_w, hy_short_b, hy_w1, hy_b1, hy_w2, hy_b2, hy_w3,
              hy_sin_freq, hy_log_decay, hy_skip, diff_lambda, diff_subln):
    layer_params = {
        'w_ada': w_ada, 'b_ada': b_ada, 'norm_ffn1': norm_ffn1, 'norm_mix': norm_mix, 'norm_ffn2': norm_ffn2,
        'ffn1_w1': ffn1_w1, 'ffn1_w3': ffn1_w3, 'ffn1_w2': ffn1_w2,
        'ffn2_w1': ffn2_w1, 'ffn2_w3': ffn2_w3, 'ffn2_w2': ffn2_w2,
        'w_in': w_in, 'w_branch': w_branch, 'w_out': w_out, 'na_rpb': na_rpb, 'swa_sink': swa_sink,
        'hy_short_w': hy_short_w, 'hy_short_b': hy_short_b, 'hy_w1': hy_w1, 'hy_b1': hy_b1,
        'hy_w2': hy_w2, 'hy_b2': hy_b2, 'hy_w3': hy_w3, 'hy_sin_freq': hy_sin_freq,
        'hy_log_decay': hy_log_decay, 'hy_skip': hy_skip, 'diff_lambda': diff_lambda, 'diff_subln': diff_subln,
    }
    x = x_prompt
    ctx_cond = c_ctx[None, :]
    collected = ([], [], [], [], [], [])
    for l in range(DEPTH):
        lp = {name: arr[l] for name, arr in layer_params.items()}
        x, ctx_out = trunk_layer(x, ctx_cond, lp, l, None)
        for store, t in zip(collected, ctx_out):
            store.append(t)
    y_prompt = rmsnorm(x, final_norm)
    new_na_k, new_na_v, new_swa_k, new_swa_v, new_diff_k, new_diff_v = [jnp.stack(s, axis=1) for s in collected]

    caches = (cache_na_k, cache_na_v, cache_swa_k, cache_swa_v, cache_diff_k, cache_diff_v)
    x = x_sample
    for l in range(DEPTH):
        lp = {name: arr[l] for name, arr in layer_params.items()}
        x, _ = trunk_layer(x, c, lp, l, tuple(t[:, l] for t in caches))
    y_sample = rmsnorm(x, final_norm)
    return (y_prompt, y_sample, new_na_k, new_na_v, new_swa_k, new_swa_v, new_diff_k, new_diff_v)


_drawn_inputs = setup_inputs


def setup_inputs(seed=0):
    import zlib

    import numpy as np

    out = dict(_drawn_inputs(seed))
    spreads = {}
    factors = {'norm_ffn1': 5.23,
     'norm_mix': 2.957,
     'norm_ffn2': 5.8,
     'final_norm': 22.267,
     'na_rpb': 64.0,
     'swa_sink': 64.0,
     'hy_short_b': 8.0,
     'hy_sin_freq': 8.0,
     'diff_subln': 43.644,
     'cache_na_k': 8.0,
     'cache_na_v': 8.0,
     'cache_swa_k': 8.0,
     'cache_swa_v': 8.0,
     'cache_diff_k': 8.0,
     'cache_diff_v': 8.0}
    for name, (base, spread) in spreads.items():
        noise = np.random.default_rng([zlib.crc32(name.encode()), seed]).standard_normal(out[name].shape)
        drawn = base * np.exp(spread * noise) if base else spread * noise
        out[name] = jnp.asarray(drawn.astype(out[name].dtype))
    for name, factor in factors.items():
        out[name] = (out[name] * factor).astype(out[name].dtype)
    return out
```

```python
import math
from contextlib import ExitStack

import numpy as np
import concourse.bass as bass
from concourse import mybir

F32 = mybir.dt.float32
F32R = mybir.dt.float32r
ALU = mybir.AluOpType
ACT = mybir.ActivationFunctionType
AX_X = mybir.AxisListType.X

D, T_CTX, T_DEN, DEPTH, PAST = 1024, 128, 256, 2, 128
GRID_W, WIN_R, WIN_C = 64, 8, 16
D_FF = 2816
P = 128
T = T_CTX + T_DEN
TB = T // P
C = D // P
FB = D_FF // P
N_MOD = 9
EPS = 1e-6
NEG = -1e30
HY_FREQS, HY_EMB, HY_HID = 16, 33, 64
GROUPS = ((0, T_CTX), (T_CTX, T))
RING = 4
AHEAD = RING - 1
THIRDS = (8, 8, 6)
SH1, SC1, G1, SH2, SC2, G2, SH3, SC3, G3 = range(N_MOD)
N_PROJ = 22
BRANCH_ORDER = (0, 1, 3, 2)
NA, SWA, DF = range(3)
LAM_INIT = [0.8 - 0.6 * math.exp(-0.3 * l) for l in range(DEPTH)]

K_ID, K_ONES, K_BONES, K_R64, K_R32 = (P * i for i in range(5))
K_NAM = 5 * P
K_SWM = K_NAM + 256
K_CP = K_SWM + 256
K_SP = K_CP + P
K_CS = K_SP + P
K_SS = K_CS + 512
K_NTN = K_SS + 512
K_TM = K_NTN + 3
K_EPS = K_TM + 3
K_COLS = K_EPS + 1
V_COND = 0
V_BADA = V_COND + 2 * C
V_NORM = V_BADA + DEPTH * N_MOD * C
V_FIN = V_NORM + DEPTH * 3 * C
V_SHORT = V_FIN + C
V_SKIP = V_SHORT + DEPTH * 24
V_MLP = V_SKIP + DEPTH * 4
V_SUBLN = V_MLP + DEPTH * 3
V_SINK = V_SUBLN + DEPTH
V_LAM = V_SINK + DEPTH * 4
V_COLS = V_LAM
TWO_PI_A = 6.28125
TWO_PI_B = float(np.float32(np.floor((2 * math.pi - TWO_PI_A) * 2 ** 20) / 2 ** 20))
TWO_PI_C = 2 * math.pi - TWO_PI_A - TWO_PI_B
ROUND = 1.5 * 2 ** 23
PI_DOWN = 3.1415925


class Phase:

    def __init__(self, kind, n0, tiles, l=0, which=0, hp=0, ffn=0, q=0, third=0, iters=0, ada=False, m=0, first=False, f0=0):
        self.kind, self.n0, self.tiles, self.l, self.which, self.hp = kind, n0, tiles, l, which, hp
        self.ffn, self.q, self.third, self.iters, self.ada, self.m, self.first, self.f0 = ffn, q, third, iters, ada, m, first, f0


def phases():
    out, n, ada_at = [], 0, 0

    def add(kind, tiles=0, **more):
        nonlocal n
        out.append(Phase(kind, n, tiles, **more))
        n += tiles

    def ada(count):
        nonlocal ada_at
        m = ada_at
        ada_at += count
        return m

    add("ada", 2 * C, m=ada(2 * C), l=0)
    for l in range(DEPTH):
        add("norm", l=l, which=0, hp=4 * l)
        for third, fbs in enumerate(THIRDS):
            for f0, iters in ((0, 1), (2, fbs // 2 - 1)) if l + third == 0 else ((0, fbs // 2),):
                add("up", 8 * iters, l=l, ffn=0, q=2 * l, third=third, iters=iters, ada=True, m=ada(4 * iters),
                    first=third + f0 == 0, f0=f0)
            add("down", C, l=l, ffn=0, q=2 * l, third=third)
        add("ada", 4, m=ada(4), l=l)
        add("norm", l=l, which=1, hp=4 * l + 1)
        add("mix", N_PROJ + 5 * C, l=l)
        add("norm", l=l, which=2, hp=4 * l + 3)
        left = (3 * C if l + 1 < DEPTH else C) // 4
        for third, fbs in enumerate(THIRDS):
            k = min(left, fbs // 2)
            left -= k
            f0 = 0
            while k:
                run = min(k, (N_MOD * C - ada_at % (N_MOD * C)) // 4)
                add("up", 8 * run, l=l, ffn=1, q=2 * l + 1, third=third, iters=run, ada=True, m=ada(4 * run),
                    first=third == 0 and f0 == 0, f0=f0)
                k, f0 = k - run, f0 + 2 * run
            if f0 < fbs:
                add("up", 2 * (fbs - f0), l=l, ffn=1, q=2 * l + 1, third=third, iters=(fbs - f0) // 2, ada=False,
                    first=third == 0 and f0 == 0, f0=f0)
            add("down", C, l=l, ffn=1, q=2 * l + 1, third=third)
    add("norm", l=DEPTH - 1, which=3, hp=4 * DEPTH)
    return out, n


PHASES, N_TILES = phases()
MIX_N0 = [p.n0 for p in PHASES if p.kind == "mix"]
WIDE = {n0 + N_PROJ + j for n0 in MIX_N0 for j in range(4 * C)}


def width(n):
    return 1280 if n in WIDE else 1024


def spread(tiles, side):
    out, done = [], 0
    for i, t in enumerate(tiles):
        upto = (i + 1) * len(side) // len(tiles)
        out += side[done:upto]
        done = upto
        out.append(t)
    return out + side[done:]


def attention_steps(kind):
    units = [(blk, hh, b) for blk in range(2) for hh in range(2) for b in range(TB)]
    out = []
    if kind == DF:
        out += [("scores", kind, 0, 0), ("scores", kind, 0, 1)]
        for u in range(12):
            out.append(("probs", kind, u))
            if u + 1 < 12:
                out.append(("scores", kind, u + 1, 0))
            out.append(("turn", kind, u))
            if u + 1 < 12:
                out.append(("scores", kind, u + 1, 1))
            out.append(("values", kind, u))
            if u % 6 == 5:
                out += [("square", u // 6), ("subnorm", u // 6)]
        return out
    out += [("scores", kind, 0, 0), ("probs", kind, 0)]
    for u in range(12):
        if u + 1 < 12:
            out.append(("scores", kind, u + 1, 0))
        out.append(("turn", kind, u))
        if u + 1 < 12:
            out.append(("probs", kind, u + 1))
        out.append(("values", kind, u))
        if u % 6 == 5:
            out.append(("outs", kind, u // 6))
    return out


def mix_plan():
    fil = [("sinmlp", 0), ("sinmlp", 1)] + [("taps", o, tk) for o in range(2) for tk in range(TB)]
    fil = fil[:5] + [("scale", 0)] + [("filter", 0, fc) for fc in range(TB)] + fil[5:] + [("scale", 1)] + \
        [("filter", 1, fc) for fc in range(TB)]
    proj = [("proj", k) for k in range(N_PROJ)]
    plan = spread(proj[:10], fil)
    plan += [("vk", 0), ("vk", 1)] + spread(proj[10:16], attention_steps(NA)[:26])
    plan += spread(proj[16:], [("vk", 2), ("vk", 3), ("vk", 4)] + [("rope", j) for j in range(7)] + attention_steps(NA)[26:])
    gates = [[("fused", i, n) for n in range(C)] for i in range(4)]
    plan += spread(gates[0], attention_steps(SWA))
    plan += spread(gates[1], attention_steps(DF))
    hy = [("short", j) for j in range(6)]
    for o in range(2):
        hy += [("ytok", o, 0), ("ytok", o, 1)] + [("spectrum", o, fc) for fc in range(TB)] + [("conv", o, 0), ("conv", o, 1)]
    hy += [("hyout", 0), ("hyout", 1)]
    plan += spread(gates[2], hy)
    plan += gates[3] + [("merged", c) for c in range(C)] + [("out", c) for c in range(C)]
    return plan


def build(nc, w_main, w_fused, consts, vecs, lam, x_in, rope, bias, logdecay, kctx, vctx, mlp_w, mlp_w3, zt, dft,
          y_out, nk, nv):
    ctx = ExitStack()
    with ctx:
        def sb(name, shape, dt=F32):
            return ctx.enter_context(nc.sbuf_tensor(name, shape, dt))

        def sem(name):
            return ctx.enter_context(nc.semaphore(name))

        x = sb("x", [P, C, T])
        h_hi, h_lo = sb("h_hi", [P, C, T], F32R), sb("h_lo", [P, C, T], F32R)
        raw = sb("raw", [P, RING, 1280])
        hi, lo = sb("hi", [P, RING, 1280], F32R), sb("lo", [P, RING, 1280], F32R)
        kk = sb("kk", [P, K_COLS])
        vv = sb("vv", [P, V_COLS])
        mod = sb("mod", [P, N_MOD * C, 2])
        coef = sb("coef", [P, 3, C, 2])
        modb = sb("modb", [P, 2, C, 2])
        c_act = sb("c_act", [P, C, 2])
        c_hi, c_lo = sb("c_hi", [P, C, 2], F32R), sb("c_lo", [P, C, 2], F32R)
        kt = sb("kt", [P, 5, 512])
        q_swa = sb("q_swa", [P, 2, T])
        vt = sb("vt", [P, 4, 640])
        areaM, areaE, areaF = sb("areaM", [P, 3072]), sb("areaE", [P, 3072]), sb("areaF", [P, 3072])
        pr = sb("pr", [P, 2, T])
        prT = sb("prT", [P, T])
        rstd = prT
        o_hi, o_lo = sb("o_hi", [P, 2, 2, T], F32R), sb("o_lo", [P, 2, 2, T], F32R)
        tiny = sb("tiny", [P, 32])
        with nc.sbuf_tensor("g_hi", [P, C, T], F32R) as g_hi, nc.sbuf_tensor("g_lo", [P, C, T], F32R) as g_lo:
            pass
        areaG = sb("areaG", [P, 2 * C * T])
        hy = areaG[:, 0:7 * T].rearrange("p (j t) -> p j t", t=T)
        q_na = areaG[:, 7 * T:9 * T].rearrange("p (j t) -> p j t", t=T)
        q_df = areaG[:, 9 * T:11 * T].rearrange("p (j t) -> p j t", t=T)
        v_all = areaG[:, 11 * T:16 * T].rearrange("p (j t) -> p j t", t=T)
        k_tok = areaG[:, 11 * T:11 * T + 640].rearrange("p (j t) -> p j t", t=P)
        th = q_na
        gated = v_all[:, 2:4, :]
        h_f = areaM[:, :].rearrange("p (c t) -> p c t", t=T)
        merged = h_f
        taps = areaM[:, 0:1536].rearrange("p (k s c) -> p k s c", k=TB, s=2)
        dft_t = areaM[:, 1536:1536 + 1280]
        na_bias = areaE[:, 0:2048].rearrange("p (b h k) -> p b h k", b=2, h=4)
        rope_t = areaE[:, 2048:3072].rearrange("p (j t) -> p j t", t=T_DEN)
        y_tok = areaE[:, 0:768].rearrange("p (k c) -> p k c", k=TB)
        spec = areaE[:, 768:2304].rearrange("p (f s c) -> p f s c", f=TB, s=2)
        spec_t = areaE[:, 2304:2816].rearrange("p (s c) -> p s c", s=2)
        sq = areaF[:, :].rearrange("p (c t) -> p c t", t=T)
        sil = areaF[:, 0:2 * T].rearrange("p (s t) -> p s t", t=T)
        gf = areaF[:, 2 * T:4 * T].rearrange("p (s t) -> p s t", t=T)
        filt = areaF[:, :].rearrange("p (o f s c) -> p o f s c", o=2, f=TB, s=2)
        fw3 = areaF[0:HY_HID, 1536:2560]
        fg = areaF[0:HY_HID, 2560:2560 + T]
        fw1 = areaF[0:HY_EMB, 2944:3008]
        fw2 = areaF[0:HY_HID, 3008:3072]
        rate = areaG[:, 0:1024]
        win = areaG[:, 1024:1536]
        hab = areaG[:, 1536:2048]
        z_t = areaG[0:HY_EMB, 2048:2048 + T]
        f_arg, f_turn = q_df[0:HY_HID, 0, :], q_df[0:HY_HID, 1, :]
        f_inv = pr[:, :, :].rearrange("p a t -> p (a t)")[:, 0:512].rearrange("p (g c) -> p g c", g=2)

        lam_vecs = areaM[:, 0:DEPTH * 128]
        ident = kk[:, K_ID:K_ID + P]
        ones = kk[:, K_ONES:K_ONES + P]
        bones = kk[:, K_BONES:K_BONES + P]
        eps = kk[:, K_EPS:K_EPS + 1]

        bank = [ctx.enter_context(nc.psum_tensor(f"bank{i}", [P, 512], F32)) for i in range(RING)]
        ps_br, ps_s, ps_t, ps_o = (ctx.enter_context(nc.psum_tensor(n, [P, 512], F32)) for n in ("ps_br", "ps_s", "ps_t", "ps_o"))

        consts_in, raw_in = sem("consts_in"), [sem(f"raw_in{i}") for i in range(RING)]
        hi_ready, lo_ready, tile_done, drained = sem("hi_ready"), sem("lo_ready"), sem("tile_done"), sem("drained")
        cond_act, cond_hi, cond_lo = sem("cond_act"), sem("cond_hi"), sem("cond_lo")
        silu_done, gf_ready, g_lo_ready = sem("silu_done"), sem("gf_ready"), sem("g_lo_ready")
        sq_ready, ss_ready, rms_ready = sem("sq_ready"), sem("ss_ready"), sem("rms_ready")
        h_ready, h_hi_ready, h_lo_ready = sem("h_ready"), sem("h_hi_ready"), sem("h_lo_ready")
        dve_order, act_order, pool_order = sem("dve_order"), sem("act_order"), sem("pool_order")
        small_in, lam_exp, lam_dot = sem("small_in"), sem("lam_exp"), sem("lam_dot")
        filt_in, ctx_in, bias_ready = sem("filt_in"), sem("ctx_in"), sem("bias_ready")
        mlp_mm, mlp_arg, mlp_sin = sem("mlp_mm"), sem("mlp_arg"), sem("mlp_sin")
        taps_mm, win_ready, taps_ready, abs_ready, sum_mm = (sem("taps_mm"), sem("win_ready"), sem("taps_ready"),
                                                             sem("abs_ready"), sem("sum_mm"))
        scale_ready, filt_mm, filt_ready = sem("scale_ready"), sem("filt_mm"), sem("filt_ready")
        t_ready, t_free = sem("t_ready"), sem("t_free")
        rot_ready, rope_done = sem("rot_ready"), sem("rope_done")
        scores_ready, max_ready, exp_done, probs_ready, probs0_used = (
            sem("scores_ready"), sem("max_ready"), sem("exp_done"), sem("probs_ready"), sem("probs0_used"))
        values_done, o_hi_ready, o_lo_ready = sem("values_done"), sem("o_hi_ready"), sem("o_lo_ready")
        osq_ready, orms_ready, onorm_ready = sem("osq_ready"), sem("orms_ready"), sem("onorm_ready")
        merged_done, th_ready = sem("merged_done"), sem("th_ready")
        y_ready, spec_mm, spec_ready, conv_mm = sem("y_ready"), sem("spec_mm"), sem("spec_ready"), sem("conv_mm")
        out_done, kv_out, y_fin = sem("out_done"), sem("kv_out"), sem("y_fin")

        plan = mix_plan()
        t_index = {s: i for i, s in enumerate([s for s in plan if s[0] in ("vk", "turn", "subnorm", "ytok")])}
        T_PER = len(t_index)
        rounds = [s for s in plan if s[0] == "scores"]
        r_index = {s: i for i, s in enumerate(rounds)}
        R_PER = len(rounds)
        U_PER = 36
        FUSED0 = N_PROJ
        TYPE_T0 = {}

        def out_pair(branch, blk):
            return 2 * BRANCH_ORDER.index(branch) + blk

        def buf(branch):
            return BRANCH_ORDER.index(branch) % 2

        BR_OF = {NA: 0, SWA: 1, DF: 3}

        def unit(u):
            return u // 6, (u // 3) % 2, u % 3

        def keys(b):
            return (0, 128) if b == 0 else (128, 512)

        F0 = {}

        def fcount(p):
            return FB * p.q + sum(THIRDS[:p.third]) + (p.f0 if p.kind == "up" else 0)

        def vcol(i):
            return vv[:, i:i + 1]

        block = ctx.enter_context(nc.Block())

        @block.sync
        def _(sp):
            for dst, src in ((vv, vecs), (kk, consts)):
                sp.dma_start(dst[:], src).then_inc(consts_in, 16)
            sp.dma_start(x[:, :, :].rearrange("p c t -> p (c t)"), x_in).then_inc(consts_in, 16)
            sp.dma_start(lam_vecs, lam).then_inc(consts_in, 16)

            def load(base, rep, src):
                slot = base % RING
                if base >= RING:
                    sp.wait_ge(lo_ready, base - RING + 1 + 4 * rep)
                    sp.wait_ge(hi_ready, base - RING + 1 + 4 * rep)
                sp.dma_start(raw[:, slot, 0:width(base)], src).then_inc(raw_in[slot], 16)

            def main(j, i=0):
                return w_main[bass.ds(j + 4 * i, 1)].rearrange("a p n -> p (a n)")

            at, n = 0, 0
            for l, mix0 in enumerate(MIX_N0 + [None]):
                stop = N_TILES if mix0 is None else mix0 + N_PROJ
                for _ in range(RING if n == 0 else 0):
                    load(n, 0, w_main[at])
                    n, at = n + 1, at + 1
                groups = (stop - n) // RING
                with sp.Fori(0, groups) as i:
                    for j in range(RING):
                        load(n + j, i, main(at + j, i))
                n, at = n + RING * groups, at + RING * groups
                while n < stop:
                    load(n, 0, w_main[at])
                    n, at = n + 1, at + 1
                if mix0 is not None:
                    with sp.Fori(0, C) as i:
                        for j in range(4):
                            load(n + j, i, w_fused[bass.ds(4 * C * l + j + 4 * i, 1)].rearrange("a p n -> p (a n)"))
                    n += 4 * C
            sp.wait_ge(y_fin, C)
            sp.dma_start(y_out, areaM[:, :]).then_inc(out_done, 16)
            sp.wait_ge(out_done, 16)

        @block.scalar
        def _(act):
            order = [0]

            def link(ins):
                order[0] += 1
                ins.then_inc(act_order, 1)
                act.wait_ge(act_order, order[0])

            def split(base, rep=0):
                if base >= N_TILES:
                    return
                slot = base % RING
                act.wait_ge(raw_in[slot], 16 * (base // RING + 1 + rep))
                if base >= RING:
                    act.wait_ge(tile_done, base - RING + 1 + 4 * rep)
                act.activation(hi[:, slot, 0:width(base)], raw[:, slot, 0:width(base)], ACT.Copy).then_inc(hi_ready, 1)

            act.wait_ge(consts_in, 64)
            act.activation(c_act[:, :, :].rearrange("p c g -> p (c g)"), vv[:, V_COND:V_COND + 2 * C], ACT.Silu).then_inc(cond_act, 1)
            act.wait_ge(cond_act, 1)
            act.activation(c_hi[:], c_act[:], ACT.Copy).then_inc(cond_hi, 1)
            act.wait_ge(lam_dot, 1)
            act.activation(tiny[:, 4:8], tiny[:, 0:4], ACT.Exp).then_inc(lam_exp, 1)
            for n in range(AHEAD):
                split(n)

            def norm(p):
                for c in range(C):
                    if p.which == 0 and p.l == 0:
                        act.wait_ge(consts_in, 64)
                    else:
                        act.wait_ge(drained, norm_n0(p) - C + c + 1)
                    act.activation(sq[:, c, :], x[:, c, :], ACT.Square).then_inc(sq_ready, 1)
                act.wait_ge(ss_ready, nidx(p) + 1)
                act.activation(rstd[:], ps_o[:, 0:T], ACT.Sqrt, bias=eps, scale=1.0 / D).then_inc(rms_ready, 1)
                if p.which == 3:
                    return
                for c in range(C):
                    act.wait_ge(h_ready, C * nidx(p) + c + 1)
                    act.activation(h_hi[:, c, :], h_f[:, c, :], ACT.Copy).then_inc(h_hi_ready, 1)

            def up(p):
                per = 8 if p.ada else 4
                with act.Fori(0, p.iters) as i:
                    for j in range(per):
                        split(p.n0 + j + AHEAD, per // 4 * i)
                        if j in (0, per // 2):
                            s = 2 * j // per
                            f = fcount(p) + s
                            act.wait_ge(tile_done, p.n0 + j + 1 + per * i)
                            if f >= 2:
                                act.wait_ge(gf_ready, f - 1 + 2 * i)
                                act.wait_ge(drained, p.n0 + j - (5 if p.ada else 2) + per * i)
                            act.activation(sil[:, s, :], bank[(p.n0 + j) % RING][:, 0:T], ACT.Silu).then_inc(silu_done, 1)

            def down(p):
                if p.n0 + 2 * RING + AHEAD > N_TILES:
                    for j in range(C):
                        split(p.n0 + j + AHEAD)
                    return
                with act.Fori(0, 2) as i:
                    for j in range(4):
                        split(p.n0 + j + AHEAD, i)

            def mix(p):
                l = p.l
                for step in plan:
                    kind = step[0]
                    if kind == "proj":
                        split(p.n0 + step[1] + AHEAD)
                    elif kind == "fused":
                        _, i, n = step
                        at = p.n0 + FUSED0 + C * i + n
                        split(at + AHEAD)
                        act.wait_ge(tile_done, at + 1)
                        act.wait_ge(drained, at - 1)
                        act.activation(th[:, n % 2, :], bank[at % RING][:, 0:T], ACT.Tanh, scale=0.5).then_inc(th_ready, 1)
                    elif kind == "out":
                        split(p.n0 + N_PROJ + 4 * C + step[1] + AHEAD)
                    elif kind == "merged":
                        c = step[1]
                        act.wait_ge(merged_done, 3 * C * l + 2 * C + c + 1)
                        act.wait_ge(tile_done, p.n0 + N_PROJ + 4 * C)
                        act.activation(h_hi[:, c, :], merged[:, c, :], ACT.Copy).then_inc(h_hi_ready, 1)
                    elif kind == "sinmlp":
                        act.wait_ge(mlp_arg, 2 * l + step[1] + 1)
                        act.activation(fg, f_arg, ACT.Sin).then_inc(mlp_sin, 1)
                    elif kind == "taps":
                        _, o, tk = step
                        q = 6 * l + 3 * o + tk
                        if o == 0 and tk == 0:
                            act.wait_ge(filt_in, 16 * 6 * (l + 1))
                            link(act.activation(rate, rate, ACT.Exp))
                        if q:
                            act.wait_ge(abs_ready, q)
                            act.wait_ge(taps_ready, q)
                        act.activation(win, rate[:, 512 * o:512 * (o + 1)], ACT.Exp, scale=kk[:, K_NTN + tk:K_NTN + tk + 1]).then_inc(win_ready, 1)
                        act.wait_ge(taps_ready, q + 1)
                        if q:
                            act.wait_ge(sum_mm, q)
                        act.activation(hab, win, ACT.Abs).then_inc(abs_ready, 1)
                    elif kind == "vk":
                        j, t = step[1], T_PER * l + t_index[step]
                        act.wait_ge(t_ready, t + 1)
                        ps3 = ps_t[:, :].rearrange("p (k c) -> p k c", k=4)
                        act.activation(vt[:, 0:3, P * j:P * (j + 1)], ps3[:, 0:3, :], ACT.Copy).then_inc(act_order, 1)
                        order[0] += 1
                        act.activation(k_tok[:, j, :], ps3[:, 3, :], ACT.Copy).then_inc(t_free, 1)
                    elif kind == "scores":
                        _, ty, u, m = step
                        r = R_PER * l + r_index[step]
                        act.wait_ge(max_ready, r + 1)
                        b = unit(u)[2]
                        nk_ = keys(b)[1] - keys(b)[0]
                        nm = tiny[:, 8 + r % 4:9 + r % 4]
                        if ty == SWA:
                            head = unit(u)[0] + 2 * unit(u)[1]
                            order[0] += 1
                            act.activation(tiny[:, 20 + r % 4:21 + r % 4], vcol(V_SINK + 4 * l + head), ACT.Exp, bias=nm).then_inc(act_order, 1)
                        g = U_PER * l + 12 * ty + u
                        if ty == DF and m == 0:
                            act.wait_ge(probs_ready, g)
                        elif ty == DF:
                            act.wait_ge(t_ready, T_PER * l + turn_t(ty, u))
                        elif g > 1:
                            act.wait_ge(t_ready, T_PER * l + turn_t(ty, u - 1) if u else T_PER * l + turn_t(ty, 0))
                        dst = pr[:, m if ty == DF else u % 2, 0:nk_]
                        act.activation(dst, ps_s[:, 0:nk_], ACT.Exp, bias=nm, accum_out=tiny[:, 12 + r % 4:13 + r % 4]).then_inc(exp_done, 1)
                    elif kind == "turn":
                        _, ty, u = step
                        t, g = T_PER * l + t_index[step], U_PER * l + 12 * ty + u
                        act.wait_ge(t_ready, t + 1)
                        if g:
                            act.wait_ge(values_done, g)
                        nk_ = keys(unit(u)[2])[1] - keys(unit(u)[2])[0]
                        act.activation(prT[:, 0:nk_], ps_t[:, 0:nk_], ACT.Copy).then_inc(t_free, 1)
                    elif kind == "outs":
                        _, ty, blk = step
                        act.wait_ge(values_done, U_PER * l + 12 * ty + 6 * (blk + 1))
                        act.activation(o_hi[:, buf(BR_OF[ty]), blk, :], ps_o[:, 0:T], ACT.Copy).then_inc(o_hi_ready, 1)
                    elif kind == "square":
                        act.wait_ge(values_done, U_PER * l + 12 * DF + 6 * (step[1] + 1))
                        act.activation(prT[:], ps_o[:, 0:T], ACT.Square).then_inc(osq_ready, 1)
                    elif kind == "subnorm":
                        blk = step[1]
                        act.wait_ge(t_ready, T_PER * l + t_index[step] + 1)
                        act.activation(prT[:], ps_t[:, 0:T], ACT.Sqrt, bias=eps, scale=1.0 / 64).then_inc(t_free, 1)
                        act.wait_ge(onorm_ready, 2 * l + blk + 1)
                        act.wait_ge(tile_done, p.n0 + FUSED0 + C)
                        act.activation(o_hi[:, buf(3), blk, :], prT[:], ACT.Copy).then_inc(o_hi_ready, 1)
                    elif kind == "ytok":
                        _, o, blk = step
                        act.wait_ge(t_ready, T_PER * l + t_index[step] + 1)
                        ps3 = ps_t[:, 0:T].rearrange("p (k c) -> p k c", k=3)
                        act.activation(y_tok[:, :, P * blk:P * (blk + 1)], ps3, ACT.Copy).then_inc(t_free, 1)
                    elif kind == "hyout":
                        blk = step[1]
                        act.wait_ge(y_ready, 6 * l + 4 + blk + 1)
                        act.wait_ge(tile_done, p.n0 + FUSED0 + 2 * C)
                        act.activation(o_hi[:, buf(2), blk, :], hy[:, blk, :], ACT.Copy).then_inc(o_hi_ready, 1)

            def turn_t(ty, u):
                return t_index[("turn", ty, u)] if u == 0 else t_index[("turn", ty, u - 1)] + 1

            for p in PHASES:
                if p.kind == "ada":
                    for j in range(p.tiles):
                        split(p.n0 + j + AHEAD)
                elif p.kind == "norm":
                    norm(p)
                elif p.kind == "up":
                    up(p)
                elif p.kind == "down":
                    down(p)
                else:
                    mix(p)

        @block.vector
        def _(dve):
            order = [0]

            def link(ins):
                order[0] += 1
                ins.then_inc(dve_order, 1)
                dve.wait_ge(dve_order, order[0])

            def split(base, rep=0):
                if base >= N_TILES:
                    return
                slot = base % RING
                dve.wait_ge(hi_ready, base + 1 + 4 * rep)
                w = width(base)
                dve.tensor_tensor(lo[:, slot, 0:w], raw[:, slot, 0:w], hi[:, slot, 0:w].bitcast(F32), ALU.subtract).then_inc(lo_ready, 1)

            dve.wait_ge(consts_in, 64)
            for l in range(DEPTH):
                for i in range(2):
                    a = 128 * l + 64 * i
                    link(dve.tensor_tensor(prT[:, 0:32], lam_vecs[:, a:a + 32], lam_vecs[:, a + 32:a + 64], ALU.mult))
                    link(dve.tensor_reduce(tiny[:, 2 * l + i:2 * l + i + 1], prT[:, 0:32], AX_X, ALU.add))
            dve.memset(tiny[:, 28:29], 0.0).then_inc(lam_dot, 1)
            dve.wait_ge(cond_hi, 1)
            dve.tensor_tensor(c_lo[:], c_act[:], c_hi[:].bitcast(F32), ALU.subtract).then_inc(cond_lo, 1)
            dve.wait_ge(lam_exp, 1)
            for l in range(DEPTH):
                nl = tiny[:, 24 + l:25 + l]
                link(dve.tensor_tensor(nl, tiny[:, 5 + 2 * l:6 + 2 * l], tiny[:, 4 + 2 * l:5 + 2 * l], ALU.subtract))
                link(dve.tensor_scalar(nl, nl, LAM_INIT[l], None, ALU.subtract))
                link(dve.tensor_scalar(tiny[:, 26 + l:27 + l], vcol(V_SUBLN + l), 1.0 - LAM_INIT[l], None, ALU.mult))
            for n in range(AHEAD):
                split(n)

            def modulation(l, v, slot):
                b = vv[:, V_BADA + N_MOD * C * l + C * v:V_BADA + N_MOD * C * l + C * (v + 1)].unsqueeze(2).broadcast_to([P, C, 2])
                link(dve.tensor_tensor(modb[:, slot], mod[:, C * v:C * (v + 1), :], b, ALU.add))

            def residual_gate(l, v):
                modulation(l, v, 0)
                link(dve.tensor_scalar(coef[:, 2], modb[:, 0], 0.5, None, ALU.mult))

            def norm(p):
                k = nidx(p)
                if p.which < 3:
                    modulation(p.l, (SC1, SC2, SC3)[p.which], 0)
                    a = V_NORM + 3 * C * p.l + C * p.which
                    w = vv[:, a:a + C].unsqueeze(2).broadcast_to([P, C, 2])
                    link(dve.scalar_tensor_tensor(coef[:, 0], modb[:, 0], 1.0, w, ALU.add, ALU.mult))
                    modulation(p.l, (SH1, SH2, SH3)[p.which], 1)
                dve.wait_ge(rms_ready, k + 1)
                link(dve.reciprocal(rstd[:], rstd[:]))
                for c in range(C):
                    link(dve.tensor_tensor(sq[:, c, :], x[:, c, :], rstd[:], ALU.mult))
                    if p.which == 3:
                        dve.tensor_scalar(h_f[:, c, :], sq[:, c, :], vcol(V_FIN + c), None, ALU.mult).then_inc(y_fin, 1)
                        continue
                    for g, (t0, t1) in enumerate(GROUPS):
                        last = dve.tensor_scalar(h_f[:, c, t0:t1], sq[:, c, t0:t1], coef[:, 0, c, g:g + 1], modb[:, 1, c, g:g + 1],
                                                 ALU.mult, ALU.add)
                    last.then_inc(h_ready, 1)
                    if c:
                        h_low(hp8(p) + c - 1, h_f[:, c - 1, :], c - 1)
                if p.which < 3:
                    h_low(hp8(p) + C - 1, h_f[:, C - 1, :], C - 1)

            def h_low(count, src, c):
                dve.wait_ge(h_hi_ready, count + 1)
                dve.tensor_tensor(h_lo[:, c, :], src, h_hi[:, c, :].bitcast(F32), ALU.subtract).then_inc(h_lo_ready, 1)

            def up(p):
                if p.first and p.ffn == 1:
                    dve.wait_ge(kv_out, 16 * 6 * (p.l + 1))
                per = 8 if p.ada else 4
                with dve.Fori(0, p.iters) as i:
                    for j in range(per):
                        n = p.n0 + j
                        split(n + AHEAD, per // 4 * i)
                        if j in (per // 4, 3 * per // 4):
                            s = 2 * j // per
                            f = fcount(p) + s
                            b = bank[n % RING][:, 0:T]
                            dve.wait_ge(silu_done, f + 1 + 2 * i)
                            dve.wait_ge(tile_done, n + 1 + per * i)
                            if f >= 2:
                                dve.wait_ge(g_lo_ready, f - 1 + 2 * i)
                            dve.tensor_tensor(gf[:, s, :], sil[:, s, :], b, ALU.mult).then_inc(gf_ready, 1)
                            dst = g_hi[:, bass.ds(p.f0 + s + 2 * i, 1), :].rearrange("p a t -> p (a t)")
                            dve.tensor_tensor(dst, sil[:, s, :], b, ALU.mult).then_inc(drained, 2)
                        elif p.ada and j % 2:
                            dve.wait_ge(tile_done, n + 1 + per * i)
                            dst = mod[:, bass.ds(p.m % 72 + j // 2 + 4 * i, 1), :].rearrange("p a g -> p (a g)")
                            dve.tensor_copy(dst, bank[n % RING][:, 0:2]).then_inc(drained, 1)

            def add_to_x(n, c, rep=0, dyn=None):
                dve.wait_ge(tile_done, n + 1 + 4 * rep)
                for g, (t0, t1) in enumerate(GROUPS):
                    if dyn is None:
                        xs, gate = x[:, c, t0:t1], coef[:, 2, c, g:g + 1]
                    else:
                        xs = x[:, bass.ds(c + 4 * dyn, 1), t0:t1].rearrange("p a t -> p (a t)")
                        gate = coef[:, 2, bass.ds(c + 4 * dyn, 1), g:g + 1].rearrange("p a g -> p (a g)")
                    last = dve.scalar_tensor_tensor(xs, bank[n % RING][:, t0:t1], gate, xs, ALU.mult, ALU.add)
                last.then_inc(drained, 1)

            def down(p):
                if p.third == 0:
                    residual_gate(p.l, (G1, G3)[p.ffn])
                if p.n0 + 2 * RING + AHEAD > N_TILES:
                    for j in range(C):
                        split(p.n0 + j + AHEAD)
                        add_to_x(p.n0 + j, j)
                    return
                with dve.Fori(0, 2) as i:
                    for j in range(4):
                        split(p.n0 + j + AHEAD, i)
                        add_to_x(p.n0 + j, j, i, i)

            def proj_place(k):
                if k < 2:
                    return q_na[:, k, :], 0.125
                if k < 4:
                    return kt[:, k - 2, 0:T], 1.0
                if k < 6:
                    return v_all[:, k - 4, :], 1.0
                if k < 8:
                    return q_swa[:, k - 6, :], 0.125
                if k == 8:
                    return kt[:, 2, 0:T], 1.0
                if k == 9:
                    return v_all[:, 2, :], 1.0
                if k < 12:
                    return q_df[:, k - 10, :], 32 ** -0.5
                if k < 14:
                    return kt[:, k - 9, 0:T], 1.0
                if k < 16:
                    return v_all[:, k - 11, :], 1.0
                return hy[:, k - 15, :], 1.0

            def mix(p):
                l = p.l
                for step in plan:
                    kind = step[0]
                    if kind == "proj":
                        k = step[1]
                        split(p.n0 + k + AHEAD)
                        dve.wait_ge(tile_done, p.n0 + k + 1)
                        dst, s = proj_place(k)
                        dve.tensor_scalar(dst, bank[(p.n0 + k) % RING][:, 0:T], s, None, ALU.mult).then_inc(drained, 1)
                    elif kind == "fused":
                        _, i, n = step
                        at = p.n0 + FUSED0 + C * i + n
                        split(at + AHEAD)
                        dve.wait_ge(th_ready, 4 * C * l + C * i + n + 1)
                        dve.wait_ge(tile_done, at + 1)
                        a = 3 * C * l + C * (i - 1) + n
                        if i == 0:
                            dst = merged[:, n, :]
                        else:
                            dst = gated[:, n % 2, :]
                            if n >= 2 or i > 1:
                                dve.wait_ge(merged_done, a - 1)
                        dve.scalar_tensor_tensor(dst, th[:, n % 2, :], 1.0, ps_br[:, 0:T], ALU.add, ALU.mult).then_inc(drained, 1)
                    elif kind == "merged":
                        h_low(C * (4 * l + 2) + step[1], merged[:, step[1], :], step[1])
                    elif kind == "out":
                        c = step[1]
                        n = p.n0 + N_PROJ + 4 * C + c
                        if c == 0:
                            residual_gate(l, G2)
                        split(n + AHEAD)
                        add_to_x(n, c)
                    elif kind == "sinmlp":
                        j = step[1]
                        dve.wait_ge(mlp_mm, 2 * l + j + 1)
                        if l + j:
                            dve.wait_ge(mlp_sin, 2 * l + j)
                        f, b = (vv[0:HY_HID, V_MLP + 3 * l + i:V_MLP + 3 * l + i + 1] for i in (0, 1 + j))
                        link(dve.tensor_scalar(f_arg, ps_s[0:HY_HID, 0:T], b, f, ALU.add, ALU.mult))
                        link(dve.tensor_scalar(f_turn, f_arg, 1.0 / (2 * math.pi), ROUND, ALU.mult, ALU.add))
                        link(dve.tensor_scalar(f_turn, f_turn, ROUND, None, ALU.subtract))
                        for part in (TWO_PI_A, TWO_PI_B, TWO_PI_C):
                            link(dve.scalar_tensor_tensor(f_arg, f_turn, -part, f_arg, ALU.mult, ALU.add))
                        dve.tensor_scalar(f_arg, f_arg, PI_DOWN, -PI_DOWN, ALU.min, ALU.max).then_inc(mlp_arg, 1)
                    elif kind == "taps":
                        _, o, tk = step
                        q = 6 * l + 3 * o + tk
                        dve.wait_ge(win_ready, q + 1)
                        dve.wait_ge(taps_mm, q + 1)
                        link(dve.tensor_tensor(win, (ps_s, ps_br)[q % 2][:, :], win, ALU.mult))
                        if tk < 2:
                            link(dve.tensor_scalar(win[:, 256:512], win[:, 256:512], kk[:, K_TM + tk:K_TM + tk + 1], None, ALU.mult))
                        if o:
                            dve.wait_ge(filt_mm, 6 * l + 3)
                        dve.tensor_tensor(taps[:, tk, 0, :], win[:, 0:256], win[:, 256:512], ALU.add)
                        dve.tensor_tensor(taps[:, tk, 1, :], win[:, 0:256], win[:, 256:512], ALU.subtract).then_inc(taps_ready, 1)
                    elif kind == "scale":
                        o = step[1]
                        dve.wait_ge(sum_mm, 6 * l + 3 * (o + 1))
                        for g, L in enumerate((T_CTX, T_DEN)):
                            order[0] += 1
                            dve.tensor_scalar(f_inv[:, g, :], ps_t[:, 256 * g:256 * (g + 1)], EPS, float(L), ALU.add, ALU.mult).then_inc(dve_order, 1)
                        dve.wait_ge(dve_order, order[0])
                        dve.reciprocal(f_inv, f_inv).then_inc(scale_ready, 1)
                    elif kind == "filter":
                        _, o, fc = step
                        q = 6 * l + 3 * o + fc
                        dve.wait_ge(filt_mm, q + 1)
                        dve.wait_ge(scale_ready, 2 * l + o + 1)
                        g = 0 if fc == 0 else 1
                        psx = (ps_o, ps_s)[q % 2][:, :].rearrange("p (s c) -> p s c", s=2)
                        inv = f_inv[:, g:g + 1, :].broadcast_to([P, 2, 256])
                        dve.tensor_tensor(filt[:, o, fc], psx, inv, ALU.mult).then_inc(filt_ready, 1)
                    elif kind == "rope":
                        j = step[1]
                        swa = j < 3
                        tgt = (q_swa[:, 0], q_swa[:, 1], kt[:, 2], q_df[:, 0], q_df[:, 1], kt[:, 3], kt[:, 4])[j][:, T_CTX:T]
                        cos, sin = (rope_t[:, 0], rope_t[:, 1]) if swa else (rope_t[:, 2], rope_t[:, 3])
                        dve.wait_ge(rot_ready, 7 * l + j + 1)
                        order[0] += 1
                        dve.tensor_tensor(spare, ps_br[:, 0:T_DEN], sin, ALU.mult).then_inc(dve_order, 1)
                        link(dve.tensor_tensor(tgt, tgt, cos, ALU.mult))
                        dve.tensor_tensor(tgt, tgt, spare, ALU.add).then_inc(rope_done, 1)
                        dve.wait_ge(rope_done, 7 * l + j + 1)
                    elif kind == "scores":
                        _, ty, u, m = step
                        blk, hh, b = unit(u)
                        r = R_PER * l + r_index[step]
                        k0, k1 = keys(b)
                        nm = tiny[:, 8 + r % 4:9 + r % 4]
                        dve.wait_ge(scores_ready, r + 1)
                        if ty == NA and b:
                            dve.wait_ge(bias_ready, l + 1)
                            link(dve.tensor_tensor(ps_s[:, 0:256], ps_s[:, 0:256], na_bias[:, b - 1, 2 * blk + hh, :], ALU.add))
                        if ty == SWA and b:
                            c0 = 128 if b == 1 else 0
                            msk = kk[:, K_SWM + P * (b - 1):K_SWM + P * b]
                            link(dve.tensor_tensor(ps_s[:, c0:c0 + P], ps_s[:, c0:c0 + P], msk, ALU.add))
                        red = dve.tensor_reduce(nm, ps_s[:, 0:k1 - k0], AX_X, ALU.max, negate=True)
                        if ty == SWA:
                            link(red)
                            head = blk + 2 * hh
                            red = dve.scalar_tensor_tensor(nm, vcol(V_SINK + 4 * l + head), -1.0, nm, ALU.mult, ALU.min)
                        red.then_inc(max_ready, 1)
                    elif kind == "probs":
                        _, ty, u = step
                        nk_ = keys(unit(u)[2])[1] - keys(unit(u)[2])[0]
                        r = R_PER * l + r_index[("scores", ty, u, 1 if ty == DF else 0)]
                        dve.wait_ge(exp_done, r + 1)
                        rs = tiny[:, 12 + r % 4:13 + r % 4]
                        rr = tiny[:, 16 + r % 4:17 + r % 4]
                        if ty == SWA:
                            link(dve.tensor_tensor(rs, rs, tiny[:, 20 + r % 4:21 + r % 4], ALU.add))
                        link(dve.reciprocal(rr, rs))
                        if ty == DF:
                            r0 = R_PER * l + r_index[("scores", ty, u, 0)]
                            rs0, rr0 = tiny[:, 12 + r0 % 4:13 + r0 % 4], tiny[:, 16 + r0 % 4:17 + r0 % 4]
                            link(dve.reciprocal(rr0, rs0))
                            link(dve.tensor_tensor(rr, rr, tiny[:, 24 + l:25 + l], ALU.mult))
                            link(dve.tensor_scalar(pr[:, 0, 0:nk_], pr[:, 0, 0:nk_], rr0, None, ALU.mult))
                            dve.scalar_tensor_tensor(pr[:, 1, 0:nk_], pr[:, 1, 0:nk_], rr, pr[:, 0, 0:nk_], ALU.mult, ALU.add).then_inc(probs_ready, 1)
                        else:
                            dst = pr[:, u % 2, 0:nk_]
                            dve.tensor_scalar(dst, dst, rr, None, ALU.mult).then_inc(probs_ready, 1)
                    elif kind == "outs":
                        _, ty, blk = step
                        br = BR_OF[ty]
                        dve.wait_ge(o_hi_ready, 8 * l + out_pair(br, blk) + 1)
                        dve.tensor_tensor(o_lo[:, buf(br), blk, :], ps_o[:, 0:T], o_hi[:, buf(br), blk, :].bitcast(F32), ALU.subtract).then_inc(o_lo_ready, 1)
                    elif kind == "subnorm":
                        blk = step[1]
                        dve.wait_ge(t_free, T_PER * l + t_index[step] + 1)
                        link(dve.reciprocal(prT[:], prT[:]))
                        dve.scalar_tensor_tensor(prT[:], ps_o[:, 0:T], tiny[:, 26 + l:27 + l], prT[:], ALU.mult, ALU.mult).then_inc(onorm_ready, 1)
                        dve.wait_ge(o_hi_ready, 8 * l + out_pair(3, blk) + 1)
                        dve.tensor_tensor(o_lo[:, buf(3), blk, :], prT[:], o_hi[:, buf(3), blk, :].bitcast(F32), ALU.subtract).then_inc(o_lo_ready, 1)
                    elif kind == "short":
                        j = step[1]
                        z, u = hy[:, j, :], hy[:, j + 1, :]
                        w0, w1, w2, b = (vcol(V_SHORT + 24 * l + 4 * j + i) for i in range(4))
                        dve.wait_ge(drained, p.n0 + 16 + j + 1)
                        link(dve.tensor_scalar(z, u, w1, b, ALU.mult, ALU.add))
                        for w, shift in ((w0, -1), (w2, 1)):
                            for t0, t1 in GROUPS:
                                a0, a1 = (t0 + 1, t1) if shift < 0 else (t0, t1 - 1)
                                link(dve.scalar_tensor_tensor(z[:, a0:a1], u[:, a0 + shift:a1 + shift], w, z[:, a0:a1], ALU.mult, ALU.add))
                        if j in (0, 1):
                            dve.memset(tiny[:, 28:29], 0.0).then_inc(y_ready, 1)
                    elif kind == "spectrum":
                        _, o, fc = step
                        q = 6 * l + 3 * o + fc
                        Y = (ps_s, ps_o)[q % 2][:, :].rearrange("p (s c) -> p s c", s=2)
                        Fr, Fs = (filt[:, o, fc, s:s + 1, :].broadcast_to([P, 2, 256]) for s in range(2))
                        dve.wait_ge(spec_mm, q + 1)
                        if o:
                            dve.wait_ge(conv_mm, 4 * l + 2)
                        Z = spec[:, fc]
                        link(dve.tensor_tensor(Z, Y, Fr, ALU.mult))
                        link(dve.tensor_tensor(spec_t, Y, Fs, ALU.mult))
                        dve.tensor_tensor(Z[:, 0, :], Z[:, 0, :], spec_t[:, 1, :], ALU.subtract)
                        dve.tensor_tensor(Z[:, 1, :], Z[:, 1, :], spec_t[:, 0, :], ALU.add).then_inc(spec_ready, 1)
                        dve.wait_ge(spec_ready, q + 1)
                    elif kind == "conv":
                        _, o, blk = step
                        y, gate = hy[:, blk, :], hy[:, 2 + 2 * o + blk, :]
                        dve.wait_ge(conv_mm, 4 * l + 2 * o + blk + 1)
                        link(dve.scalar_tensor_tensor(y, y, vcol(V_SKIP + 4 * l + 2 * o + blk), (ps_s, ps_o)[blk][:, 0:T], ALU.mult, ALU.add))
                        dve.tensor_tensor(y, y, gate, ALU.mult).then_inc(y_ready, 1)
                        dve.wait_ge(y_ready, 6 * l + 2 + 2 * o + blk + 1)
                    elif kind == "hyout":
                        blk = step[1]
                        dve.wait_ge(o_hi_ready, 8 * l + out_pair(2, blk) + 1)
                        dve.tensor_tensor(o_lo[:, buf(2), blk, :], hy[:, blk, :], o_hi[:, buf(2), blk, :].bitcast(F32), ALU.subtract).then_inc(o_lo_ready, 1)

            spare = areaM[:, 2816:3072]
            for p in PHASES:
                if p.kind == "ada":
                    for j in range(p.tiles):
                        n = p.n0 + j
                        split(n + AHEAD)
                        dve.wait_ge(tile_done, n + 1)
                        dve.tensor_copy(mod[:, p.m % 72 + j, :], bank[n % RING][:, 0:2]).then_inc(drained, 1)
                    dve.wait_ge(drained, p.n0 + p.tiles)
                elif p.kind == "norm":
                    norm(p)
                elif p.kind == "up":
                    up(p)
                elif p.kind == "down":
                    down(p)
                    dve.wait_ge(drained, p.n0 + p.tiles)
                else:
                    mix(p)
                    dve.wait_ge(drained, p.n0 + p.tiles)

        @block.gpsimd
        def _(pool):
            def up(p):
                with pool.Fori(0, p.iters) as i:
                    for s in range(2):
                        f = fcount(p) + s
                        per = 8 if p.ada else 4
                        n = p.n0 + per // 4 * (2 * s + 1)
                        pool.wait_ge(gf_ready, f + 1 + 2 * i)
                        pool.wait_ge(drained, n + 1 + per * i)
                        at = bass.ds(p.f0 + s + 2 * i, 1)
                        pool.tensor_tensor(g_lo[:, at, :].rearrange("p a t -> p (a t)"), gf[:, s, :],
                                           g_hi[:, at, :].rearrange("p a t -> p (a t)").bitcast(F32), ALU.subtract).then_inc(g_lo_ready, 1)

            def layer_loads(l):
                if l:
                    pool.wait_ge(tile_done, MIX_N0[l - 1] + N_PROJ + 5 * C)
                pool.dma_start(areaE[:, 0:2048], bias[l]).then_inc(ctx_in, 16)
                pool.dma_start(areaE[:, 2048:3072], rope).then_inc(ctx_in, 16)
                pool.dma_start(kt[:, :, T:512], kctx[l]).then_inc(ctx_in, 16)
                pool.dma_start(vt[:, 3, :], vctx[l]).then_inc(ctx_in, 16)
                pool.wait_ge(ctx_in, 64 * (l + 1))
                m = kk[:, K_NAM:K_NAM + 256].unsqueeze(1).broadcast_to([P, 8, 256])
                b8 = areaE[:, 0:2048].rearrange("p (b k) -> p b k", b=8)
                if l == 0:
                    pool.wait_ge(consts_in, 64)
                pool.tensor_tensor(b8, b8, m, ALU.add).then_inc(bias_ready, 1)

            def mix(p):
                l = p.l
                pool.wait_ge(h_lo_ready, C * (4 * l + 1) + C)
                pool.dma_start(fw1, mlp_w[l, 0:HY_EMB, 0:64]).then_inc(filt_in, 16)
                pool.dma_start(z_t, zt).then_inc(filt_in, 16)
                pool.dma_start(fw2, mlp_w[l, 0:HY_HID, 64:128]).then_inc(filt_in, 16)
                pool.dma_start(rate, logdecay[l]).then_inc(filt_in, 16)
                pool.dma_start(fw3, mlp_w3[l]).then_inc(filt_in, 16)
                pool.dma_start(dft_t, dft).then_inc(filt_in, 16)
                for step in plan:
                    if step[0] == "vk" and step[1] in (1, 2, 4):
                        ty = (1, 2, 4).index(step[1])
                        a, b = ((0, 2), (2, 3), (3, 5))[ty]
                        pool.wait_ge(t_free, T_PER * l + t_index[step] + 1)
                        src = k_tok[:, a:b, :].rearrange("p j t -> p (j t)").rearrange("p (h d) -> p h d", d=64)
                        pool.dma_start(nk[ty][l].rearrange("h s d -> s h d"), src).then_inc(kv_out, 16)
                        src = vt[:, 0, P * a:P * b].rearrange("p (h d) -> p h d", d=64)
                        pool.dma_start(nv[ty][l].rearrange("h s d -> s h d"), src).then_inc(kv_out, 16)
                    elif step[0] == "fused" and step[1]:
                        _, i, n = step
                        a = 3 * C * l + C * (i - 1) + n
                        pool.wait_ge(drained, p.n0 + FUSED0 + C * i + n + 1)
                        if a:
                            pool.wait_ge(merged_done, a)
                        pool.tensor_tensor(merged[:, n, :], merged[:, n, :], gated[:, n % 2, :], ALU.add).then_inc(merged_done, 1)

            for p in PHASES:
                if p.kind == "up":
                    if p.first and p.ffn == 0:
                        layer_loads(p.l)
                    if p.first and p.ffn == 1:
                        pool.wait_ge(kv_out, 16 * 6 * (p.l + 1))
                    up(p)
                elif p.kind == "mix":
                    mix(p)
            pool.wait_ge(kv_out, 16 * 6 * DEPTH)

        @block.tensor
        def _(pe):
            def ready(base, rep=0):
                pe.wait_ge(lo_ready, base + 1 + 4 * rep)
                if base >= RING:
                    pe.wait_ge(drained, base - RING + 1 + 4 * rep)

            def tile(base, a_hi, a_lo, chunks, cols, before=None, off=0, out=None, count=True):
                slot = base % RING
                dst = (bank[slot] if out is None else out)[:, 0:cols]
                for c in range(chunks):
                    if before is not None:
                        before(c)
                    w = slice(off + P * c, off + P * (c + 1))
                    for k, (wt, ac) in enumerate(((hi, a_hi), (hi, a_lo), (lo, a_hi))):
                        last = pe.matmul(dst, wt[:, slot, w], ac[:, c, :], start=c == 0 and k == 0, stop=c == chunks - 1 and k == 2)
                return last.then_inc(tile_done, 1) if count else last

            def norm(p):
                k = nidx(p)
                for c in range(C):
                    pe.wait_ge(sq_ready, C * k + c + 1)
                    last = pe.matmul(ps_o[:, 0:T], ones, sq[:, c, :], start=c == 0, stop=c == C - 1)
                last.then_inc(ss_ready, 1)

            def up(p):
                def first(c):
                    if p.first:
                        pe.wait_ge(h_lo_ready, hp8(p) + c + 1)

                per = 8 if p.ada else 4
                with pe.Fori(0, p.iters) as i:
                    for j in range(per):
                        ready(p.n0 + j, per // 4 * i)
                        if p.ada and j in (0, 4) and fcount(p) + j // 4 >= 1:
                            pe.wait_ge(silu_done, fcount(p) + j // 4 + 2 * i)
                        if not (p.ada and j % 2):
                            tile(p.n0 + j, h_hi, h_lo, C, T, first if j == 0 else None)
                        else:
                            tile(p.n0 + j, c_hi, c_lo, C, 2)

            def down(p):
                f = FB * p.q + sum(THIRDS[:p.third])

                def product(c):
                    pe.wait_ge(g_lo_ready, f + c + 1)

                pe.wait_ge(silu_done, f + THIRDS[p.third])
                with pe.Fori(0, 2) as i:
                    for j in range(4):
                        ready(p.n0 + j, i)
                        tile(p.n0 + j, g_hi, g_lo, THIRDS[p.third], T, product if j == 0 else None)

            def mix(p):
                l = p.l

                def have(k):
                    pe.wait_ge(drained, p.n0 + k + 1)

                for step in plan:
                    kind = step[0]
                    if kind == "proj":
                        k = step[1]
                        ready(p.n0 + k)
                        tile(p.n0 + k, h_hi, h_lo, C, T, (lambda c: pe.wait_ge(h_lo_ready, C * (4 * l + 1) + c + 1)) if k == 0 else None)
                    elif kind == "fused":
                        _, i, n = step
                        at = p.n0 + FUSED0 + C * i + n
                        ready(at)
                        tile(at, h_hi, h_lo, C, T, count=False)
                        br = BRANCH_ORDER[i]
                        pe.wait_ge(o_lo_ready, 8 * l + 2 * i + 2)
                        pe.wait_ge(drained, at)
                        if i == 0 and n == 0:
                            pe.wait_ge(rope_done, 7 * (l + 1))
                        tile(at, o_hi[:, buf(br)], o_lo[:, buf(br)], 2, T, off=D, out=ps_br)
                    elif kind == "out":
                        c = step[1]
                        ready(p.n0 + N_PROJ + 4 * C + c)
                        tile(p.n0 + N_PROJ + 4 * C + c, h_hi, h_lo, C, T,
                             (lambda k: pe.wait_ge(h_lo_ready, C * (4 * l + 2) + k + 1)) if c == 0 else None)
                    elif kind == "sinmlp":
                        j = step[1]
                        if j == 0:
                            pe.wait_ge(filt_in, 16 * 6 * (l + 1))
                            pe.matmul(ps_s[0:HY_HID, 0:T], fw1, z_t, start=True, stop=True).then_inc(mlp_mm, 1)
                        else:
                            pe.wait_ge(mlp_sin, 2 * l + 1)
                            pe.matmul(ps_s[0:HY_HID, 0:T], fw2, fg, start=True, stop=True).then_inc(mlp_mm, 1)
                    elif kind == "taps":
                        _, o, tk = step
                        q = 6 * l + 3 * o + tk
                        pe.wait_ge(mlp_sin, 2 * l + 2)
                        pe.wait_ge(mlp_arg, 2 * l + 2)
                        if q >= 2:
                            pe.wait_ge(taps_ready, q - 1)
                        if o:
                            pe.wait_ge(filt_ready, 6 * l + 3)
                        if l:
                            pe.wait_ge(drained, p.n0)
                        pe.matmul((ps_s, ps_br)[q % 2][:, :], fg[:, P * tk:P * (tk + 1)], fw3[:, 512 * o:512 * (o + 1)],
                                  start=True, stop=True).then_inc(taps_mm, 1)
                        pe.wait_ge(abs_ready, q + 1)
                        if o and tk == 0:
                            pe.wait_ge(scale_ready, 2 * l + 1)
                        g = 0 if tk == 0 else 1
                        for s in range(2):
                            last = pe.matmul(ps_t[:, 256 * g:256 * (g + 1)], ones, hab[:, 256 * s:256 * (s + 1)],
                                             start=s == 0 and tk < 2, stop=s == 1 and tk != 1)
                        last.then_inc(sum_mm, 1)
                    elif kind == "filter":
                        _, o, fc = step
                        q = 6 * l + 3 * o + fc
                        pe.wait_ge(taps_ready, 6 * l + 3 * (o + 1))
                        if q >= 2:
                            pe.wait_ge(filt_ready, q - 1)
                        dst = (ps_o, ps_s)[q % 2]
                        for s in range(2):
                            if fc == 0:
                                last = pe.matmul(dst[:, 256 * s:256 * (s + 1)], dft_t[:, P * s:P * (s + 1)], taps[:, 0, s, :], start=True, stop=True)
                            else:
                                for tk in range(2):
                                    a = 256 + 512 * s + 256 * tk + P * (fc - 1)
                                    last = pe.matmul(dst[:, 256 * s:256 * (s + 1)], dft_t[:, a:a + P], taps[:, 1 + tk, s, :],
                                                     start=tk == 0, stop=tk == 1)
                        last.then_inc(filt_mm, 1)
                    elif kind == "vk":
                        j, t = step[1], T_PER * l + t_index[step]
                        have((5, 5, 9, 15, 15)[j])
                        if t:
                            pe.wait_ge(t_free, t)
                        pe.wait_ge(scale_ready, 2 * (l + 1))
                        for tk in range(TB):
                            pe.transpose(ps_t[:, P * tk:P * (tk + 1)], v_all[:, j, P * tk:P * (tk + 1)], ident)
                        pe.transpose(ps_t[:, 3 * P:4 * P], kt[:, j, 0:P], ident).then_inc(t_ready, 1)
                    elif kind == "rope":
                        j = step[1]
                        src = (q_swa[:, 0], q_swa[:, 1], kt[:, 2], q_df[:, 0], q_df[:, 1], kt[:, 3], kt[:, 4])[j][:, T_CTX:T]
                        have(15)
                        pe.wait_ge(ctx_in, 64 * (l + 1))
                        pe.wait_ge(taps_ready, 6 * (l + 1))
                        if j + l:
                            pe.wait_ge(rope_done, 7 * l + j)
                        r = kk[:, K_R64:K_R64 + P] if j < 3 else kk[:, K_R32:K_R32 + P]
                        pe.matmul(ps_br[:, 0:T_DEN], r, src, start=True, stop=True).then_inc(rot_ready, 1)
                    elif kind == "scores":
                        _, ty, u, m = step
                        blk, hh, b = unit(u)
                        r = R_PER * l + r_index[step]
                        q = (q_na, q_swa, q_df)[ty]
                        kb = (blk, 2, 3 + blk)[ty]
                        if ty == NA:
                            have(5)
                        else:
                            pe.wait_ge(rope_done, 7 * (l + 1))
                        pe.wait_ge(ctx_in, 64 * (l + 1))
                        pe.wait_ge(filt_ready, 6 * (l + 1))
                        if r:
                            pe.wait_ge(exp_done, r)
                        k0, k1 = keys(b)
                        a = 64 * hh + 32 * m
                        e = a + (32 if ty == DF else 64)
                        pe.matmul(ps_s[:, 0:k1 - k0], q[a:e, blk, P * b:P * (b + 1)], kt[a:e, kb, k0:k1], start=True, stop=True).then_inc(scores_ready, 1)
                    elif kind == "turn":
                        _, ty, u = step
                        b = unit(u)[2]
                        t, g = T_PER * l + t_index[step], U_PER * l + 12 * ty + u
                        pe.wait_ge(probs_ready, g + 1)
                        pe.wait_ge(t_free, t)
                        n = (keys(b)[1] - keys(b)[0]) // P
                        for i in range(n):
                            last = pe.transpose(ps_t[:, P * i:P * (i + 1)], pr[:, 1 if ty == DF else u % 2, P * i:P * (i + 1)], ident)
                        last.then_inc(t_ready, 1)
                    elif kind == "values":
                        _, ty, u = step
                        blk, hh, b = unit(u)
                        pe.wait_ge(t_free, T_PER * l + t_index[("turn", ty, u)] + 1)
                        if u % 6 == 0:
                            pe.wait_ge(o_lo_ready, 8 * l + 2 * ty + blk)
                            if ty == NA:
                                pe.wait_ge(filt_ready, 6 * (l + 1))
                        col = (64 * (2 * blk + hh), 256 + 64 * hh, 384 + 64 * (2 * blk + hh))[ty]
                        chunks = (0,) if b == 0 else (1, 2, 3)
                        for i, ch in enumerate(chunks):
                            last = pe.matmul(ps_o[64 * hh:64 * hh + 64, P * b:P * (b + 1)], vt[:, ch, col:col + 64], prT[:, P * i:P * (i + 1)],
                                             start=i == 0, stop=i == len(chunks) - 1)
                        last.then_inc(values_done, 1)
                    elif kind == "subnorm":
                        blk, t = step[1], T_PER * l + t_index[step]
                        pe.wait_ge(osq_ready, 2 * l + blk + 1)
                        pe.wait_ge(t_free, t)
                        pe.matmul(ps_t[:, 0:T], bones, prT[:], start=True, stop=True).then_inc(t_ready, 1)
                    elif kind == "ytok":
                        _, o, blk = step
                        pe.wait_ge(y_ready, 6 * l + 2 * o + blk + 1)
                        pe.wait_ge(t_free, T_PER * l + t_index[step])
                        for tk in range(TB):
                            last = pe.transpose(ps_t[:, P * tk:P * (tk + 1)], hy[:, blk, P * tk:P * (tk + 1)], ident)
                        last.then_inc(t_ready, 1)
                    elif kind == "spectrum":
                        _, o, fc = step
                        q = 6 * l + 3 * o + fc
                        pe.wait_ge(t_free, T_PER * l + t_index[("ytok", o, 1)] + 1)
                        pe.wait_ge(exp_done, R_PER * (l + 1))
                        pe.wait_ge(o_lo_ready, 8 * l + 6)
                        if o:
                            pe.wait_ge(y_ready, 6 * l + 4)
                        if q >= 2:
                            pe.wait_ge(spec_ready, q - 1)
                        dst = (ps_s, ps_o)[q % 2]
                        for s in range(2):
                            if fc == 0:
                                a = (K_CP, K_SP)[s]
                                last = pe.matmul(dst[:, 256 * s:256 * (s + 1)], kk[:, a:a + P], y_tok[:, 0, :], start=True, stop=True)
                            else:
                                for tk in range(2):
                                    a = (K_CS, K_SS)[s] + 256 * tk + P * (fc - 1)
                                    last = pe.matmul(dst[:, 256 * s:256 * (s + 1)], kk[:, a:a + P], y_tok[:, 1 + tk, :], start=tk == 0, stop=tk == 1)
                        last.then_inc(spec_mm, 1)
                    elif kind == "conv":
                        _, o, blk = step
                        pe.wait_ge(spec_ready, 6 * l + 3 * (o + 1))
                        dst = (ps_s, ps_o)[blk]
                        for s in range(2):
                            a = (K_CP, K_SP)[s]
                            pe.matmul(dst[:, 0:T_CTX], spec[:, 0, s, P * blk:P * (blk + 1)], kk[:, a:a + P], start=s == 0, stop=s == 1)
                        for fc in range(2):
                            for s in range(2):
                                a = (K_CS, K_SS)[s] + 256 * fc
                                last = pe.matmul(dst[:, T_CTX:T], spec[:, 1 + fc, s, P * blk:P * (blk + 1)], kk[:, a:a + T_DEN],
                                                 start=fc + s == 0, stop=fc + s == 2)
                        last.then_inc(conv_mm, 1)

            pe.wait_ge(consts_in, 64)
            pe.wait_ge(cond_lo, 1)
            for p in PHASES:
                if p.kind == "ada":
                    for j in range(p.tiles):
                        ready(p.n0 + j)
                        tile(p.n0 + j, c_hi, c_lo, C, 2)
                elif p.kind == "norm":
                    norm(p)
                elif p.kind == "up":
                    up(p)
                elif p.kind == "down":
                    down(p)
                else:
                    mix(p)


NORM_PHASES = [p for p in PHASES if p.kind == "norm"]


def nidx(p):
    return [id(q) for q in NORM_PHASES].index(id(p))


def hp8(p):
    if p.kind == "norm":
        return C * p.hp
    return C * (4 * p.l + (0 if p.ffn == 0 else 3))


def norm_n0(p):
    return p.n0 - (4 if p.which == 1 else 0)



def shape_constants():
    k = np.zeros((P, K_COLS), np.float64)
    i = np.arange(P)
    k[:, K_ID:K_ID + P] = np.eye(P)
    k[:, K_ONES:K_ONES + P] = 1
    k[:, K_BONES:K_BONES + P] = (i[:, None] // 64) == (i[None, :] // 64)
    for col, dh in ((K_R64, 64), (K_R32, 32)):
        nf = dh // 4
        r = np.zeros((P, P))
        for m in range(P):
            if (m // nf) % 2 == 0:
                r[m + nf, m] = -1
            else:
                r[m - nf, m] = 1
        k[:, col:col + P] = r
    qc, kc = i % GRID_W, np.arange(256) % GRID_W
    c0 = np.clip(qc - WIN_C // 2, 0, GRID_W - WIN_C)
    ok = (kc[None, :] >= c0[:, None]) & (kc[None, :] < c0[:, None] + WIN_C)
    k[:, K_NAM:K_NAM + 256] = np.where(ok, 0, NEG)
    k[:, K_SWM:K_SWM + P] = np.where(i[None, :] <= i[:, None], 0, NEG)
    k[:, K_SWM + P:K_SWM + 2 * P] = np.where(i[:, None] <= i[None, :], 0, NEG)

    def half(L, fn):
        a = np.arange(L)
        return fn(math.pi * np.outer(2 * a + 1, 2 * a + 1) / (4 * L))

    def whole(L, fn):
        a = np.arange(L)
        return fn(math.pi * np.outer(a, 2 * a + 1) / (2 * L))

    def rows(m):
        return m.reshape(2, P, 256).transpose(1, 0, 2).reshape(P, 512)

    k[:, K_CP:K_CP + P], k[:, K_SP:K_SP + P] = half(T_CTX, np.cos), half(T_CTX, np.sin)
    k[:, K_CS:K_CS + 512], k[:, K_SS:K_SS + 512] = rows(half(T_DEN, np.cos)), rows(half(T_DEN, np.sin))
    t = np.stack([i / T_CTX, i / T_DEN, (i + P) / T_DEN], 1)
    k[:, K_NTN:K_NTN + 3] = -t
    k[:, K_TM:K_TM + 3] = 1
    k[0, K_TM:K_TM + 2] = 0
    k[:, K_EPS] = EPS
    dft = np.concatenate([whole(T_CTX, np.cos), whole(T_CTX, np.sin), rows(whole(T_DEN, np.cos)), rows(whole(T_DEN, np.sin))], 1)
    tok = np.arange(T_DEN)
    rope = np.zeros((P, 4, T_DEN))
    for j, dh in ((0, 64), (2, 32)):
        nf = dh // 4
        f = (10000.0 ** (-np.arange(nf, dtype=np.float32) / nf)).astype(np.float32)
        for m in range(P):
            pos = (tok // GRID_W if (m % dh) < dh // 2 else tok % GRID_W).astype(np.float32)
            ang = (pos * f[m % nf]).astype(np.float32).astype(np.float64)
            rope[m, j], rope[m, j + 1] = np.cos(ang), np.sin(ang)
    z = []
    for L in (T_CTX, T_DEN):
        tn = (np.arange(L, dtype=np.float32) / L)
        ang = (np.float32(2.0 * math.pi) * tn[:, None] * np.arange(1, HY_FREQS + 1, dtype=np.float32)[None, :]).astype(np.float64)
        z.append(np.concatenate([tn[:, None], np.cos(ang), np.sin(ang)], 1))
    z = np.concatenate(z, 0).T
    f = lambda a: np.ascontiguousarray(a, dtype=np.float32)
    return f(k), f(dft), f(rope.reshape(P, 4 * T_DEN)), f(z)


def kernel(**inp):
    import concourse.bacc as bacc
    from concourse.bass_utils import run_bass_kernel_spmd as run

    a = {k: np.asarray(v) for k, v in inp.items()}
    f32 = np.float32

    def blocks(w):
        K, N = w.shape
        return w.reshape(K // P, P, N // P, P).transpose(2, 1, 0, 3).reshape(N // P, P, K)

    def cols(v):
        return v.reshape(-1, P).T

    n_main = N_TILES - len(WIDE)
    w_main = np.zeros((n_main, P, 1024), f32)
    w_fused = np.zeros((DEPTH * 4 * C, P, 1280), f32)
    ada = np.concatenate([blocks(a["w_ada"][l]) for l in range(DEPTH)])
    at = 0
    heads = np.r_[0:64, 128:192, 64:128, 192:256]
    for p in PHASES:
        if p.kind == "ada":
            w_main[at:at + p.tiles] = ada[p.m:p.m + p.tiles]
            at += p.tiles
        elif p.kind == "up":
            w1, w3 = (blocks(a[f"ffn{p.ffn + 1}_{w}"][p.l]) for w in ("w1", "w3"))
            fb = sum(THIRDS[:p.third]) + p.f0
            for i in range(p.iters):
                for s in range(2):
                    for w in (w1, w3):
                        w_main[at] = w[fb + 2 * i + s]
                        at += 1
                        if p.ada:
                            w_main[at] = ada[p.m + 4 * i + 2 * s + (w is w3)]
                            at += 1
        elif p.kind == "down":
            r0 = P * sum(THIRDS[:p.third])
            k = P * THIRDS[p.third]
            w_main[at:at + C, :, 0:k] = blocks(a[f"ffn{p.ffn + 1}_w2"][p.l][r0:r0 + k])
            at += C
        elif p.kind == "mix":
            w = blocks(a["w_in"][p.l])
            q = a["w_in"][p.l][:, 768:1024][:, heads]
            w[6:8] = blocks(q)
            w_main[at:at + 10] = w[0:10]
            w_main[at + 10:at + 16] = w[16:22]
            w_main[at + 16:at + 22] = w[10:16]
            at += N_PROJ
            for i, br in enumerate(BRANCH_ORDER):
                wb = a["w_branch"][p.l, br]
                if br == 1:
                    wb = wb[heads]
                dst = w_fused[4 * C * p.l + C * i:4 * C * p.l + C * (i + 1)]
                dst[:, :, 0:1024] = w[22 + C * br:22 + C * (br + 1)]
                dst[:, :, 1024:] = blocks(wb)
            w_main[at:at + C] = blocks(a["w_out"][p.l])
            at += C
    assert at == n_main

    consts, dft, rope, zt = shape_constants()
    v = np.zeros((P, V_COLS), f32)
    v[:, V_COND:V_COND + 2 * C] = np.stack([cols(a["c_ctx"]), cols(a["c"][0])], 2).reshape(P, 2 * C)
    lam = np.zeros((P, DEPTH * 128), f32)
    mlp_w = np.zeros((DEPTH, 64, 128), f32)
    d_row = np.arange(4)[None, :] - np.arange(4)[:, None] + WIN_R - 1
    d_col = np.clip(np.arange(GRID_W)[None, :] - np.arange(GRID_W)[:, None] + WIN_C - 1, 0, 2 * WIN_C - 2)
    bias = np.zeros((DEPTH, P, 2, 4, 256), f32)
    kctx = np.zeros((DEPTH, P, 5, P), f32)
    vctx = np.zeros((DEPTH, P, 640), f32)
    for l in range(DEPTH):
        v[:, V_BADA + 72 * l:V_BADA + 72 * (l + 1)] = cols(a["b_ada"][l])
        for i, nm in enumerate(("norm_ffn1", "norm_mix", "norm_ffn2")):
            v[:, V_NORM + 24 * l + 8 * i:V_NORM + 24 * l + 8 * (i + 1)] = cols(a[nm][l])
        short = np.stack([cols(a["hy_short_w"][l, i]) for i in range(3)] + [cols(a["hy_short_b"][l])], 2)
        v[:, V_SHORT + 24 * l:V_SHORT + 24 * (l + 1)] = short.reshape(P, 24)
        v[:, V_SKIP + 4 * l:V_SKIP + 4 * (l + 1)] = np.concatenate([cols(a["hy_skip"][l, o]) for o in range(2)], 1)
        for i, nm in enumerate(("hy_sin_freq", "hy_b1", "hy_b2")):
            v[0:64, V_MLP + 3 * l + i] = a[nm][l]
        v[:, V_SUBLN + l] = np.tile(a["diff_subln"][l], 2)
        v[:, V_SINK + 4 * l:V_SINK + 4 * (l + 1)] = a["swa_sink"][l][None, :]
        lam[:, 128 * l:128 * (l + 1)] = a["diff_lambda"][l].reshape(1, 128)
        mlp_w[l, 0:HY_EMB, 0:64], mlp_w[l, :, 64:128] = a["hy_w1"][l], a["hy_w2"][l]
        e = a["na_rpb"][l][:, d_row[:, None, :, None], d_col[None, :, None, :]]
        bias[l] = e.reshape(4, 2, P, 256).transpose(2, 1, 0, 3)
        kc = [a[f"cache_{nm}_k"][0, l].transpose(0, 2, 1).reshape(-1, P, PAST) for nm in ("na", "swa", "diff")]
        kctx[l] = np.concatenate(kc).transpose(1, 0, 2)
        vc = [a[f"cache_{nm}_v"][0, l].transpose(1, 0, 2).reshape(PAST, -1) for nm in ("na", "swa", "diff")]
        vctx[l] = np.concatenate(vc, 1)
    v[:, V_FIN:V_FIN + C] = cols(a["final_norm"])
    xs = np.concatenate([a["x_prompt"][0], a["x_sample"][0]], 0)
    x_in = xs.T.reshape(C, P, T).transpose(1, 0, 2).reshape(P, C * T)
    logdecay = np.broadcast_to(a["hy_log_decay"][:, None, :], (DEPTH, P, 1024))

    arrays = dict(w_main=w_main, w_fused=w_fused, consts=consts, vecs=v, lam=lam, x_in=x_in, rope=rope,
                  bias=bias.reshape(DEPTH, P, 2048), logdecay=logdecay, kctx=kctx, vctx=vctx,
                  mlp_w=mlp_w, mlp_w3=a["hy_w3"], zt=zt, dft=dft)
    arrays = {k: np.ascontiguousarray(w) for k, w in arrays.items()}
    nc = bacc.Bacc("TRN2", target_bir_lowering=False, num_devices=1)
    ins = [nc.dram_tensor(k, w.shape, mybir.dt.from_np(w.dtype), kind="ExternalInput").ap() for k, w in arrays.items()]
    y_out = nc.dram_tensor("y_out", (P, C * T), F32, kind="ExternalOutput").ap()
    kv = {}
    for nm, h in (("na", 4), ("swa", 2), ("diff", 4)):
        for w in "kv":
            kv[nm + w] = nc.dram_tensor(f"new_{nm}_{w}", (DEPTH, h, T_CTX, 64), F32, kind="ExternalOutput").ap()
    build(nc, *ins, y_out, [kv["nak"], kv["swak"], kv["diffk"]], [kv["nav"], kv["swav"], kv["diffv"]])
    r = run(nc, [arrays], core_ids=[0]).results[0]
    y = r["y_out"].reshape(P, C, T).transpose(2, 1, 0).reshape(T, D)
    return (y[None, 0:T_CTX], y[None, T_CTX:T], r["new_na_k"][None], r["new_na_v"][None], r["new_swa_k"][None],
            r["new_swa_v"][None], r["new_diff_k"][None], r["new_diff_v"][None])
```

```python
import math
from contextlib import ExitStack

import numpy as np
import concourse.bass as bass
from concourse import mybir

F32 = mybir.dt.float32
F32R = mybir.dt.float32r
ALU = mybir.AluOpType
ACT = mybir.ActivationFunctionType
AX_X = mybir.AxisListType.X

D, T_CTX, T_DEN, DEPTH, PAST = 1024, 128, 256, 2, 128
GRID_W, WIN_R, WIN_C = 64, 8, 16
D_FF = 2816
P = 128
T = T_CTX + T_DEN
TB = T // P
C = D // P
FB = D_FF // P
N_MOD = 9
EPS = 1e-6
NEG = -1e30
HY_FREQS, HY_EMB, HY_HID = 16, 33, 64
GROUPS = ((0, T_CTX), (T_CTX, T))
RING = 4
AHEAD = RING - 1
PARTS = 4
FILTER_TILES = 12
POOL_FROM = 640
THIRDS = (8, 8, 6)
SH1, SC1, G1, SH2, SC2, G2, SH3, SC3, G3 = range(N_MOD)
N_PROJ = 22
BRANCH_ORDER = (0, 1, 3, 2)
NA, SWA, DF = range(3)
LAM_INIT = [0.8 - 0.6 * math.exp(-0.3 * l) for l in range(DEPTH)]

K_ID, K_ONES, K_BONES, K_R64, K_R32 = (P * i for i in range(5))
K_NAM = 5 * P
K_SWM = K_NAM + 256
K_CP = K_SWM + 256
K_SP = K_CP + P
K_CS = K_SP + P
K_SS = K_CS + 512
K_NTN = K_SS + 512
K_TM = K_NTN + 3
K_EPS = K_TM + 3
K_SEL = K_EPS + 1
K_COLS = K_SEL + 2
V_COND = 0
V_BADA = V_COND + 2 * C
V_NORM = V_BADA + DEPTH * N_MOD * C
V_FIN = V_NORM + DEPTH * 3 * C
V_SHORT = V_FIN + C
V_SKIP = V_SHORT + DEPTH * 24
V_MLP = V_SKIP + DEPTH * 4
V_SUBLN = V_MLP + DEPTH * 3
V_SINK = V_SUBLN + DEPTH
V_LAM = V_SINK + DEPTH * 4
V_COLS = V_LAM
TWO_PI_A = 6.28125
TWO_PI_B = float(np.float32(np.floor((2 * math.pi - TWO_PI_A) * 2 ** 20) / 2 ** 20))
TWO_PI_C = 2 * math.pi - TWO_PI_A - TWO_PI_B
ROUND = 1.5 * 2 ** 23
PI_DOWN = 3.1415925


class Phase:

    def __init__(self, kind, n0, tiles, l=0, which=0, hp=0, ffn=0, q=0, third=0, iters=0, ada=False, m=0, first=False, f0=0):
        self.kind, self.n0, self.tiles, self.l, self.which, self.hp = kind, n0, tiles, l, which, hp
        self.ffn, self.q, self.third, self.iters, self.ada, self.m, self.first, self.f0 = ffn, q, third, iters, ada, m, first, f0


def phases():
    out, n, ada_at = [], 0, 0

    def add(kind, tiles=0, **more):
        nonlocal n
        out.append(Phase(kind, n, tiles, **more))
        n += tiles

    def ada(count):
        nonlocal ada_at
        m = ada_at
        ada_at += count
        return m

    add("ada", 2 * C, m=ada(2 * C), l=0)
    for l in range(DEPTH):
        add("norm", l=l, which=0, hp=4 * l)
        for third, fbs in enumerate(THIRDS):
            for f0, iters in ((0, 1), (2, fbs // 2 - 1)) if l + third == 0 else ((0, fbs // 2),):
                add("up", 8 * iters, l=l, ffn=0, q=2 * l, third=third, iters=iters, ada=True, m=ada(4 * iters),
                    first=third + f0 == 0, f0=f0)
            add("down", C, l=l, ffn=0, q=2 * l, third=third)
        add("norm", l=l, which=1, hp=4 * l + 1)
        add("mix", N_PROJ + 5 * C + 4, l=l, m=ada(4))
        add("norm", l=l, which=2, hp=4 * l + 3)
        left = (3 * C if l + 1 < DEPTH else C) // 4
        for third, fbs in enumerate(THIRDS):
            k = min(left, fbs // 2)
            left -= k
            f0 = 0
            while k:
                run = min(k, (N_MOD * C - ada_at % (N_MOD * C)) // 4)
                add("up", 8 * run, l=l, ffn=1, q=2 * l + 1, third=third, iters=run, ada=True, m=ada(4 * run),
                    first=third == 0 and f0 == 0, f0=f0)
                k, f0 = k - run, f0 + 2 * run
            if f0 < fbs:
                add("up", 2 * (fbs - f0), l=l, ffn=1, q=2 * l + 1, third=third, iters=(fbs - f0) // 2, ada=False,
                    first=third == 0 and f0 == 0, f0=f0)
            add("down", C, l=l, ffn=1, q=2 * l + 1, third=third)
    add("norm", l=DEPTH - 1, which=3, hp=4 * DEPTH)
    return out, n


PHASES, N_TILES = phases()
MIX_N0 = [p.n0 for p in PHASES if p.kind == "mix"]
WIDE = {n0 + N_PROJ + j for n0 in MIX_N0 for j in range(4 * C)}


def width(n):
    return 1280 if n in WIDE else 1024


def parts(tiles):
    return [(*t, part) for t in tiles for part in range(PARTS)]


def spread(tiles, side):
    out, done = [], 0
    side = [s for x in side for s in (x * [None] if isinstance(x, int) else [x])]
    tiles = parts(tiles)
    for i, t in enumerate(tiles):
        upto = (i + 1) * len(side) // len(tiles)
        out += side[done:upto]
        done = upto
        out.append(t)
    return [s for s in out + side[done:] if s is not None]


def attention_steps(kind):
    units = [(blk, hh, b) for blk in range(2) for hh in range(2) for b in range(TB)]
    out = []
    if kind == DF:
        out += [("scores", kind, 0, 0), ("scores", kind, 0, 1)]
        for u in range(12):
            out.append(("probs", kind, u))
            if u + 1 < 12:
                out.append(("scores", kind, u + 1, 0))
            out.append(("turn", kind, u))
            if u + 1 < 12:
                out.append(("scores", kind, u + 1, 1))
            out.append(("values", kind, u))
            if u % 6 == 5:
                out += [("square", u // 6), ("subnorm", u // 6)]
        return out
    out += [("scores", kind, 0, 0), ("probs", kind, 0)]
    for u in range(12):
        if u + 1 < 12:
            out.append(("scores", kind, u + 1, 0))
        out.append(("turn", kind, u))
        if u + 1 < 12:
            out.append(("probs", kind, u + 1))
        out.append(("values", kind, u))
        if u % 6 == 5:
            out.append(("outs", kind, u // 6))
    return out


def mix_plan():
    fil = [4, ("sinmlp", 0), 6, ("sinmlp", 1), 5]
    for o in range(2):
        for tk in range(TB):
            fil += [("taps", o, tk), 2, ("tapsum", o, tk)]
        fil += [("scale", o), 4] + [("filter", o, fc) for fc in range(TB)]
    proj = [("proj", k) for k in range(N_PROJ)]
    plan = spread(proj[:FILTER_TILES], fil)
    na = attention_steps(NA)
    turns = [("vk", 2), ("vk", 3), ("vk", 4)] + [("rope", j) for j in range(7)]
    plan += [("vk", 0), ("vk", 1)] + spread(proj[FILTER_TILES:16], na[:20])
    plan += spread(proj[16:], [s for pair in zip(turns, na[20:20 + len(turns)]) for s in pair] + na[20 + len(turns):])
    gates = [[("fused", i, n) for n in range(C)] for i in range(4)]
    swa, df = attention_steps(SWA), attention_steps(DF)
    short = [("short", j) for j in range(6)]
    for j in range(6):
        df.insert(9 * (j + 1), short[j])
    plan += spread(gates[0] + gates[1], swa + df)
    hy = []
    for o in range(2):
        hy += [("ytok", o, 0), ("ytok", o, 1), 2]
        for fc in range(TB):
            hy += [("spectrum", o, fc), 1]
        hy += [2, ("conv", o, 0), ("conv", o, 1), 2]
    hy += [("hyout", 0), ("hyout", 1), 2]
    plan += spread(gates[2], hy)
    plan += parts(gates[3])
    out = [parts([("out", c)]) for c in range(C)]
    plan += [("moda", 0), ("moda", 1)] + [("merged", c) for c in range(C)] + [("modrow", 0), ("modrow", 1)]
    for c in range(C):
        plan += out[c]
        plan += {0: [("modcol", 0), ("modcol", 1)], 1: [("moda", 2), ("modrow", 2)], 2: [("modcol", 2)],
                 3: [("moda", 3), ("modrow", 3)], 4: [("modcol", 3)]}.get(c, [])
        if c:
            plan.append(("xsquare", c - 1))
    return plan


def build(nc, w_main, w_fused, consts, vecs, lam, x_in, rope, bias, logdecay, kctx, vctx, mlp_w, mlp_w3, zt, dft,
          y_out, nk, nv):
    ctx = ExitStack()
    with ctx:
        def sb(name, shape, dt=F32):
            return ctx.enter_context(nc.sbuf_tensor(name, shape, dt))

        def sem(name):
            return ctx.enter_context(nc.semaphore(name))

        x = sb("x", [P, C, T])
        h_hi, h_lo = sb("h_hi", [P, C, T], F32R), sb("h_lo", [P, C, T], F32R)
        raw = sb("raw", [P, RING, 1280])
        hi, lo = sb("hi", [P, RING, 1280], F32R), sb("lo", [P, RING, 1280], F32R)
        kk = sb("kk", [P, K_COLS])
        vv = sb("vv", [P, V_COLS])
        mod = sb("mod", [P, N_MOD * C, 2])
        coef = sb("coef", [P, 3, C, 2])
        modb = sb("modb", [P, 2, C, 2])
        c_act = sb("c_act", [P, C, 2])
        c_parts = sb("c_parts", [P, C, 4], F32R)
        kt = sb("kt", [P, 5, 512])
        q_swa = sb("q_swa", [P, 2, T])
        vt = sb("vt", [P, 4, 640])
        areaM, areaE, areaF = sb("areaM", [P, 3072]), sb("areaE", [P, 3072]), sb("areaF", [P, 3072])
        pr = sb("pr", [P, 2, T])
        prT = sb("prT", [P, T])
        rstd = prT
        o_hi, o_lo = sb("o_hi", [P, 2, 2, T], F32R), sb("o_lo", [P, 2, 2, T], F32R)
        tiny = sb("tiny", [P, 32])
        with nc.sbuf_tensor("g_hi", [P, C, T], F32R) as g_hi, nc.sbuf_tensor("g_lo", [P, C, T], F32R) as g_lo:
            pass
        areaG = sb("areaG", [P, 2 * C * T])
        hy = areaG[:, 0:7 * T].rearrange("p (j t) -> p j t", t=T)
        q_na = areaG[:, 7 * T:9 * T].rearrange("p (j t) -> p j t", t=T)
        q_df = areaG[:, 9 * T:11 * T].rearrange("p (j t) -> p j t", t=T)
        v_all = areaG[:, 11 * T:16 * T].rearrange("p (j t) -> p j t", t=T)
        k_tok = areaG[:, 11 * T:11 * T + 640].rearrange("p (j t) -> p j t", t=P)
        th = q_na
        mod_row = pr[0:4, :, 0:P]
        gated = v_all[:, 2:4, :]
        h_f = areaM[:, :].rearrange("p (c t) -> p c t", t=T)
        merged = h_f
        taps = areaM[:, 0:1536].rearrange("p (k s c) -> p k s c", k=TB, s=2)
        dft_t = areaM[:, 1536:1536 + 1280]
        na_bias = areaE[:, 0:2048].rearrange("p (b h k) -> p b h k", b=2, h=4)
        rope_t = areaE[:, 2048:3072].rearrange("p (j t) -> p j t", t=T_DEN)
        y_tok = areaE[:, 0:768].rearrange("p (k c) -> p k c", k=TB)
        spec = areaE[:, 768:2304].rearrange("p (f s c) -> p f s c", f=TB, s=2)
        spec_t = areaE[:, 2304:2816].rearrange("p (s c) -> p s c", s=2)
        sq = areaF[:, :].rearrange("p (c t) -> p c t", t=T)
        sil = areaF[:, 0:2 * T].rearrange("p (s t) -> p s t", t=T)
        gf = areaF[:, 2 * T:4 * T].rearrange("p (s t) -> p s t", t=T)
        filt = areaF[:, :].rearrange("p (o f s c) -> p o f s c", o=2, f=TB, s=2)
        fw3 = areaF[0:HY_HID, 1536:2560]
        fg = areaF[0:HY_HID, 2560:2560 + T]
        fw1 = areaF[0:HY_EMB, 2944:3008]
        fw2 = areaF[0:HY_HID, 3008:3072]
        rate = areaG[:, 0:1024]
        win = areaG[:, 1024:1536]
        hab = areaG[:, 1536:2048]
        z_t = areaG[0:HY_EMB, 2048:2048 + T]
        f_arg, f_turn = q_df[0:HY_HID, 0, :], q_df[0:HY_HID, 1, :]
        f_inv = pr[:, :, :].rearrange("p a t -> p (a t)")[:, 0:512].rearrange("p (g c) -> p g c", g=2)

        lam_vecs = areaM[:, 0:DEPTH * 128]
        ident = kk[:, K_ID:K_ID + P]
        ones = kk[:, K_ONES:K_ONES + P]
        bones = kk[:, K_BONES:K_BONES + P]
        eps = kk[:, K_EPS:K_EPS + 1]

        bank = [ctx.enter_context(nc.psum_tensor(f"bank{i}", [P, 512], F32)) for i in range(RING)]
        ps_br, ps_s, ps_t, ps_o = (ctx.enter_context(nc.psum_tensor(n, [P, 512], F32)) for n in ("ps_br", "ps_s", "ps_t", "ps_o"))

        vecs_in, lo_pool, xn_ready = sem("vecs_in"), sem("lo_pool"), sem("xn_ready")
        taps_h, spec_prod = sem("taps_h"), sem("spec_prod")
        consts_in, raw_in = sem("consts_in"), [sem(f"raw_in{i}") for i in range(RING)]
        hi_ready, lo_ready, tile_done, drained = sem("hi_ready"), sem("lo_ready"), sem("tile_done"), sem("drained")
        cond_act, cond_hi, cond_lo = sem("cond_act"), sem("cond_hi"), sem("cond_lo")
        mod_turned, mod_done = sem("mod_turned"), sem("mod_done")
        silu_done, gf_ready, g_lo_ready = sem("silu_done"), sem("gf_ready"), sem("g_lo_ready")
        sq_ready, ss_ready, rms_ready = sem("sq_ready"), sem("ss_ready"), sem("rms_ready")
        h_ready, h_hi_ready, h_lo_ready = sem("h_ready"), sem("h_hi_ready"), sem("h_lo_ready")
        dve_order, act_order, pool_order = sem("dve_order"), sem("act_order"), sem("pool_order")
        small_in, lam_exp, lam_dot = sem("small_in"), sem("lam_exp"), sem("lam_dot")
        filt_in, ctx_in, bias_ready = sem("filt_in"), sem("ctx_in"), sem("bias_ready")
        mlp_mm, mlp_arg, mlp_sin = sem("mlp_mm"), sem("mlp_arg"), sem("mlp_sin")
        taps_mm, win_ready, taps_ready, abs_ready, sum_mm = (sem("taps_mm"), sem("win_ready"), sem("taps_ready"),
                                                             sem("abs_ready"), sem("sum_mm"))
        scale_ready, filt_mm, filt_ready = sem("scale_ready"), sem("filt_mm"), sem("filt_ready")
        t_ready, t_free = sem("t_ready"), sem("t_free")
        rot_ready, rope_done = sem("rot_ready"), sem("rope_done")
        scores_ready, max_ready, exp_done, probs_ready, probs0_used = (
            sem("scores_ready"), sem("max_ready"), sem("exp_done"), sem("probs_ready"), sem("probs0_used"))
        values_done, o_hi_ready, o_lo_ready = sem("values_done"), sem("o_hi_ready"), sem("o_lo_ready")
        osq_ready, orms_ready, onorm_ready = sem("osq_ready"), sem("orms_ready"), sem("onorm_ready")
        merged_done, th_ready = sem("merged_done"), sem("th_ready")
        y_ready, spec_mm, spec_ready, conv_mm = sem("y_ready"), sem("spec_mm"), sem("spec_ready"), sem("conv_mm")
        out_done, kv_out, y_fin = sem("out_done"), sem("kv_out"), sem("y_fin")

        plan = mix_plan()
        t_index = {s: i for i, s in enumerate([s for s in plan if s[0] in ("vk", "turn", "subnorm", "ytok")])}
        T_PER = len(t_index)
        rounds = [s for s in plan if s[0] == "scores"]
        r_index = {s: i for i, s in enumerate(rounds)}
        R_PER = len(rounds)
        U_PER = 36
        FUSED0 = N_PROJ
        TYPE_T0 = {}

        def out_pair(branch, blk):
            return 2 * BRANCH_ORDER.index(branch) + blk

        def buf(branch):
            return BRANCH_ORDER.index(branch) % 2

        BR_OF = {NA: 0, SWA: 1, DF: 3}

        tiles = {}
        for step in plan:
            if step[0] in ("proj", "fused", "out"):
                tiles.setdefault(step[:-1], len(tiles))
            elif step[0] == "moda":
                tiles.setdefault(step, len(tiles))

        def tile_of(step):
            return tiles[step if step[0] == "moda" else step[:-1]]

        def unit(u):
            return u // 6, (u // 3) % 2, u % 3

        def keys(b):
            return (0, 128) if b == 0 else (128, 512)

        F0 = {}

        def fcount(p):
            return FB * p.q + sum(THIRDS[:p.third]) + (p.f0 if p.kind == "up" else 0)

        def vcol(i):
            return vv[:, i:i + 1]

        block = ctx.enter_context(nc.Block())

        @block.sync
        def _(sp):
            sp.dma_start(vv[:], vecs).then_inc(vecs_in, 16)
            sp.dma_start(lam_vecs, lam).then_inc(vecs_in, 16)

            def load(base, rep, src, pool=None):
                slot = base % RING
                if base >= RING:
                    sp.wait_ge(lo_ready, base - RING + 1 + 4 * rep)
                if pool is not None:
                    sp.wait_ge(lo_pool, pool)
                sp.dma_start(raw[:, slot, 0:width(base)], src).then_inc(raw_in[slot], 16)

            def main(j, i=0):
                return w_main[bass.ds(j + 4 * i, 1)].rearrange("a p n -> p (a n)")

            at, n = 0, 0
            for l, mix0 in enumerate(MIX_N0 + [None]):
                stop = N_TILES if mix0 is None else mix0 + N_PROJ
                for j in range(RING):
                    load(n, 0, w_main[at], 4 * C * l - 3 + j if l else None)
                    n, at = n + 1, at + 1
                if l == 0:
                    sp.dma_start(kk[:], consts).then_inc(consts_in, 16)
                    sp.dma_start(x[:, :, :].rearrange("p c t -> p (c t)"), x_in).then_inc(consts_in, 16)
                groups = (stop - n) // RING
                with sp.Fori(0, groups) as i:
                    for j in range(RING):
                        load(n + j, i, main(at + j, i))
                n, at = n + RING * groups, at + RING * groups
                while n < stop:
                    load(n, 0, w_main[at])
                    n, at = n + 1, at + 1
                if mix0 is not None:
                    for j in range(4 * C):
                        load(n, 0, w_fused[4 * C * l + j], 4 * C * l + j - 3 if j >= RING else None)
                        n += 1
            for c in range(C):
                sp.wait_ge(y_fin, c + 1)
                sp.dma_start(y_out[:, T * c:T * (c + 1)], h_f[:, c, :]).then_inc(out_done, 16)
            sp.wait_ge(out_done, 16 * C)

        @block.scalar
        def _(act):
            order = [0]

            def link(ins):
                order[0] += 1
                ins.then_inc(act_order, 1)
                act.wait_ge(act_order, order[0])

            def split(base, rep=0):
                if base >= N_TILES:
                    return
                slot = base % RING
                act.wait_ge(raw_in[slot], 16 * (base // RING + 1 + rep))
                if base >= RING:
                    act.wait_ge(tile_done, base - RING + 1 + 4 * rep)
                act.activation(hi[:, slot, 0:width(base)], raw[:, slot, 0:width(base)], ACT.Copy).then_inc(hi_ready, 1)

            act.wait_ge(vecs_in, 32)
            act.activation(c_act[:, :, :].rearrange("p c g -> p (c g)"), vv[:, V_COND:V_COND + 2 * C], ACT.Silu).then_inc(cond_act, 1)
            act.wait_ge(cond_act, 1)
            act.activation(c_parts[:, :, 0:2], c_act[:], ACT.Copy).then_inc(cond_hi, 1)
            act.wait_ge(lam_dot, 1)
            act.activation(tiny[:, 4:8], tiny[:, 0:4], ACT.Exp).then_inc(lam_exp, 1)
            for n in range(AHEAD):
                split(n)

            def x_square(c, drained_at):
                if drained_at is None:
                    act.wait_ge(consts_in, 32)
                else:
                    act.wait_ge(drained, drained_at)
                act.activation(sq[:, c, :], x[:, c, :], ACT.Square).then_inc(sq_ready, 1)

            def norm(p):
                if p.l + p.which == 0:
                    for c in range(C):
                        x_square(c, None)
                else:
                    act.preload_act_table(ACT.Sqrt)
                    x_square(C - 1, p.n0)
                act.wait_ge(ss_ready, nidx(p) + 1)
                act.activation(rstd[:], ps_o[:, 0:T], ACT.Sqrt, bias=eps, scale=1.0 / D).then_inc(rms_ready, 1)
                if p.which != 3:
                    act.preload_act_table(ACT.Sin if p.which == 1 else ACT.Silu)
                if p.which == 3:
                    return
                for c in range(C):
                    act.wait_ge(h_ready, C * nidx(p) + c + 1)
                    act.activation(h_hi[:, c, :], h_f[:, c, :], ACT.Copy).then_inc(h_hi_ready, 1)

            def up(p):
                per = 8 if p.ada else 4
                with act.Fori(0, p.iters) as i:
                    for j in range(per):
                        split(p.n0 + j + AHEAD, per // 4 * i)
                        if j in ((1, 5) if p.ada else (0, 2)):
                            s = 2 * j // per
                            f = fcount(p) + s
                            act.wait_ge(tile_done, p.n0 + j + 1 + per * i)
                            if f >= 2:
                                act.wait_ge(gf_ready, f - 1 + 2 * i)
                                act.wait_ge(drained, p.n0 + j - (5 if p.ada else 2) + per * i)
                            act.activation(sil[:, s, :], bank[(p.n0 + j) % RING][:, 0:T], ACT.Silu).then_inc(silu_done, 1)

            def down(p):
                if p.third == 2:
                    for j in range(C):
                        split(p.n0 + j + AHEAD)
                        if j:
                            x_square(j - 1, p.n0 + j)
                    return
                with act.Fori(0, 2) as i:
                    for j in range(4):
                        split(p.n0 + j + AHEAD, i)

            def mix(p):
                l = p.l
                for step in plan:
                    kind = step[0]
                    if kind == "moda" or kind in ("proj", "out", "fused") and step[-1] == 0:
                        split(p.n0 + tile_of(step) + AHEAD)
                    elif kind == "xsquare":
                        x_square(step[1], p.n0 + tile_of(("out", step[1], 0)) + 1)
                    elif kind == "fused" and step[-1] == PARTS - 1:
                        at, n = p.n0 + tile_of(step), step[2]
                        act.wait_ge(tile_done, at + 1)
                        act.wait_ge(drained, at - 1)
                        act.activation(th[:, n % 2, :], bank[at % RING][:, 0:T], ACT.Tanh, scale=0.5).then_inc(th_ready, 1)
                    elif kind == "merged":
                        c = step[1]
                        act.wait_ge(merged_done, 3 * C * l + 2 * C + c + 1)
                        act.wait_ge(tile_done, p.n0 + N_PROJ + 4 * C)
                        act.activation(h_hi[:, c, :], merged[:, c, :], ACT.Copy).then_inc(h_hi_ready, 1)
                    elif kind == "sinmlp":
                        act.wait_ge(mlp_arg, 2 * l + step[1] + 1)
                        act.activation(fg, f_arg, ACT.Sin).then_inc(mlp_sin, 1)
                    elif kind == "taps":
                        _, o, tk = step
                        q = 6 * l + 3 * o + tk
                        if o == 0 and tk == 0:
                            act.wait_ge(filt_in, 16 * 6 * (l + 1))
                            link(act.activation(rate, rate, ACT.Exp))
                        if q:
                            act.wait_ge(abs_ready, q)
                            act.wait_ge(taps_ready, q)
                        act.activation(win, rate[:, 512 * o:512 * (o + 1)], ACT.Exp, scale=kk[:, K_NTN + tk:K_NTN + tk + 1]).then_inc(win_ready, 1)
                    elif kind == "tapsum":
                        _, o, tk = step
                        q = 6 * l + 3 * o + tk
                        act.wait_ge(taps_h, q + 1)
                        if q:
                            act.wait_ge(sum_mm, q)
                        act.activation(hab, win, ACT.Abs).then_inc(abs_ready, 1)
                    elif kind == "vk":
                        j, t = step[1], T_PER * l + t_index[step]
                        act.wait_ge(t_ready, t + 1)
                        ps3 = ps_t[:, :].rearrange("p (k c) -> p k c", k=4)
                        act.activation(vt[:, 0:3, P * j:P * (j + 1)], ps3[:, 0:3, :], ACT.Copy).then_inc(act_order, 1)
                        order[0] += 1
                        act.activation(k_tok[:, j, :], ps3[:, 3, :], ACT.Copy).then_inc(t_free, 1)
                    elif kind == "scores":
                        _, ty, u, m = step
                        r = R_PER * l + r_index[step]
                        act.wait_ge(max_ready, r + 1)
                        b = unit(u)[2]
                        nk_ = keys(b)[1] - keys(b)[0]
                        nm = tiny[:, 8 + r % 4:9 + r % 4]
                        if ty == SWA:
                            head = unit(u)[0] + 2 * unit(u)[1]
                            order[0] += 1
                            act.activation(tiny[:, 20 + r % 4:21 + r % 4], vcol(V_SINK + 4 * l + head), ACT.Exp, bias=nm).then_inc(act_order, 1)
                        g = U_PER * l + 12 * ty + u
                        if ty == DF and m == 0:
                            act.wait_ge(probs_ready, g)
                        elif ty == DF:
                            act.wait_ge(t_ready, T_PER * l + turn_t(ty, u))
                        elif g > 1:
                            act.wait_ge(t_ready, T_PER * l + turn_t(ty, u - 1) if u else T_PER * l + turn_t(ty, 0))
                        dst = pr[:, m if ty == DF else u % 2, 0:nk_]
                        act.activation(dst, ps_s[:, 0:nk_], ACT.Exp, bias=nm, accum_out=tiny[:, 12 + r % 4:13 + r % 4]).then_inc(exp_done, 1)
                    elif kind == "turn":
                        _, ty, u = step
                        t, g = T_PER * l + t_index[step], U_PER * l + 12 * ty + u
                        act.wait_ge(t_ready, t + 1)
                        if g:
                            act.wait_ge(values_done, g)
                        nk_ = keys(unit(u)[2])[1] - keys(unit(u)[2])[0]
                        act.activation(prT[:, 0:nk_], ps_t[:, 0:nk_], ACT.Copy).then_inc(t_free, 1)
                    elif kind == "outs":
                        _, ty, blk = step
                        act.wait_ge(values_done, U_PER * l + 12 * ty + 6 * (blk + 1))
                        act.activation(o_hi[:, buf(BR_OF[ty]), blk, :], ps_o[:, 0:T], ACT.Copy).then_inc(o_hi_ready, 1)
                    elif kind == "square":
                        act.wait_ge(values_done, U_PER * l + 12 * DF + 6 * (step[1] + 1))
                        act.activation(prT[:], ps_o[:, 0:T], ACT.Square).then_inc(osq_ready, 1)
                    elif kind == "subnorm":
                        blk = step[1]
                        act.wait_ge(t_ready, T_PER * l + t_index[step] + 1)
                        act.activation(prT[:], ps_t[:, 0:T], ACT.Sqrt, bias=eps, scale=1.0 / 64).then_inc(t_free, 1)
                        act.wait_ge(onorm_ready, 2 * l + blk + 1)
                        act.wait_ge(tile_done, p.n0 + FUSED0 + C)
                        act.activation(o_hi[:, buf(3), blk, :], prT[:], ACT.Copy).then_inc(o_hi_ready, 1)
                    elif kind == "ytok":
                        _, o, blk = step
                        act.wait_ge(t_ready, T_PER * l + t_index[step] + 1)
                        ps3 = ps_t[:, 0:T].rearrange("p (k c) -> p k c", k=3)
                        act.activation(y_tok[:, :, P * blk:P * (blk + 1)], ps3, ACT.Copy).then_inc(t_free, 1)
                    elif kind == "hyout":
                        blk = step[1]
                        act.wait_ge(y_ready, 6 * l + 4 + blk + 1)
                        act.wait_ge(tile_done, p.n0 + FUSED0 + 2 * C)
                        act.activation(o_hi[:, buf(2), blk, :], hy[:, blk, :], ACT.Copy).then_inc(o_hi_ready, 1)

            def turn_t(ty, u):
                return t_index[("turn", ty, u)] if u == 0 else t_index[("turn", ty, u - 1)] + 1

            for p in PHASES:
                if p.kind == "ada":
                    for j in range(p.tiles):
                        split(p.n0 + j + AHEAD)
                elif p.kind == "norm":
                    norm(p)
                elif p.kind == "up":
                    up(p)
                elif p.kind == "down":
                    down(p)
                else:
                    mix(p)

        @block.vector
        def _(dve):
            order = [0]

            def link(ins):
                order[0] += 1
                ins.then_inc(dve_order, 1)
                dve.wait_ge(dve_order, order[0])

            def split(base, rep=0):
                if base >= N_TILES:
                    return
                slot = base % RING
                dve.wait_ge(hi_ready, base + 1 + 4 * rep)
                w = POOL_FROM if base in WIDE else width(base)
                dve.tensor_tensor(lo[:, slot, 0:w], raw[:, slot, 0:w], hi[:, slot, 0:w].bitcast(F32), ALU.subtract).then_inc(lo_ready, 1)

            dve.wait_ge(vecs_in, 32)
            for l in range(DEPTH):
                for i in range(2):
                    a = 128 * l + 64 * i
                    link(dve.tensor_tensor(prT[:, 0:32], lam_vecs[:, a:a + 32], lam_vecs[:, a + 32:a + 64], ALU.mult))
                    link(dve.tensor_reduce(tiny[:, 2 * l + i:2 * l + i + 1], prT[:, 0:32], AX_X, ALU.add))
            dve.memset(tiny[:, 28:29], 0.0).then_inc(lam_dot, 1)
            dve.wait_ge(cond_hi, 1)
            dve.tensor_tensor(c_parts[:, :, 2:4], c_act[:], c_parts[:, :, 0:2].bitcast(F32), ALU.subtract).then_inc(cond_lo, 1)
            dve.wait_ge(lam_exp, 1)
            for l in range(DEPTH):
                nl = tiny[:, 24 + l:25 + l]
                link(dve.tensor_tensor(nl, tiny[:, 5 + 2 * l:6 + 2 * l], tiny[:, 4 + 2 * l:5 + 2 * l], ALU.subtract))
                link(dve.tensor_scalar(nl, nl, LAM_INIT[l], None, ALU.subtract))
                link(dve.tensor_scalar(tiny[:, 26 + l:27 + l], vcol(V_SUBLN + l), 1.0 - LAM_INIT[l], None, ALU.mult))
            for n in range(AHEAD):
                split(n)

            def modulation(l, v, slot):
                dve.wait_ge(mod_done, N_MOD * C * l + C * (v + 1))
                b = vv[:, V_BADA + N_MOD * C * l + C * v:V_BADA + N_MOD * C * l + C * (v + 1)].unsqueeze(2).broadcast_to([P, C, 2])
                link(dve.tensor_tensor(modb[:, slot], mod[:, C * v:C * (v + 1), :], b, ALU.add))

            def residual_gate(l, v):
                modulation(l, v, 0)
                link(dve.tensor_scalar(coef[:, 2], modb[:, 0], 0.5, None, ALU.mult))

            def norm(p):
                k = nidx(p)
                if p.which < 3:
                    modulation(p.l, (SC1, SC2, SC3)[p.which], 0)
                    a = V_NORM + 3 * C * p.l + C * p.which
                    w = vv[:, a:a + C].unsqueeze(2).broadcast_to([P, C, 2])
                    link(dve.scalar_tensor_tensor(coef[:, 0], modb[:, 0], 1.0, w, ALU.add, ALU.mult))
                    modulation(p.l, (SH1, SH2, SH3)[p.which], 1)
                dve.wait_ge(rms_ready, k + 1)
                link(dve.reciprocal(rstd[:], rstd[:]))

                def scaled(c):
                    dve.tensor_tensor(sq[:, c, :], x[:, c, :], rstd[:], ALU.mult).then_inc(xn_ready, 1)

                scaled(0)
                for c in range(C):
                    if c + 1 < C:
                        scaled(c + 1)
                    dve.wait_ge(xn_ready, C * k + c + 1)
                    if p.which == 3:
                        dve.tensor_scalar(h_f[:, c, :], sq[:, c, :], vcol(V_FIN + c), None, ALU.mult).then_inc(y_fin, 1)
                        continue
                    for g, (t0, t1) in enumerate(GROUPS):
                        last = dve.tensor_scalar(h_f[:, c, t0:t1], sq[:, c, t0:t1], coef[:, 0, c, g:g + 1], modb[:, 1, c, g:g + 1],
                                                 ALU.mult, ALU.add)
                    last.then_inc(h_ready, 1)

            def h_low(count, src, c):
                dve.wait_ge(h_hi_ready, count + 1)
                dve.tensor_tensor(h_lo[:, c, :], src, h_hi[:, c, :].bitcast(F32), ALU.subtract).then_inc(h_lo_ready, 1)

            def up(p):
                if p.first and p.ffn == 1:
                    dve.wait_ge(kv_out, 16 * 6 * (p.l + 1))
                per = 8 if p.ada else 4
                with dve.Fori(0, p.iters) as i:
                    for j in range(per):
                        n = p.n0 + j
                        split(n + AHEAD, per // 4 * i)
                        if j in ((3, 7) if p.ada else (1, 3)):
                            s = 2 * j // per
                            f = fcount(p) + s
                            b = bank[n % RING][:, 0:T]
                            dve.wait_ge(silu_done, f + 1 + 2 * i)
                            dve.wait_ge(tile_done, n + 1 + per * i)
                            if f >= 2:
                                dve.wait_ge(g_lo_ready, f - 1 + 2 * i)
                            dve.tensor_tensor(gf[:, s, :], sil[:, s, :], b, ALU.mult).then_inc(gf_ready, 1)
                            dst = g_hi[:, bass.ds(p.f0 + s + 2 * i, 1), :].rearrange("p a t -> p (a t)")
                            dve.tensor_tensor(dst, sil[:, s, :], b, ALU.mult).then_inc(drained, 2)
                        if p.ada and j % 2 == 0:
                            modulation_row(n, p.m + j // 2, per // 4 * i)
                        elif p.ada:
                            modulation_column(p.m + j // 2, 4 * i)

            def modulation_row(n, a, rep=0):
                dve.wait_ge(tile_done, n + 1 + 4 * rep)
                dve.tensor_copy(mod_row[:, a % 2, :], bank[n % RING][0:4, 0:P]).then_inc(drained, 1)

            def modulation_column(a, more=0):
                dve.wait_ge(mod_turned, a + 1 + more)
                dst = mod[:, bass.ds(a % (N_MOD * C) + more, 1), :].rearrange("p a g -> p (a g)")
                dve.tensor_copy(dst, ps_t[:, 0:2]).then_inc(mod_done, 1)

            def add_to_x(n, c, rep=0, dyn=None):
                dve.wait_ge(tile_done, n + 1 + 4 * rep)
                for g, (t0, t1) in enumerate(GROUPS):
                    if dyn is None:
                        xs, gate = x[:, c, t0:t1], coef[:, 2, c, g:g + 1]
                    else:
                        xs = x[:, bass.ds(c + 4 * dyn, 1), t0:t1].rearrange("p a t -> p (a t)")
                        gate = coef[:, 2, bass.ds(c + 4 * dyn, 1), g:g + 1].rearrange("p a g -> p (a g)")
                    last = dve.scalar_tensor_tensor(xs, bank[n % RING][:, t0:t1], gate, xs, ALU.mult, ALU.add)
                last.then_inc(drained, 1)

            def down(p):
                if p.third == 0:
                    residual_gate(p.l, (G1, G3)[p.ffn])
                if p.third == 2:
                    for j in range(C):
                        split(p.n0 + j + AHEAD)
                        add_to_x(p.n0 + j, j)
                    return
                with dve.Fori(0, 2) as i:
                    for j in range(4):
                        split(p.n0 + j + AHEAD, i)
                        add_to_x(p.n0 + j, j, i, i)

            def proj_place(k):
                if k < 2:
                    return q_na[:, k, :], 0.125
                if k < 4:
                    return kt[:, k - 2, 0:T], 1.0
                if k < 6:
                    return v_all[:, k - 4, :], 1.0
                if k < 8:
                    return q_swa[:, k - 6, :], 0.125
                if k == 8:
                    return kt[:, 2, 0:T], 1.0
                if k == 9:
                    return v_all[:, 2, :], 1.0
                if k < 12:
                    return q_df[:, k - 10, :], 32 ** -0.5
                if k < 14:
                    return kt[:, k - 9, 0:T], 1.0
                if k < 16:
                    return v_all[:, k - 11, :], 1.0
                return hy[:, k - 15, :], 1.0

            def mix(p):
                l = p.l
                for step in plan:
                    kind = step[0]
                    if kind == "moda" or kind in ("proj", "out", "fused") and step[-1] == 0:
                        split(p.n0 + tile_of(step) + AHEAD)
                        if kind == "out" and step[1] == 0:
                            residual_gate(l, G2)
                    elif kind in ("proj", "out", "fused") and step[-1] < PARTS - 1:
                        pass
                    elif kind == "modrow":
                        modulation_row(p.n0 + tile_of(("moda", step[1])), p.m + step[1])
                    elif kind == "modcol":
                        modulation_column(p.m + step[1])
                    elif kind == "proj":
                        k = step[1]
                        if k == 10:
                            dve.wait_ge(mlp_sin, 2 * (l + 1))
                        dve.wait_ge(tile_done, p.n0 + k + 1)
                        dst, s = proj_place(k)
                        dve.tensor_scalar(dst, bank[(p.n0 + k) % RING][:, 0:T], s, None, ALU.mult).then_inc(drained, 1)
                    elif kind == "fused":
                        _, i, n, _ = step
                        at = p.n0 + FUSED0 + C * i + n
                        dve.wait_ge(th_ready, 4 * C * l + C * i + n + 1)
                        dve.wait_ge(tile_done, at + 1)
                        a = 3 * C * l + C * (i - 1) + n
                        if i == 0:
                            dst = merged[:, n, :]
                        else:
                            dst = gated[:, n % 2, :]
                            if n >= 2 or i > 1:
                                dve.wait_ge(merged_done, a - 1)
                        dve.scalar_tensor_tensor(dst, th[:, n % 2, :], 1.0, ps_br[:, 0:T], ALU.add, ALU.mult).then_inc(drained, 1)
                    elif kind == "merged":
                        h_low(C * (4 * l + 2) + step[1], merged[:, step[1], :], step[1])
                    elif kind == "out":
                        c = step[1]
                        n = p.n0 + tile_of(step)
                        add_to_x(n, c)
                    elif kind == "sinmlp":
                        j = step[1]
                        dve.wait_ge(mlp_mm, 2 * l + j + 1)
                        if l + j:
                            dve.wait_ge(mlp_sin, 2 * l + j)
                        f, b = (vv[0:HY_HID, V_MLP + 3 * l + i:V_MLP + 3 * l + i + 1] for i in (0, 1 + j))
                        link(dve.tensor_scalar(f_arg, ps_s[0:HY_HID, 0:T], b, f, ALU.add, ALU.mult))
                        link(dve.tensor_scalar(f_turn, f_arg, 1.0 / (2 * math.pi), ROUND, ALU.mult, ALU.add))
                        link(dve.tensor_scalar(f_turn, f_turn, ROUND, None, ALU.subtract))
                        for part in (TWO_PI_A, TWO_PI_B, TWO_PI_C):
                            link(dve.scalar_tensor_tensor(f_arg, f_turn, -part, f_arg, ALU.mult, ALU.add))
                        dve.tensor_scalar(f_arg, f_arg, PI_DOWN, -PI_DOWN, ALU.min, ALU.max).then_inc(mlp_arg, 1)
                    elif kind == "taps":
                        _, o, tk = step
                        q = 6 * l + 3 * o + tk
                        dve.wait_ge(win_ready, q + 1)
                        dve.wait_ge(taps_mm, q + 1)
                        ins = dve.tensor_tensor(win, (ps_s, ps_br)[q % 2][:, :], win, ALU.mult)
                        if tk < 2:
                            link(ins)
                            ins = dve.tensor_scalar(win[:, 256:512], win[:, 256:512], kk[:, K_TM + tk:K_TM + tk + 1], None, ALU.mult)
                        ins.then_inc(taps_h, 1)
                    elif kind == "scale":
                        o = step[1]
                        dve.wait_ge(sum_mm, 6 * l + 3 * (o + 1))
                        for g, L in enumerate((T_CTX, T_DEN)):
                            order[0] += 1
                            dve.tensor_scalar(f_inv[:, g, :], ps_t[:, 256 * g:256 * (g + 1)], EPS, float(L), ALU.add, ALU.mult).then_inc(dve_order, 1)
                        dve.wait_ge(dve_order, order[0])
                        dve.reciprocal(f_inv, f_inv).then_inc(scale_ready, 1)
                    elif kind == "filter":
                        _, o, fc = step
                        q = 6 * l + 3 * o + fc
                        dve.wait_ge(filt_mm, q + 1)
                        dve.wait_ge(scale_ready, 2 * l + o + 1)
                        g = 0 if fc == 0 else 1
                        psx = (ps_o, ps_s)[q % 2][:, :].rearrange("p (s c) -> p s c", s=2)
                        inv = f_inv[:, g:g + 1, :].broadcast_to([P, 2, 256])
                        dve.tensor_tensor(filt[:, o, fc], psx, inv, ALU.mult).then_inc(filt_ready, 1)
                    elif kind == "rope":
                        j = step[1]
                        swa = j < 3
                        tgt = (q_swa[:, 0], q_swa[:, 1], kt[:, 2], q_df[:, 0], q_df[:, 1], kt[:, 3], kt[:, 4])[j][:, T_CTX:T]
                        cos, sin = (rope_t[:, 0], rope_t[:, 1]) if swa else (rope_t[:, 2], rope_t[:, 3])
                        dve.wait_ge(rot_ready, 7 * l + j + 1)
                        order[0] += 1
                        dve.tensor_tensor(spare, ps_br[:, 0:T_DEN], sin, ALU.mult).then_inc(dve_order, 1)
                        link(dve.tensor_tensor(tgt, tgt, cos, ALU.mult))
                        dve.tensor_tensor(tgt, tgt, spare, ALU.add).then_inc(rope_done, 1)
                        dve.wait_ge(rope_done, 7 * l + j + 1)
                    elif kind == "scores":
                        _, ty, u, m = step
                        blk, hh, b = unit(u)
                        r = R_PER * l + r_index[step]
                        k0, k1 = keys(b)
                        nm = tiny[:, 8 + r % 4:9 + r % 4]
                        dve.wait_ge(scores_ready, r + 1)
                        if ty == NA and b:
                            dve.wait_ge(bias_ready, l + 1)
                            link(dve.tensor_tensor(ps_s[:, 0:256], ps_s[:, 0:256], na_bias[:, b - 1, 2 * blk + hh, :], ALU.add))
                        if ty == SWA and b:
                            c0 = 128 if b == 1 else 0
                            msk = kk[:, K_SWM + P * (b - 1):K_SWM + P * b]
                            link(dve.tensor_tensor(ps_s[:, c0:c0 + P], ps_s[:, c0:c0 + P], msk, ALU.add))
                        red = dve.tensor_reduce(nm, ps_s[:, 0:k1 - k0], AX_X, ALU.max, negate=True)
                        if ty == SWA:
                            link(red)
                            head = blk + 2 * hh
                            red = dve.scalar_tensor_tensor(nm, vcol(V_SINK + 4 * l + head), -1.0, nm, ALU.mult, ALU.min)
                        red.then_inc(max_ready, 1)
                    elif kind == "probs":
                        _, ty, u = step
                        nk_ = keys(unit(u)[2])[1] - keys(unit(u)[2])[0]
                        r = R_PER * l + r_index[("scores", ty, u, 1 if ty == DF else 0)]
                        dve.wait_ge(exp_done, r + 1)
                        rs = tiny[:, 12 + r % 4:13 + r % 4]
                        rr = tiny[:, 16 + r % 4:17 + r % 4]
                        if ty == SWA:
                            link(dve.tensor_tensor(rs, rs, tiny[:, 20 + r % 4:21 + r % 4], ALU.add))
                        link(dve.reciprocal(rr, rs))
                        if ty == DF:
                            r0 = R_PER * l + r_index[("scores", ty, u, 0)]
                            rs0, rr0 = tiny[:, 12 + r0 % 4:13 + r0 % 4], tiny[:, 16 + r0 % 4:17 + r0 % 4]
                            link(dve.reciprocal(rr0, rs0))
                            link(dve.tensor_tensor(rr, rr, tiny[:, 24 + l:25 + l], ALU.mult))
                            link(dve.tensor_scalar(pr[:, 0, 0:nk_], pr[:, 0, 0:nk_], rr0, None, ALU.mult))
                            dve.scalar_tensor_tensor(pr[:, 1, 0:nk_], pr[:, 1, 0:nk_], rr, pr[:, 0, 0:nk_], ALU.mult, ALU.add).then_inc(probs_ready, 1)
                        else:
                            dst = pr[:, u % 2, 0:nk_]
                            dve.tensor_scalar(dst, dst, rr, None, ALU.mult).then_inc(probs_ready, 1)
                    elif kind == "outs":
                        _, ty, blk = step
                        br = BR_OF[ty]
                        dve.wait_ge(o_hi_ready, 8 * l + out_pair(br, blk) + 1)
                        dve.tensor_tensor(o_lo[:, buf(br), blk, :], ps_o[:, 0:T], o_hi[:, buf(br), blk, :].bitcast(F32), ALU.subtract).then_inc(o_lo_ready, 1)
                    elif kind == "subnorm":
                        blk = step[1]
                        dve.wait_ge(t_free, T_PER * l + t_index[step] + 1)
                        link(dve.reciprocal(prT[:], prT[:]))
                        dve.scalar_tensor_tensor(prT[:], ps_o[:, 0:T], tiny[:, 26 + l:27 + l], prT[:], ALU.mult, ALU.mult).then_inc(onorm_ready, 1)
                        dve.wait_ge(o_hi_ready, 8 * l + out_pair(3, blk) + 1)
                        dve.tensor_tensor(o_lo[:, buf(3), blk, :], prT[:], o_hi[:, buf(3), blk, :].bitcast(F32), ALU.subtract).then_inc(o_lo_ready, 1)
                    elif kind == "short":
                        j = step[1]
                        z, u = hy[:, j, :], hy[:, j + 1, :]
                        w0, w1, w2, b = (vcol(V_SHORT + 24 * l + 4 * j + i) for i in range(4))
                        dve.wait_ge(drained, p.n0 + 16 + j + 1)
                        link(dve.tensor_scalar(z, u, w1, b, ALU.mult, ALU.add))
                        for w, shift in ((w0, -1), (w2, 1)):
                            for t0, t1 in GROUPS:
                                a0, a1 = (t0 + 1, t1) if shift < 0 else (t0, t1 - 1)
                                link(dve.scalar_tensor_tensor(z[:, a0:a1], u[:, a0 + shift:a1 + shift], w, z[:, a0:a1], ALU.mult, ALU.add))
                        if j in (0, 1):
                            dve.memset(tiny[:, 28:29], 0.0).then_inc(y_ready, 1)
                    elif kind == "spectrum":
                        _, o, fc = step
                        q = 6 * l + 3 * o + fc
                        Y = (ps_s, ps_o)[q % 2][:, :].rearrange("p (s c) -> p s c", s=2)
                        Fr, Fs = (filt[:, o, fc, s:s + 1, :].broadcast_to([P, 2, 256]) for s in range(2))
                        dve.wait_ge(spec_mm, q + 1)
                        if o:
                            dve.wait_ge(conv_mm, 4 * l + 2)
                        if q:
                            dve.wait_ge(spec_ready, q)
                        dve.tensor_tensor(spec[:, fc], Y, Fr, ALU.mult)
                        dve.tensor_tensor(spec_t, Y, Fs, ALU.mult).then_inc(spec_prod, 1)
                    elif kind == "conv":
                        _, o, blk = step
                        y, gate = hy[:, blk, :], hy[:, 2 + 2 * o + blk, :]
                        dve.wait_ge(conv_mm, 4 * l + 2 * o + blk + 1)
                        link(dve.scalar_tensor_tensor(y, y, vcol(V_SKIP + 4 * l + 2 * o + blk), (ps_s, ps_o)[blk][:, 0:T], ALU.mult, ALU.add))
                        dve.tensor_tensor(y, y, gate, ALU.mult).then_inc(y_ready, 1)
                        dve.wait_ge(y_ready, 6 * l + 2 + 2 * o + blk + 1)
                    elif kind == "hyout":
                        blk = step[1]
                        dve.wait_ge(o_hi_ready, 8 * l + out_pair(2, blk) + 1)
                        dve.tensor_tensor(o_lo[:, buf(2), blk, :], hy[:, blk, :], o_hi[:, buf(2), blk, :].bitcast(F32), ALU.subtract).then_inc(o_lo_ready, 1)

            spare = areaM[:, 2816:3072]
            for p in PHASES:
                if p.kind == "ada":
                    for j in range(p.tiles):
                        n = p.n0 + j
                        split(n + AHEAD)
                        modulation_row(n, p.m + j)
                        if j:
                            modulation_column(p.m + j - 1)
                    modulation_column(p.m + p.tiles - 1)
                elif p.kind == "norm":
                    norm(p)
                elif p.kind == "up":
                    up(p)
                elif p.kind == "down":
                    down(p)
                    dve.wait_ge(drained, p.n0 + p.tiles)
                else:
                    mix(p)
                    dve.wait_ge(drained, p.n0 + p.tiles)

        @block.gpsimd
        def _(pool):
            def up(p):
                with pool.Fori(0, p.iters) as i:
                    for s in range(2):
                        f = fcount(p) + s
                        per = 8 if p.ada else 4
                        n = p.n0 + (4 * s + 3 if p.ada else 2 * s + 1)
                        pool.wait_ge(gf_ready, f + 1 + 2 * i)
                        pool.wait_ge(drained, n + 1 + per * i)
                        at = bass.ds(p.f0 + s + 2 * i, 1)
                        pool.tensor_tensor(g_lo[:, at, :].rearrange("p a t -> p (a t)"), gf[:, s, :],
                                           g_hi[:, at, :].rearrange("p a t -> p (a t)").bitcast(F32), ALU.subtract).then_inc(g_lo_ready, 1)

            def norm(p):
                if p.which == 3:
                    return
                for c in range(C):
                    pool.wait_ge(h_hi_ready, hp8(p) + c + 1)
                    pool.tensor_tensor(h_lo[:, c, :], h_f[:, c, :], h_hi[:, c, :].bitcast(F32), ALU.subtract).then_inc(h_lo_ready, 1)

            def split(base):
                if base not in WIDE:
                    return
                pool.wait_ge(hi_ready, base + 1)
                slot = base % RING
                pool.tensor_tensor(lo[:, slot, POOL_FROM:1280], raw[:, slot, POOL_FROM:1280],
                                   hi[:, slot, POOL_FROM:1280].bitcast(F32), ALU.subtract).then_inc(lo_pool, 1)

            def layer_loads(l):
                if l:
                    pool.wait_ge(tile_done, MIX_N0[l - 1] + N_PROJ + 5 * C)
                pool.dma_start(areaE[:, 0:2048], bias[l]).then_inc(ctx_in, 16)
                pool.dma_start(areaE[:, 2048:3072], rope).then_inc(ctx_in, 16)
                pool.dma_start(kt[:, :, T:512], kctx[l]).then_inc(ctx_in, 16)
                pool.dma_start(vt[:, 3, :], vctx[l]).then_inc(ctx_in, 16)
                pool.wait_ge(ctx_in, 64 * (l + 1))
                m = kk[:, K_NAM:K_NAM + 256].unsqueeze(1).broadcast_to([P, 8, 256])
                b8 = areaE[:, 0:2048].rearrange("p (b k) -> p b k", b=8)
                if l == 0:
                    pool.wait_ge(consts_in, 32)
                pool.tensor_tensor(b8, b8, m, ALU.add).then_inc(bias_ready, 1)

            def mix(p):
                l = p.l
                pool.wait_ge(h_lo_ready, C * (4 * l + 1) + C)
                pool.dma_start(fw1, mlp_w[l, 0:HY_EMB, 0:64]).then_inc(filt_in, 16)
                pool.dma_start(z_t, zt).then_inc(filt_in, 16)
                pool.dma_start(fw2, mlp_w[l, 0:HY_HID, 64:128]).then_inc(filt_in, 16)
                pool.dma_start(rate, logdecay[l]).then_inc(filt_in, 16)
                pool.dma_start(fw3, mlp_w3[l]).then_inc(filt_in, 16)
                pool.dma_start(dft_t, dft).then_inc(filt_in, 16)
                for step in plan:
                    if step[0] == "vk" and step[1] in (1, 2, 4):
                        ty = (1, 2, 4).index(step[1])
                        a, b = ((0, 2), (2, 3), (3, 5))[ty]
                        pool.wait_ge(t_free, T_PER * l + t_index[step] + 1)
                        src = k_tok[:, a:b, :].rearrange("p j t -> p (j t)").rearrange("p (h d) -> p h d", d=64)
                        pool.dma_start(nk[ty][l].rearrange("h s d -> s h d"), src).then_inc(kv_out, 16)
                        src = vt[:, 0, P * a:P * b].rearrange("p (h d) -> p h d", d=64)
                        pool.dma_start(nv[ty][l].rearrange("h s d -> s h d"), src).then_inc(kv_out, 16)
                    elif step[0] in ("proj", "fused") and step[-1] == 0:
                        split(p.n0 + tile_of(step) + AHEAD)
                    elif step[0] == "taps":
                        _, o, tk = step
                        q = 6 * l + 3 * o + tk
                        pool.wait_ge(taps_h, q + 1)
                        if o:
                            pool.wait_ge(filt_mm, 6 * l + 3)
                        pool.tensor_tensor(taps[:, tk, 0, :], win[:, 0:256], win[:, 256:512], ALU.add)
                        pool.tensor_tensor(taps[:, tk, 1, :], win[:, 0:256], win[:, 256:512], ALU.subtract).then_inc(taps_ready, 1)
                    elif step[0] == "spectrum":
                        _, o, fc = step
                        q = 6 * l + 3 * o + fc
                        Z = spec[:, fc]
                        pool.wait_ge(spec_prod, q + 1)
                        pool.tensor_tensor(Z[:, 0, :], Z[:, 0, :], spec_t[:, 1, :], ALU.subtract)
                        pool.tensor_tensor(Z[:, 1, :], Z[:, 1, :], spec_t[:, 0, :], ALU.add).then_inc(spec_ready, 1)
                    elif step[0] == "fused" and step[1] and step[-1] == PARTS - 1:
                        _, i, n, _ = step
                        a = 3 * C * l + C * (i - 1) + n
                        pool.wait_ge(drained, p.n0 + FUSED0 + C * i + n + 1)
                        if a:
                            pool.wait_ge(merged_done, a)
                        pool.tensor_tensor(merged[:, n, :], merged[:, n, :], gated[:, n % 2, :], ALU.add).then_inc(merged_done, 1)

            for p in PHASES:
                if p.kind == "norm":
                    norm(p)
                elif p.kind == "up":
                    if p.first and p.ffn == 0:
                        layer_loads(p.l)
                    if p.first and p.ffn == 1:
                        pool.wait_ge(kv_out, 16 * 6 * (p.l + 1))
                    up(p)
                elif p.kind == "mix":
                    mix(p)
            pool.wait_ge(kv_out, 16 * 6 * DEPTH)

        @block.tensor
        def _(pe):
            def ready(base, rep=0):
                pe.wait_ge(lo_ready, base + 1 + 4 * rep)
                if base >= RING:
                    pe.wait_ge(drained, base - RING + 1 + 4 * rep)

            def tile(base, a_hi, a_lo, chunks, cols, before=None, off=0, out=None, count=True, part=None):
                slot = base % RING
                dst = (bank[slot] if out is None else out)[:, 0:cols]
                for c in range(chunks) if part is None else range(chunks // PARTS * part, chunks // PARTS * (part + 1)):
                    if before is not None:
                        before(c)
                    w = slice(off + P * c, off + P * (c + 1))
                    for k, (wt, ac) in enumerate(((hi, a_hi), (hi, a_lo), (lo, a_hi))):
                        last = pe.matmul(dst, wt[:, slot, w], ac[:, c, :], start=c == 0 and k == 0, stop=c == chunks - 1 and k == 2)
                if count and part in (None, PARTS - 1):
                    last.then_inc(tile_done, 1)

            def modulation_tile(base):
                slot = base % RING
                for c in range(C):
                    for k, wt in enumerate((hi, lo)):
                        last = pe.matmul(bank[slot][0:4, 0:P], c_parts[:, c, :], wt[:, slot, P * c:P * (c + 1)],
                                         start=c + k == 0, stop=c == C - 1 and k == 1)
                last.then_inc(tile_done, 1)

            def turn(a, drained_at, more=0, tiles=0):
                pe.wait_ge(drained, drained_at + tiles)
                if a:
                    pe.wait_ge(mod_done, a + more)
                pe.matmul(ps_t[:, 0:2], mod_row[:, a % 2, :], kk[0:4, K_SEL:K_SEL + 2], start=True, stop=True).then_inc(mod_turned, 1)

            def square_sum(k, c):
                pe.wait_ge(sq_ready, C * k + c + 1)
                last = pe.matmul(ps_o[:, 0:T], ones, sq[:, c, :], start=c == 0, stop=c == C - 1)
                if c == C - 1:
                    last.then_inc(ss_ready, 1)

            def norm(p):
                for c in range(C) if p.l + p.which == 0 else (C - 1,):
                    square_sum(nidx(p), c)

            def norms_by(p):
                return nidx(PHASES[[q is p for q in PHASES].index(True) + 1])

            def up(p):
                def first(c):
                    if p.first:
                        pe.wait_ge(h_lo_ready, hp8(p) + c + 1)

                per = 8 if p.ada else 4
                with pe.Fori(0, p.iters) as i:
                    for j in range(per):
                        ready(p.n0 + j, per // 4 * i)
                        if p.ada and j in (1, 5) and fcount(p) + j // 4 >= 1:
                            pe.wait_ge(silu_done, fcount(p) + j // 4 + 2 * i)
                        if p.ada and j % 2 == 0:
                            modulation_tile(p.n0 + j)
                            continue
                        tile(p.n0 + j, h_hi, h_lo, C, T, first if j == int(p.ada) else None)
                        if p.ada:
                            turn(p.m + j // 2, p.n0 + j - (j % 4 == 3), 4 * i, per * i)

            def down(p):
                f = FB * p.q + sum(THIRDS[:p.third])

                def product(c):
                    pe.wait_ge(g_lo_ready, f + c + 1)

                pe.wait_ge(silu_done, f + THIRDS[p.third])
                if p.third == 2:
                    for j in range(C):
                        ready(p.n0 + j)
                        tile(p.n0 + j, g_hi, g_lo, THIRDS[p.third], T, product if j == 0 else None)
                        if j:
                            square_sum(norms_by(p), j - 1)
                    return
                with pe.Fori(0, 2) as i:
                    for j in range(4):
                        ready(p.n0 + j, i)
                        tile(p.n0 + j, g_hi, g_lo, THIRDS[p.third], T, product if j == 0 else None)

            def mix(p):
                l = p.l

                def have(k):
                    pe.wait_ge(drained, p.n0 + k + 1)

                for step in plan:
                    kind = step[0]
                    if kind == "moda" or kind in ("proj", "fused", "out") and step[-1] == 0:
                        ready(p.n0 + tile_of(step))
                    if kind in ("proj", "out"):
                        before = None
                        if step[1] == 0:
                            hp = 4 * l + (1 if kind == "proj" else 2)

                            def before(c, hp=hp):
                                pe.wait_ge(h_lo_ready, C * hp + c + 1)
                        tile(p.n0 + tile_of(step), h_hi, h_lo, C, T, before, part=step[-1])
                    elif kind == "fused":
                        _, i, n, part = step
                        at = p.n0 + tile_of(step)

                        def pooled(c, m=4 * C * l + C * i + n + 1):
                            if P * (c + 1) > POOL_FROM:
                                pe.wait_ge(lo_pool, m)
                        tile(at, h_hi, h_lo, C, T, pooled, count=False, part=part)
                        if part < PARTS - 1:
                            continue
                        br = BRANCH_ORDER[i]
                        pe.wait_ge(o_lo_ready, 8 * l + 2 * i + 2)
                        pe.wait_ge(drained, at)
                        if i == 0 and n == 0:
                            pe.wait_ge(rope_done, 7 * (l + 1))
                        tile(at, o_hi[:, buf(br)], o_lo[:, buf(br)], 2, T, off=D, out=ps_br)
                    elif kind == "moda":
                        modulation_tile(p.n0 + tile_of(step))
                    elif kind == "modcol":
                        turn(p.m + step[1], p.n0 + tile_of(("moda", step[1])) + 1)
                    elif kind == "xsquare":
                        square_sum(norms_by(p), step[1])
                    elif kind == "sinmlp":
                        j = step[1]
                        if j == 0:
                            pe.wait_ge(filt_in, 16 * 6 * (l + 1))
                            pe.matmul(ps_s[0:HY_HID, 0:T], fw1, z_t, start=True, stop=True).then_inc(mlp_mm, 1)
                        else:
                            pe.wait_ge(mlp_sin, 2 * l + 1)
                            pe.matmul(ps_s[0:HY_HID, 0:T], fw2, fg, start=True, stop=True).then_inc(mlp_mm, 1)
                    elif kind == "taps":
                        _, o, tk = step
                        q = 6 * l + 3 * o + tk
                        pe.wait_ge(mlp_sin, 2 * l + 2)
                        pe.wait_ge(mlp_arg, 2 * l + 2)
                        if q >= 2:
                            pe.wait_ge(taps_h, q - 1)
                        if o:
                            pe.wait_ge(filt_ready, 6 * l + 3)
                        if l:
                            pe.wait_ge(drained, p.n0)
                        pe.matmul((ps_s, ps_br)[q % 2][:, :], fg[:, P * tk:P * (tk + 1)], fw3[:, 512 * o:512 * (o + 1)],
                                  start=True, stop=True).then_inc(taps_mm, 1)
                    elif kind == "tapsum":
                        _, o, tk = step
                        q = 6 * l + 3 * o + tk
                        pe.wait_ge(abs_ready, q + 1)
                        if o and tk == 0:
                            pe.wait_ge(scale_ready, 2 * l + 1)
                        g = 0 if tk == 0 else 1
                        for s in range(2):
                            last = pe.matmul(ps_t[:, 256 * g:256 * (g + 1)], ones, hab[:, 256 * s:256 * (s + 1)],
                                             start=s == 0 and tk < 2, stop=s == 1 and tk != 1)
                        last.then_inc(sum_mm, 1)
                    elif kind == "filter":
                        _, o, fc = step
                        q = 6 * l + 3 * o + fc
                        pe.wait_ge(taps_ready, 6 * l + 3 * (o + 1))
                        if q >= 2:
                            pe.wait_ge(filt_ready, q - 1)
                        dst = (ps_o, ps_s)[q % 2]
                        for s in range(2):
                            if fc == 0:
                                last = pe.matmul(dst[:, 256 * s:256 * (s + 1)], dft_t[:, P * s:P * (s + 1)], taps[:, 0, s, :], start=True, stop=True)
                            else:
                                for tk in range(2):
                                    a = 256 + 512 * s + 256 * tk + P * (fc - 1)
                                    last = pe.matmul(dst[:, 256 * s:256 * (s + 1)], dft_t[:, a:a + P], taps[:, 1 + tk, s, :],
                                                     start=tk == 0, stop=tk == 1)
                        last.then_inc(filt_mm, 1)
                    elif kind == "vk":
                        j, t = step[1], T_PER * l + t_index[step]
                        have((5, 5, 9, 15, 15)[j])
                        if t:
                            pe.wait_ge(t_free, t)
                        pe.wait_ge(scale_ready, 2 * (l + 1))
                        for tk in range(TB):
                            pe.transpose(ps_t[:, P * tk:P * (tk + 1)], v_all[:, j, P * tk:P * (tk + 1)], ident)
                        pe.transpose(ps_t[:, 3 * P:4 * P], kt[:, j, 0:P], ident).then_inc(t_ready, 1)
                    elif kind == "rope":
                        j = step[1]
                        src = (q_swa[:, 0], q_swa[:, 1], kt[:, 2], q_df[:, 0], q_df[:, 1], kt[:, 3], kt[:, 4])[j][:, T_CTX:T]
                        have(15)
                        pe.wait_ge(ctx_in, 64 * (l + 1))
                        pe.wait_ge(taps_ready, 6 * (l + 1))
                        if j + l:
                            pe.wait_ge(rope_done, 7 * l + j)
                        r = kk[:, K_R64:K_R64 + P] if j < 3 else kk[:, K_R32:K_R32 + P]
                        pe.matmul(ps_br[:, 0:T_DEN], r, src, start=True, stop=True).then_inc(rot_ready, 1)
                    elif kind == "scores":
                        _, ty, u, m = step
                        blk, hh, b = unit(u)
                        r = R_PER * l + r_index[step]
                        q = (q_na, q_swa, q_df)[ty]
                        kb = (blk, 2, 3 + blk)[ty]
                        if ty == NA:
                            have(5)
                        else:
                            pe.wait_ge(rope_done, 7 * (l + 1))
                        pe.wait_ge(ctx_in, 64 * (l + 1))
                        pe.wait_ge(filt_ready, 6 * (l + 1))
                        if r:
                            pe.wait_ge(exp_done, r)
                        k0, k1 = keys(b)
                        a = 64 * hh + 32 * m
                        e = a + (32 if ty == DF else 64)
                        pe.matmul(ps_s[:, 0:k1 - k0], q[a:e, blk, P * b:P * (b + 1)], kt[a:e, kb, k0:k1], start=True, stop=True).then_inc(scores_ready, 1)
                    elif kind == "turn":
                        _, ty, u = step
                        b = unit(u)[2]
                        t, g = T_PER * l + t_index[step], U_PER * l + 12 * ty + u
                        pe.wait_ge(probs_ready, g + 1)
                        pe.wait_ge(t_free, t)
                        n = (keys(b)[1] - keys(b)[0]) // P
                        for i in range(n):
                            last = pe.transpose(ps_t[:, P * i:P * (i + 1)], pr[:, 1 if ty == DF else u % 2, P * i:P * (i + 1)], ident)
                        last.then_inc(t_ready, 1)
                    elif kind == "values":
                        _, ty, u = step
                        blk, hh, b = unit(u)
                        pe.wait_ge(t_free, T_PER * l + t_index[("turn", ty, u)] + 1)
                        if u % 6 == 0:
                            pe.wait_ge(o_lo_ready, 8 * l + 2 * ty + blk)
                            if ty == NA:
                                pe.wait_ge(filt_ready, 6 * (l + 1))
                        col = (64 * (2 * blk + hh), 256 + 64 * hh, 384 + 64 * (2 * blk + hh))[ty]
                        chunks = (0,) if b == 0 else (1, 2, 3)
                        for i, ch in enumerate(chunks):
                            last = pe.matmul(ps_o[64 * hh:64 * hh + 64, P * b:P * (b + 1)], vt[:, ch, col:col + 64], prT[:, P * i:P * (i + 1)],
                                             start=i == 0, stop=i == len(chunks) - 1)
                        last.then_inc(values_done, 1)
                    elif kind == "subnorm":
                        blk, t = step[1], T_PER * l + t_index[step]
                        pe.wait_ge(osq_ready, 2 * l + blk + 1)
                        pe.wait_ge(t_free, t)
                        pe.matmul(ps_t[:, 0:T], bones, prT[:], start=True, stop=True).then_inc(t_ready, 1)
                    elif kind == "ytok":
                        _, o, blk = step
                        pe.wait_ge(y_ready, 6 * l + 2 * o + blk + 1)
                        pe.wait_ge(t_free, T_PER * l + t_index[step])
                        for tk in range(TB):
                            last = pe.transpose(ps_t[:, P * tk:P * (tk + 1)], hy[:, blk, P * tk:P * (tk + 1)], ident)
                        last.then_inc(t_ready, 1)
                    elif kind == "spectrum":
                        _, o, fc = step
                        q = 6 * l + 3 * o + fc
                        pe.wait_ge(t_free, T_PER * l + t_index[("ytok", o, 1)] + 1)
                        pe.wait_ge(exp_done, R_PER * (l + 1))
                        pe.wait_ge(o_lo_ready, 8 * l + 6)
                        if o:
                            pe.wait_ge(y_ready, 6 * l + 4)
                        if q >= 2:
                            pe.wait_ge(spec_ready, q - 1)
                        dst = (ps_s, ps_o)[q % 2]
                        for s in range(2):
                            if fc == 0:
                                a = (K_CP, K_SP)[s]
                                last = pe.matmul(dst[:, 256 * s:256 * (s + 1)], kk[:, a:a + P], y_tok[:, 0, :], start=True, stop=True)
                            else:
                                for tk in range(2):
                                    a = (K_CS, K_SS)[s] + 256 * tk + P * (fc - 1)
                                    last = pe.matmul(dst[:, 256 * s:256 * (s + 1)], kk[:, a:a + P], y_tok[:, 1 + tk, :], start=tk == 0, stop=tk == 1)
                        last.then_inc(spec_mm, 1)
                    elif kind == "conv":
                        _, o, blk = step
                        pe.wait_ge(spec_ready, 6 * l + 3 * (o + 1))
                        dst = (ps_s, ps_o)[blk]
                        for s in range(2):
                            a = (K_CP, K_SP)[s]
                            pe.matmul(dst[:, 0:T_CTX], spec[:, 0, s, P * blk:P * (blk + 1)], kk[:, a:a + P], start=s == 0, stop=s == 1)
                        for fc in range(2):
                            for s in range(2):
                                a = (K_CS, K_SS)[s] + 256 * fc
                                last = pe.matmul(dst[:, T_CTX:T], spec[:, 1 + fc, s, P * blk:P * (blk + 1)], kk[:, a:a + T_DEN],
                                                 start=fc + s == 0, stop=fc + s == 2)
                        last.then_inc(conv_mm, 1)

            pe.wait_ge(consts_in, 32)
            pe.wait_ge(cond_lo, 1)
            for p in PHASES:
                if p.kind == "ada":
                    for j in range(p.tiles):
                        ready(p.n0 + j)
                        modulation_tile(p.n0 + j)
                        if j:
                            turn(p.m + j - 1, p.n0 + j)
                    turn(p.m + p.tiles - 1, p.n0 + p.tiles)
                elif p.kind == "norm":
                    norm(p)
                elif p.kind == "up":
                    up(p)
                elif p.kind == "down":
                    down(p)
                else:
                    mix(p)


NORM_PHASES = [p for p in PHASES if p.kind == "norm"]


def nidx(p):
    return [id(q) for q in NORM_PHASES].index(id(p))


def hp8(p):
    if p.kind == "norm":
        return C * p.hp
    return C * (4 * p.l + (0 if p.ffn == 0 else 3))



def shape_constants():
    k = np.zeros((P, K_COLS), np.float64)
    i = np.arange(P)
    k[:, K_ID:K_ID + P] = np.eye(P)
    k[:, K_ONES:K_ONES + P] = 1
    k[:, K_BONES:K_BONES + P] = (i[:, None] // 64) == (i[None, :] // 64)
    for col, dh in ((K_R64, 64), (K_R32, 32)):
        nf = dh // 4
        r = np.zeros((P, P))
        for m in range(P):
            if (m // nf) % 2 == 0:
                r[m + nf, m] = -1
            else:
                r[m - nf, m] = 1
        k[:, col:col + P] = r
    qc, kc = i % GRID_W, np.arange(256) % GRID_W
    c0 = np.clip(qc - WIN_C // 2, 0, GRID_W - WIN_C)
    ok = (kc[None, :] >= c0[:, None]) & (kc[None, :] < c0[:, None] + WIN_C)
    k[:, K_NAM:K_NAM + 256] = np.where(ok, 0, NEG)
    k[:, K_SWM:K_SWM + P] = np.where(i[None, :] <= i[:, None], 0, NEG)
    k[:, K_SWM + P:K_SWM + 2 * P] = np.where(i[:, None] <= i[None, :], 0, NEG)

    def half(L, fn):
        a = np.arange(L)
        return fn(math.pi * np.outer(2 * a + 1, 2 * a + 1) / (4 * L))

    def whole(L, fn):
        a = np.arange(L)
        return fn(math.pi * np.outer(a, 2 * a + 1) / (2 * L))

    def rows(m):
        return m.reshape(2, P, 256).transpose(1, 0, 2).reshape(P, 512)

    k[:, K_CP:K_CP + P], k[:, K_SP:K_SP + P] = half(T_CTX, np.cos), half(T_CTX, np.sin)
    k[:, K_CS:K_CS + 512], k[:, K_SS:K_SS + 512] = rows(half(T_DEN, np.cos)), rows(half(T_DEN, np.sin))
    t = np.stack([i / T_CTX, i / T_DEN, (i + P) / T_DEN], 1)
    k[:, K_NTN:K_NTN + 3] = -t
    k[:, K_TM:K_TM + 3] = 1
    k[0, K_TM:K_TM + 2] = 0
    k[:, K_EPS] = EPS
    k[0, K_SEL] = k[1, K_SEL + 1] = k[2, K_SEL] = k[3, K_SEL + 1] = 1
    dft = np.concatenate([whole(T_CTX, np.cos), whole(T_CTX, np.sin), rows(whole(T_DEN, np.cos)), rows(whole(T_DEN, np.sin))], 1)
    tok = np.arange(T_DEN)
    rope = np.zeros((P, 4, T_DEN))
    for j, dh in ((0, 64), (2, 32)):
        nf = dh // 4
        f = (10000.0 ** (-np.arange(nf, dtype=np.float32) / nf)).astype(np.float32)
        for m in range(P):
            pos = (tok // GRID_W if (m % dh) < dh // 2 else tok % GRID_W).astype(np.float32)
            ang = (pos * f[m % nf]).astype(np.float32).astype(np.float64)
            rope[m, j], rope[m, j + 1] = np.cos(ang), np.sin(ang)
    z = []
    for L in (T_CTX, T_DEN):
        tn = (np.arange(L, dtype=np.float32) / L)
        ang = (np.float32(2.0 * math.pi) * tn[:, None] * np.arange(1, HY_FREQS + 1, dtype=np.float32)[None, :]).astype(np.float64)
        z.append(np.concatenate([tn[:, None], np.cos(ang), np.sin(ang)], 1))
    z = np.concatenate(z, 0).T
    f = lambda a: np.ascontiguousarray(a, dtype=np.float32)
    return f(k), f(dft), f(rope.reshape(P, 4 * T_DEN)), f(z)


def kernel(**inp):
    import concourse.bacc as bacc
    from concourse.bass_utils import run_bass_kernel_spmd as run

    a = {k: np.asarray(v) for k, v in inp.items()}
    f32 = np.float32

    def blocks(w):
        K, N = w.shape
        return w.reshape(K // P, P, N // P, P).transpose(2, 1, 0, 3).reshape(N // P, P, K)

    def cols(v):
        return v.reshape(-1, P).T

    n_main = N_TILES - len(WIDE)
    w_main = np.zeros((n_main, P, 1024), f32)
    w_fused = np.zeros((DEPTH * 4 * C, P, 1280), f32)
    ada = np.concatenate([blocks(a["w_ada"][l]) for l in range(DEPTH)])
    at = 0
    heads = np.r_[0:64, 128:192, 64:128, 192:256]
    for p in PHASES:
        if p.kind == "ada":
            w_main[at:at + p.tiles] = ada[p.m:p.m + p.tiles]
            at += p.tiles
        elif p.kind == "up":
            w1, w3 = (blocks(a[f"ffn{p.ffn + 1}_{w}"][p.l]) for w in ("w1", "w3"))
            fb = sum(THIRDS[:p.third]) + p.f0
            for i in range(p.iters):
                for s in range(2):
                    for w in (w1, w3):
                        if p.ada:
                            w_main[at] = ada[p.m + 4 * i + 2 * s + (w is w3)]
                            at += 1
                        w_main[at] = w[fb + 2 * i + s]
                        at += 1
        elif p.kind == "down":
            r0 = P * sum(THIRDS[:p.third])
            k = P * THIRDS[p.third]
            w_main[at:at + C, :, 0:k] = blocks(a[f"ffn{p.ffn + 1}_w2"][p.l][r0:r0 + k])
            at += C
        elif p.kind == "mix":
            w = blocks(a["w_in"][p.l])
            q = a["w_in"][p.l][:, 768:1024][:, heads]
            w[6:8] = blocks(q)
            w_main[at:at + 10] = w[0:10]
            w_main[at + 10:at + 16] = w[16:22]
            w_main[at + 16:at + 22] = w[10:16]
            at += N_PROJ
            for i, br in enumerate(BRANCH_ORDER):
                wb = a["w_branch"][p.l, br]
                if br == 1:
                    wb = wb[heads]
                dst = w_fused[4 * C * p.l + C * i:4 * C * p.l + C * (i + 1)]
                dst[:, :, 0:1024] = w[22 + C * br:22 + C * (br + 1)]
                dst[:, :, 1024:] = blocks(wb)
            wo = blocks(a["w_out"][p.l])
            done = set()
            for step in mix_plan():
                if step[0] in ("moda", "out") and step[:2] not in done:
                    done.add(step[:2])
                    w_main[at] = wo[step[1]] if step[0] == "out" else ada[p.m + step[1]]
                    at += 1
    assert at == n_main

    consts, dft, rope, zt = shape_constants()
    v = np.zeros((P, V_COLS), f32)
    v[:, V_COND:V_COND + 2 * C] = np.stack([cols(a["c_ctx"]), cols(a["c"][0])], 2).reshape(P, 2 * C)
    lam = np.zeros((P, DEPTH * 128), f32)
    mlp_w = np.zeros((DEPTH, 64, 128), f32)
    d_row = np.arange(4)[None, :] - np.arange(4)[:, None] + WIN_R - 1
    d_col = np.clip(np.arange(GRID_W)[None, :] - np.arange(GRID_W)[:, None] + WIN_C - 1, 0, 2 * WIN_C - 2)
    bias = np.zeros((DEPTH, P, 2, 4, 256), f32)
    kctx = np.zeros((DEPTH, P, 5, P), f32)
    vctx = np.zeros((DEPTH, P, 640), f32)
    for l in range(DEPTH):
        v[:, V_BADA + 72 * l:V_BADA + 72 * (l + 1)] = cols(a["b_ada"][l])
        for i, nm in enumerate(("norm_ffn1", "norm_mix", "norm_ffn2")):
            v[:, V_NORM + 24 * l + 8 * i:V_NORM + 24 * l + 8 * (i + 1)] = cols(a[nm][l])
        short = np.stack([cols(a["hy_short_w"][l, i]) for i in range(3)] + [cols(a["hy_short_b"][l])], 2)
        v[:, V_SHORT + 24 * l:V_SHORT + 24 * (l + 1)] = short.reshape(P, 24)
        v[:, V_SKIP + 4 * l:V_SKIP + 4 * (l + 1)] = np.concatenate([cols(a["hy_skip"][l, o]) for o in range(2)], 1)
        for i, nm in enumerate(("hy_sin_freq", "hy_b1", "hy_b2")):
            v[0:64, V_MLP + 3 * l + i] = a[nm][l]
        v[:, V_SUBLN + l] = np.tile(a["diff_subln"][l], 2)
        v[:, V_SINK + 4 * l:V_SINK + 4 * (l + 1)] = a["swa_sink"][l][None, :]
        lam[:, 128 * l:128 * (l + 1)] = a["diff_lambda"][l].reshape(1, 128)
        mlp_w[l, 0:HY_EMB, 0:64], mlp_w[l, :, 64:128] = a["hy_w1"][l], a["hy_w2"][l]
        e = a["na_rpb"][l][:, d_row[:, None, :, None], d_col[None, :, None, :]]
        bias[l] = e.reshape(4, 2, P, 256).transpose(2, 1, 0, 3)
        kc = [a[f"cache_{nm}_k"][0, l].transpose(0, 2, 1).reshape(-1, P, PAST) for nm in ("na", "swa", "diff")]
        kctx[l] = np.concatenate(kc).transpose(1, 0, 2)
        vc = [a[f"cache_{nm}_v"][0, l].transpose(1, 0, 2).reshape(PAST, -1) for nm in ("na", "swa", "diff")]
        vctx[l] = np.concatenate(vc, 1)
    v[:, V_FIN:V_FIN + C] = cols(a["final_norm"])
    xs = np.concatenate([a["x_prompt"][0], a["x_sample"][0]], 0)
    x_in = xs.T.reshape(C, P, T).transpose(1, 0, 2).reshape(P, C * T)
    logdecay = np.broadcast_to(a["hy_log_decay"][:, None, :], (DEPTH, P, 1024))

    arrays = dict(w_main=w_main, w_fused=w_fused, consts=consts, vecs=v, lam=lam, x_in=x_in, rope=rope,
                  bias=bias.reshape(DEPTH, P, 2048), logdecay=logdecay, kctx=kctx, vctx=vctx,
                  mlp_w=mlp_w, mlp_w3=a["hy_w3"], zt=zt, dft=dft)
    arrays = {k: np.ascontiguousarray(w) for k, w in arrays.items()}
    nc = bacc.Bacc("TRN2", target_bir_lowering=False, num_devices=1)
    ins = [nc.dram_tensor(k, w.shape, mybir.dt.from_np(w.dtype), kind="ExternalInput").ap() for k, w in arrays.items()]
    y_out = nc.dram_tensor("y_out", (P, C * T), F32, kind="ExternalOutput").ap()
    kv = {}
    for nm, h in (("na", 4), ("swa", 2), ("diff", 4)):
        for w in "kv":
            kv[nm + w] = nc.dram_tensor(f"new_{nm}_{w}", (DEPTH, h, T_CTX, 64), F32, kind="ExternalOutput").ap()
    build(nc, *ins, y_out, [kv["nak"], kv["swak"], kv["diffk"]], [kv["nav"], kv["swav"], kv["diffv"]])
    r = run(nc, [arrays], core_ids=[0]).results[0]
    y = r["y_out"].reshape(P, C, T).transpose(2, 1, 0).reshape(T, D)
    return (y[None, 0:T_CTX], y[None, T_CTX:T], r["new_na_k"][None], r["new_na_v"][None], r["new_swa_k"][None],
            r["new_swa_v"][None], r["new_diff_k"][None], r["new_diff_v"][None])
```

```python
import math
from contextlib import ExitStack

import numpy as np
import concourse.bass as bass
from concourse import mybir

F32 = mybir.dt.float32
F32R = mybir.dt.float32r
ALU = mybir.AluOpType
ACT = mybir.ActivationFunctionType
AX_X = mybir.AxisListType.X

D, T_CTX, T_DEN, DEPTH, PAST = 1024, 128, 256, 2, 128
GRID_W, WIN_R, WIN_C = 64, 8, 16
D_FF = 2816
P = 128
T = T_CTX + T_DEN
TB = T // P
C = D // P
FB = D_FF // P
N_MOD = 9
EPS = 1e-6
NEG = -1e30
HY_FREQS, HY_EMB, HY_HID = 16, 33, 64
GROUPS = ((0, T_CTX), (T_CTX, T))
RING = 4
AHEAD = RING - 1
PARTS = 4
FILTER_TILES = 12
NA_EARLY = 3
BEHIND = 4
POOL_FROM = 640
THIRDS = (8, 8, 6)
SH1, SC1, G1, SH2, SC2, G2, SH3, SC3, G3 = range(N_MOD)
N_PROJ = 22
BRANCH_ORDER = (0, 1, 3, 2)
NA, SWA, DF = range(3)
LAM_INIT = [0.8 - 0.6 * math.exp(-0.3 * l) for l in range(DEPTH)]

K_ID, K_ONES = 0, P
K_EPS = 2 * P
K_EARLY = K_EPS + 1
K_BONES, K_R64, K_R32 = (K_EARLY + P * i for i in range(3))
K_NAM = K_EARLY + 3 * P
K_SWM = K_NAM + 256
K_CP = K_SWM + 256
K_SP = K_CP + P
K_CS = K_SP + P
K_SS = K_CS + 512
K_NTN = K_SS + 512
K_TM = K_NTN + 3
K_COLS = K_TM + 3
V_COND = 0
V_BADA = V_COND + 2 * C
V_NORM = V_BADA + DEPTH * N_MOD * C
V_FIN = V_NORM + DEPTH * 3 * C
V_SHORT = V_FIN + C
V_SKIP = V_SHORT + DEPTH * 24
V_MLP = V_SKIP + DEPTH * 4
V_SUBLN = V_MLP + DEPTH * 3
V_SINK = V_SUBLN + DEPTH
V_SEL = V_SINK + DEPTH * 4
V_COLS = V_SEL + 2
TWO_PI_A = 6.28125
TWO_PI_B = float(np.float32(np.floor((2 * math.pi - TWO_PI_A) * 2 ** 20) / 2 ** 20))
TWO_PI_C = 2 * math.pi - TWO_PI_A - TWO_PI_B
ROUND = 1.5 * 2 ** 23
PI_DOWN = 3.1415925


class Phase:

    def __init__(self, kind, n0, tiles, l=0, which=0, hp=0, ffn=0, q=0, third=0, iters=0, ada=False, m=0, first=False, f0=0):
        self.kind, self.n0, self.tiles, self.l, self.which, self.hp = kind, n0, tiles, l, which, hp
        self.ffn, self.q, self.third, self.iters, self.ada, self.m, self.first, self.f0 = ffn, q, third, iters, ada, m, first, f0


def phases():
    out, n, ada_at = [], 0, 0

    def add(kind, tiles=0, **more):
        nonlocal n
        out.append(Phase(kind, n, tiles, **more))
        n += tiles

    def ada(count):
        nonlocal ada_at
        m = ada_at
        ada_at += count
        return m

    add("ada", 2 * C, m=ada(2 * C), l=0)
    for l in range(DEPTH):
        add("norm", l=l, which=0, hp=4 * l)
        for third, fbs in enumerate(THIRDS):
            for f0, iters in ((0, 1), (2, fbs // 2 - 1)) if l + third == 0 else ((0, fbs // 2),):
                add("up", 8 * iters, l=l, ffn=0, q=2 * l, third=third, iters=iters, ada=True, m=ada(4 * iters),
                    first=third + f0 == 0, f0=f0)
            add("down", C, l=l, ffn=0, q=2 * l, third=third)
        add("norm", l=l, which=1, hp=4 * l + 1)
        add("mix", N_PROJ + 5 * C + 4, l=l, m=ada(4))
        add("norm", l=l, which=2, hp=4 * l + 3)
        left = (3 * C if l + 1 < DEPTH else C) // 4
        for third, fbs in enumerate(THIRDS):
            k = min(left, fbs // 2)
            left -= k
            f0 = 0
            while k:
                run = min(k, (N_MOD * C - ada_at % (N_MOD * C)) // 4)
                add("up", 8 * run, l=l, ffn=1, q=2 * l + 1, third=third, iters=run, ada=True, m=ada(4 * run),
                    first=third == 0 and f0 == 0, f0=f0)
                k, f0 = k - run, f0 + 2 * run
            if f0 < fbs:
                add("up", 2 * (fbs - f0), l=l, ffn=1, q=2 * l + 1, third=third, iters=(fbs - f0) // 2, ada=False,
                    first=third == 0 and f0 == 0, f0=f0)
            add("down", C, l=l, ffn=1, q=2 * l + 1, third=third)
    add("norm", l=DEPTH - 1, which=3, hp=4 * DEPTH)
    return out, n


PHASES, N_TILES = phases()
MIX_N0 = [p.n0 for p in PHASES if p.kind == "mix"]
WIDE = {n0 + N_PROJ + j for n0 in MIX_N0 for j in range(4 * C)}


def width(n):
    return 1280 if n in WIDE else 1024


def parts(tiles):
    return [(*t, part) for t in tiles for part in range(PARTS)]


def paced(tiles, side):
    out = []
    scale = len(tiles) / sum(x for x in side if not isinstance(x, tuple))
    at, done = 0.0, 0
    for x in side:
        if isinstance(x, tuple):
            out.append(x)
            continue
        at += x * scale
        upto = min(len(tiles), int(at + 0.5))
        out += tiles[done:upto]
        done = upto
    return out + tiles[done:]


def attention_steps(kind):
    out = []
    if kind == DF:
        out += [("scores", kind, 0, 0), 1.3, ("scores", kind, 0, 1), ("probs", kind, 0), 1.5]
        for u in range(12):
            if u + 1 < 12:
                out.append(("scores", kind, u + 1, 0))
            if u < 6:
                out.append(("short", u))
            if 7 <= u < 7 + TB:
                out.append(("subinv", 0, u - 7))
            if u == 7 + TB:
                out.append(("subout", 0))
            out += [0.9, ("turn", kind, u), 0.9, ("values", kind, u), 0.1]
            if u + 1 < 12:
                out += [("scores", kind, u + 1, 1), ("probs", kind, u + 1)]
            out.append(1.5)
            if u % 6 == 5:
                out += [("square", u // 6), 0.6, ("subnorm", u // 6)]
        return out + [0.8] + [("subinv", 1, b) for b in range(TB)] + [0.6, ("subout", 1), 0.2]
    out += [("scores", kind, 0, 0), ("probs", kind, 0), 1.5]
    for u in range(12):
        if u + 1 < 12:
            out.append(("scores", kind, u + 1, 0))
        out += [1.0, ("turn", kind, u)]
        if u + 1 < 12:
            out.append(("probs", kind, u + 1))
        out += [1.2, ("values", kind, u), 0.2]
        if u % 6 == 5:
            out.append(("outs", kind, u // 6))
    return out


def staged(plan):
    out, fed, gates = [], [], []

    def flush(what):
        out.extend(what)
        what.clear()

    for s in plan:
        tile = s[0] in ("proj", "fused", "out")
        if tile and s[-1] == PARTS - 1:
            flush(fed)
        out.append(s)
        if tile and s[-1] == 0:
            fed.append(("feed", *s))
            flush(gates)
        if s[0] == "turn" or s[0] in ("proj", "out") and s[-1] == 1:
            flush(fed)
        if s[0] == "fused" and s[-1] == PARTS - 1:
            gates.append(("gate", *s[1:]))
            if s[1:3] == (3, C - 1):
                flush(gates)
    return out


def mix_plan():
    fil = [1.5, ("sinmlp", 1), 5.5]
    for o in range(2):
        for tk in range(TB):
            fil += [("taps", o, tk), 3.3, ("tapsum", o, tk), 0.3]
        fil += [("scale", o), 3.0]
        for fc in range(TB):
            fil += [("filter", o, fc), 0.8]
    proj = [("proj", k) for k in range(N_PROJ)]
    plan = [("sinmlp", 0)] + [s for pair in zip(parts(proj[0:1]), parts(proj[1:2])) for s in pair]
    plan += paced(parts(proj[2:FILTER_TILES]), fil)
    na = attention_steps(NA)
    cut = na.index(("values", NA, NA_EARLY))
    turns = [("vk", 2), ("vk", 3), ("vk", 4)] + [("rope", j) for j in range(7)]
    rest = []
    for s in na[cut:]:
        rest.append(s)
        if turns and isinstance(s, tuple) and s[0] == "values":
            rest += [0.5, turns.pop(0), 0.3]
    for s in turns:
        rest += [s, 0.8]
    plan += paced(parts(proj[FILTER_TILES:16]), [("vk", 0), 0.8, ("vk", 1), 0.2] + na[:cut]) + paced(parts(proj[16:]), rest)
    gates = [[("fused", i, n) for n in range(C)] for i in range(4)]
    swa, df = attention_steps(SWA), attention_steps(DF)
    gate_parts = parts(gates[0] + gates[1] + gates[2])
    until = len(parts(gates[0] + gates[1])) + 1
    plan += paced(gate_parts[:until], swa + df)
    hy = [0.4]
    for o in range(2):
        hy += [("ytok", o, 0), 1.2, ("ytok", o, 1), 1.5]
        for fc in range(TB):
            hy += [("spectrum", o, fc), 0.8]
        hy += [1.0, ("conv", o, 0), 0.8, ("conv", o, 1), 2.0]
    hy += [("hyout", 0), ("hyout", 1), 0.5]
    plan += paced(gate_parts[until:], hy)
    plan += parts(gates[3])
    out = [parts([("out", c)]) for c in range(C)]
    merged = [("merged", c) for c in range(C)]
    plan += merged[0:3] + [("moda", 0)] + merged[3:6] + [("moda", 1)] + merged[6:] + [("modrow", 0), ("modrow", 1)]
    for c in range(C):
        plan += out[c]
        if c:
            plan.append(("xsquare", c - 1))
        plan += {1: [("modcol", 0), ("modcol", 1), ("moda", 2), ("modrow", 2)], 2: [("modcol", 2)],
                 3: [("moda", 3), ("modrow", 3)], 4: [("modcol", 3)]}.get(c, [])
    return staged(plan)


def build(nc, w_main, w_fused, consts, vecs, lam, x_in, rope, bias, logdecay, kctx, vctx, mlp_w, mlp_w3, zt, dft,
          y_out, nk, nv):
    ctx = ExitStack()
    with ctx:
        def sb(name, shape, dt=F32):
            return ctx.enter_context(nc.sbuf_tensor(name, shape, dt))

        def sem(name):
            return ctx.enter_context(nc.semaphore(name))

        x = sb("x", [P, C, T])
        h_hi, h_lo = sb("h_hi", [P, C, T], F32R), sb("h_lo", [P, C, T], F32R)
        raw = sb("raw", [P, RING, 1280])
        hi, lo = sb("hi", [P, RING, 1280], F32R), sb("lo", [P, RING, 1280], F32R)
        kk = sb("kk", [P, K_COLS])
        vv = sb("vv", [P, V_COLS])
        mod = sb("mod", [P, N_MOD * C, 2])
        coef = sb("coef", [P, 3, C, 2])
        modb = sb("modb", [P, 2, C, 2])
        c_act = sb("c_act", [P, C, 2])
        c_parts = sb("c_parts", [P, C, 4], F32R)
        kt = sb("kt", [P, 5, 512])
        q_swa = sb("q_swa", [P, 2, T])
        vt = sb("vt", [P, 4, 640])
        areaM, areaE, areaF = sb("areaM", [P, 3072]), sb("areaE", [P, 3072]), sb("areaF", [P, 3072])
        pr = sb("pr", [P, 2, T])
        prT = sb("prT", [P, T])
        diag = prT[:, :].rearrange("p (b t) -> p b t", b=TB)
        o_hi, o_lo = sb("o_hi", [P, 2, 2, T], F32R), sb("o_lo", [P, 2, 2, T], F32R)
        tiny = sb("tiny", [P, 32])
        with nc.sbuf_tensor("g_hi", [P, C, T], F32R) as g_hi, nc.sbuf_tensor("g_lo", [P, C, T], F32R) as g_lo:
            pass
        areaG = sb("areaG", [P, 2 * C * T])
        hy = areaG[:, 0:7 * T].rearrange("p (j t) -> p j t", t=T)
        q_na = areaG[:, 7 * T:9 * T].rearrange("p (j t) -> p j t", t=T)
        q_df = areaG[:, 9 * T:11 * T].rearrange("p (j t) -> p j t", t=T)
        v_all = areaG[:, 11 * T:16 * T].rearrange("p (j t) -> p j t", t=T)
        k_tok = areaG[:, 11 * T:11 * T + 640].rearrange("p (j t) -> p j t", t=P)
        th = q_na
        mod_row = pr[0:4, :, 0:P]
        gated = v_all[:, 2:4, :]
        h_f = areaM[:, :].rearrange("p (c t) -> p c t", t=T)
        merged = h_f
        taps = areaM[:, 0:1536].rearrange("p (k s c) -> p k s c", k=TB, s=2)
        dft_t = areaM[:, 1536:1536 + 1280]
        na_bias = areaE[:, 0:2048].rearrange("p (b h k) -> p b h k", b=2, h=4)
        rope_t = areaE[:, 2048:3072].rearrange("p (j t) -> p j t", t=T_DEN)
        y_tok = areaE[:, 0:768].rearrange("p (k c) -> p k c", k=TB)
        spec = areaE[:, 768:2304].rearrange("p (f s c) -> p f s c", f=TB, s=2)
        spec_t = areaE[:, 2304:2816].rearrange("p (s c) -> p s c", s=2)
        sub_n, sub_o = areaE[:, 2304:2304 + T], areaE[:, 2304 + T:2304 + 2 * T]
        sq = areaF[:, :].rearrange("p (c t) -> p c t", t=T)
        sil = areaF[:, 0:2 * T].rearrange("p (s t) -> p s t", t=T)
        gf = areaF[:, 2 * T:4 * T].rearrange("p (s t) -> p s t", t=T)
        filt = areaF[:, :].rearrange("p (o f s c) -> p o f s c", o=2, f=TB, s=2)
        fw3 = areaF[0:HY_HID, 1536:2560]
        fg = areaF[0:HY_HID, 2560:2560 + T]
        rate = areaG[:, 0:1024]
        win = areaG[:, 1024:1536]
        hab = areaG[:, 1536:2048]
        z_t = areaG[0:HY_EMB, 2048:2048 + T]
        fw1 = areaG[0:HY_EMB, 2432:2496]
        fw2 = areaG[0:HY_HID, 2496:2560]
        f_arg, f_turn = q_df[0:HY_HID, 0, :], q_df[0:HY_HID, 1, :]
        f_inv = pr[:, :, :].rearrange("p a t -> p (a t)")[:, 0:512].rearrange("p (g c) -> p g c", g=2)

        lam_vecs = areaM[:, 0:DEPTH * 128]
        ident = kk[:, K_ID:K_ID + P]
        ones = kk[:, K_ONES:K_ONES + P]
        bones = kk[:, K_BONES:K_BONES + P]
        eps = kk[:, K_EPS:K_EPS + 1]

        bank = [ctx.enter_context(nc.psum_tensor(f"bank{i}", [P, 512], F32)) for i in range(RING)]
        ps_br, ps_s, ps_t, ps_o = (ctx.enter_context(nc.psum_tensor(n, [P, 512], F32)) for n in ("ps_br", "ps_s", "ps_t", "ps_o"))

        ss, rms, inv_rms = ps_o[:, T:T + TB], tiny[:, 16:16 + TB], tiny[:, 29:29 + TB]

        vecs_in, lo_pool, xn_ready = sem("vecs_in"), sem("lo_pool"), sem("xn_ready")
        taps_h, spec_prod = sem("taps_h"), sem("spec_prod")
        consts_in, raw_in = sem("consts_in"), [sem(f"raw_in{i}") for i in range(RING)]
        hi_ready, lo_ready, tile_done, drained = sem("hi_ready"), sem("lo_ready"), sem("tile_done"), sem("drained")
        cond_act, cond_hi, cond_lo = sem("cond_act"), sem("cond_hi"), sem("cond_lo")
        mod_turned, mod_done = sem("mod_turned"), sem("mod_done")
        silu_done, gf_ready, g_lo_ready = sem("silu_done"), sem("gf_ready"), sem("g_lo_ready")
        sq_ready, ss_ready, rms_ready = sem("sq_ready"), sem("ss_ready"), sem("rms_ready")
        diag_ready, rstd_ready = sem("diag_ready"), sem("rstd_ready")
        h_ready, h_hi_ready, h_lo_ready = sem("h_ready"), sem("h_hi_ready"), sem("h_lo_ready")
        dve_order, act_order = sem("dve_order"), sem("act_order")
        lam_exp, lam_dot = sem("lam_exp"), sem("lam_dot")
        mlp_in, tables_in = sem("mlp_in"), sem("tables_in")
        filt_in, ctx_in, bias_ready = sem("filt_in"), sem("ctx_in"), sem("bias_ready")
        mlp_mm, mlp_arg, mlp_sin = sem("mlp_mm"), sem("mlp_arg"), sem("mlp_sin")
        taps_mm, win_ready, taps_ready, abs_ready, sum_mm = (sem("taps_mm"), sem("win_ready"), sem("taps_ready"),
                                                             sem("abs_ready"), sem("sum_mm"))
        scale_ready, filt_mm, filt_ready = sem("scale_ready"), sem("filt_mm"), sem("filt_ready")
        t_ready, t_free = sem("t_ready"), sem("t_free")
        rot_ready, rope_done = sem("rot_ready"), sem("rope_done")
        scores_ready, max_ready, exp_done, probs_ready = (
            sem("scores_ready"), sem("max_ready"), sem("exp_done"), sem("probs_ready"))
        values_done, o_hi_ready, o_lo_ready = sem("values_done"), sem("o_hi_ready"), sem("o_lo_ready")
        osq_ready, onorm_ready = sem("osq_ready"), sem("onorm_ready")
        merged_done, th_ready = sem("merged_done"), sem("th_ready")
        y_ready, spec_mm, spec_ready, conv_mm = sem("y_ready"), sem("spec_mm"), sem("spec_ready"), sem("conv_mm")
        out_done, kv_out, y_fin = sem("out_done"), sem("kv_out"), sem("y_fin")

        plan = mix_plan()
        t_index = {s: i for i, s in enumerate([s for s in plan if s[0] in ("vk", "turn", "subnorm", "ytok")])}
        T_PER = len(t_index)
        rounds = [s for s in plan if s[0] == "scores"]
        r_index = {s: i for i, s in enumerate(rounds)}
        R_PER = len(rounds)
        U_PER = 36
        FUSED0 = N_PROJ

        def out_pair(branch, blk):
            return 2 * BRANCH_ORDER.index(branch) + blk

        def buf(branch):
            return BRANCH_ORDER.index(branch) % 2

        BR_OF = {NA: 0, SWA: 1, DF: 3}

        tiles = {}
        for step in plan:
            if step[0] in ("proj", "fused", "out"):
                tiles.setdefault(step[:-1], len(tiles))
            elif step[0] == "moda":
                tiles.setdefault(step, len(tiles))

        def tile_of(step):
            return tiles[step if step[0] == "moda" else ("fused" if step[0] == "gate" else step[0], *step[1:-1])]

        def unit(u):
            return u // 6, (u // 3) % 2, u % 3

        def keys(b):
            return (0, 128) if b == 0 else (128, 512)

        def fcount(p):
            return FB * p.q + sum(THIRDS[:p.third]) + (p.f0 if p.kind == "up" else 0)

        def vcol(i):
            return vv[:, i:i + 1]

        block = ctx.enter_context(nc.Block())

        @block.sync
        def _(sp):
            sp.dma_start(vv[:], vecs).then_inc(vecs_in, 16)
            sp.dma_start(lam_vecs, lam).then_inc(vecs_in, 16)

            def load(base, rep, src, pool=None):
                slot = base % RING
                if base >= RING:
                    sp.wait_ge(lo_ready, base - RING + 1 + 4 * rep)
                if pool is not None:
                    sp.wait_ge(lo_pool, pool)
                sp.dma_start(raw[:, slot, 0:width(base)], src).then_inc(raw_in[slot], 16)

            def main(j, i=0):
                return w_main[bass.ds(j + 4 * i, 1)].rearrange("a p n -> p (a n)")

            at, n = 0, 0
            for l, mix0 in enumerate(MIX_N0 + [None]):
                stop = N_TILES if mix0 is None else mix0 + N_PROJ
                for j in range(RING):
                    load(n, 0, w_main[at], 4 * C * l - 3 + j if l else None)
                    n, at = n + 1, at + 1
                if l == 0:
                    for j in range(RING):
                        load(n, 0, w_main[at])
                        n, at = n + 1, at + 1
                    sp.dma_start(kk[:, 0:K_EARLY], consts[:, 0:K_EARLY]).then_inc(consts_in, 16)
                    sp.dma_start(x[:, :, :].rearrange("p c t -> p (c t)"), x_in).then_inc(consts_in, 16)
                if l == 0:
                    for j in range(3 * RING):
                        load(n, 0, w_main[at])
                        n, at = n + 1, at + 1
                    sp.dma_start(kk[:, K_EARLY:K_COLS], consts[:, K_EARLY:K_COLS]).then_inc(tables_in, 16)
                groups = (stop - n) // RING
                with sp.Fori(0, groups) as i:
                    for j in range(RING):
                        load(n + j, i, main(at + j, i))
                n, at = n + RING * groups, at + RING * groups
                while n < stop:
                    load(n, 0, w_main[at])
                    n, at = n + 1, at + 1
                if mix0 is not None:
                    for j in range(4 * C):
                        load(n, 0, w_fused[4 * C * l + j], 4 * C * l + j - 3 if j >= RING else None)
                        n += 1
            for c in range(C):
                sp.wait_ge(y_fin, c + 1)
                sp.dma_start(y_out[:, T * c:T * (c + 1)], h_f[:, c, :]).then_inc(out_done, 16)
            sp.wait_ge(out_done, 16 * C)

        @block.scalar
        def _(act):
            order = [0]

            def link(ins):
                order[0] += 1
                ins.then_inc(act_order, 1)
                act.wait_ge(act_order, order[0])

            def split(base, rep=0):
                if base >= N_TILES:
                    return
                slot = base % RING
                act.wait_ge(raw_in[slot], 16 * (base // RING + 1 + rep))
                if base >= RING:
                    act.wait_ge(tile_done, base - RING + 1 + 4 * rep)
                act.activation(hi[:, slot, 0:width(base)], raw[:, slot, 0:width(base)], ACT.Copy).then_inc(hi_ready, 1)

            act.wait_ge(vecs_in, 32)
            act.activation(c_act[:, :, :].rearrange("p c g -> p (c g)"), vv[:, V_COND:V_COND + 2 * C], ACT.Silu).then_inc(cond_act, 1)
            act.wait_ge(cond_act, 1)
            act.activation(c_parts[:, :, 0:2], c_act[:], ACT.Copy).then_inc(cond_hi, 1)
            act.wait_ge(lam_dot, 1)
            act.activation(tiny[:, 4:8], tiny[:, 0:4], ACT.Exp).then_inc(lam_exp, 1)
            for n in range(AHEAD):
                split(n)

            def x_square(c, drained_at):
                if drained_at is None:
                    act.wait_ge(consts_in, 32)
                else:
                    act.wait_ge(drained, drained_at)
                act.activation(sq[:, c, :], x[:, c, :], ACT.Square).then_inc(sq_ready, 1)

            def norm(p):
                act.preload_act_table(ACT.Sqrt)
                if p.l + p.which:
                    x_square(C - 1, p.n0)
                act.wait_ge(ss_ready, nidx(p) + 1)
                act.activation(rms, ss, ACT.Sqrt, bias=eps, scale=1.0 / D).then_inc(rms_ready, 1)
                if p.which != 3:
                    split(p.n0 + AHEAD)
                    act.preload_act_table(ACT.Sin if p.which == 1 else ACT.Silu)
                if p.which == 3:
                    return
                for c in range(C):
                    act.wait_ge(h_ready, C * nidx(p) + c + 1)
                    act.activation(h_hi[:, c, :], h_f[:, c, :], ACT.Copy).then_inc(h_hi_ready, 1)

            def up(p):
                per = 8 if p.ada else 4

                def step(j, n0, f0, i=0):
                    if n0 + j != p.n0 or not p.first:
                        split(n0 + j + AHEAD, per // 4 * i)
                    if j in ((1, 5) if p.ada else (0, 2)):
                        s = 2 * j // per
                        f = f0 + s
                        act.wait_ge(tile_done, n0 + j + 1 + per * i)
                        if f >= 2:
                            act.wait_ge(gf_ready, f - 1 + 2 * i)
                            act.wait_ge(drained, n0 + j - (5 if p.ada else 2) + per * i)
                        act.activation(sil[:, s, :], bank[(n0 + j) % RING][:, 0:T], ACT.Silu).then_inc(silu_done, 1)

                peeled = int(p.first)
                for j in range(per * peeled):
                    step(j, p.n0, fcount(p))
                if p.iters > peeled:
                    with act.Fori(0, p.iters - peeled) as i:
                        for j in range(per):
                            step(j, p.n0 + per * peeled, fcount(p) + 2 * peeled, i)

            def down(p):
                if p.third == 2:
                    for j in range(C):
                        split(p.n0 + j + AHEAD)
                        if j:
                            x_square(j - 1, p.n0 + j)
                    return
                with act.Fori(0, 2) as i:
                    for j in range(4):
                        split(p.n0 + j + AHEAD, i)

            def mix(p):
                l = p.l
                if l == 0:
                    act.wait_ge(tables_in, 16)
                for step in plan:
                    kind = step[0]
                    if kind in ("moda", "feed"):
                        of = step[1:] if kind == "feed" else step
                        if tile_of(of):
                            split(p.n0 + tile_of(of) + AHEAD)
                    elif kind == "xsquare":
                        x_square(step[1], p.n0 + tile_of(("out", step[1], 0)) + 1)
                    elif kind == "gate":
                        at, n = p.n0 + tile_of(step), step[2]
                        act.wait_ge(tile_done, at + 1)
                        act.wait_ge(drained, at - 1)
                        act.activation(th[:, n % 2, :], bank[at % RING][:, 0:T], ACT.Tanh, scale=0.5).then_inc(th_ready, 1)
                    elif kind == "merged":
                        c = step[1]
                        act.wait_ge(merged_done, 3 * C * l + 2 * C + c + 1)
                        act.wait_ge(tile_done, p.n0 + N_PROJ + 4 * C)
                        act.activation(h_hi[:, c, :], merged[:, c, :], ACT.Copy).then_inc(h_hi_ready, 1)
                    elif kind == "sinmlp":
                        act.wait_ge(mlp_arg, 2 * l + step[1] + 1)
                        act.activation(fg, f_arg, ACT.Sin).then_inc(mlp_sin, 1)
                    elif kind == "taps":
                        _, o, tk = step
                        q = 6 * l + 3 * o + tk
                        if o == 0 and tk == 0:
                            act.wait_ge(mlp_in, 16 * 4 * (l + 1))
                            link(act.activation(rate, rate, ACT.Exp))
                        if q:
                            act.wait_ge(abs_ready, q)
                            act.wait_ge(taps_ready, q)
                        act.activation(win, rate[:, 512 * o:512 * (o + 1)], ACT.Exp, scale=kk[:, K_NTN + tk:K_NTN + tk + 1]).then_inc(win_ready, 1)
                    elif kind == "tapsum":
                        _, o, tk = step
                        q = 6 * l + 3 * o + tk
                        act.wait_ge(taps_h, q + 1)
                        if q:
                            act.wait_ge(sum_mm, q)
                        act.activation(hab, win, ACT.Abs).then_inc(abs_ready, 1)
                    elif kind == "vk":
                        j, t = step[1], T_PER * l + t_index[step]
                        act.wait_ge(t_ready, t + 1)
                        ps3 = ps_t[:, :].rearrange("p (k c) -> p k c", k=4)
                        act.activation(vt[:, 0:3, P * j:P * (j + 1)], ps3[:, 0:3, :], ACT.Copy).then_inc(act_order, 1)
                        order[0] += 1
                        act.activation(k_tok[:, j, :], ps3[:, 3, :], ACT.Copy).then_inc(t_free, 1)
                    elif kind == "scores":
                        _, ty, u, m = step
                        r = R_PER * l + r_index[step]
                        act.wait_ge(max_ready, r + 1)
                        b = unit(u)[2]
                        nk_ = keys(b)[1] - keys(b)[0]
                        nm = tiny[:, 8 + r % 4:9 + r % 4]
                        if ty == SWA:
                            head = unit(u)[0] + 2 * unit(u)[1]
                            order[0] += 1
                            act.activation(tiny[:, 20 + r % 4:21 + r % 4], vcol(V_SINK + 4 * l + head), ACT.Exp, bias=nm).then_inc(act_order, 1)
                        g = U_PER * l + 12 * ty + u
                        if ty == DF and m == 0:
                            act.wait_ge(probs_ready, g)
                        elif ty == DF:
                            act.wait_ge(t_ready, T_PER * l + turn_t(ty, u))
                        elif g > 1:
                            act.wait_ge(t_ready, T_PER * l + turn_t(ty, u - 1) if u else T_PER * l + turn_t(ty, 0))
                        dst = pr[:, m if ty == DF else u % 2, 0:nk_]
                        act.activation(dst, ps_s[:, 0:nk_], ACT.Exp, bias=nm, accum_out=tiny[:, 12 + r % 4:13 + r % 4]).then_inc(exp_done, 1)
                    elif kind == "turn":
                        _, ty, u = step
                        t, g = T_PER * l + t_index[step], U_PER * l + 12 * ty + u
                        act.wait_ge(t_ready, t + 1)
                        if g:
                            act.wait_ge(values_done, g)
                        nk_ = keys(unit(u)[2])[1] - keys(unit(u)[2])[0]
                        act.activation(prT[:, 0:nk_], ps_t[:, 0:nk_], ACT.Copy).then_inc(t_free, 1)
                    elif kind == "outs":
                        _, ty, blk = step
                        act.wait_ge(values_done, U_PER * l + 12 * ty + 6 * (blk + 1))
                        act.activation(o_hi[:, buf(BR_OF[ty]), blk, :], ps_o[:, 0:T], ACT.Copy).then_inc(o_hi_ready, 1)
                    elif kind == "square":
                        act.wait_ge(values_done, U_PER * l + 12 * DF + 6 * (step[1] + 1))
                        if step[1]:
                            act.wait_ge(o_lo_ready, 8 * l + out_pair(3, 0) + 1)
                        act.activation(sub_n, ps_o[:, 0:T], ACT.Square)
                        act.activation(sub_o, ps_o[:, 0:T], ACT.Copy).then_inc(osq_ready, 1)
                    elif kind == "subnorm":
                        blk = step[1]
                        act.wait_ge(t_ready, T_PER * l + t_index[step] + 1)
                        act.activation(sub_n, ps_t[:, 0:T], ACT.Sqrt, bias=eps, scale=1.0 / 64).then_inc(t_free, 1)
                    elif kind == "subout":
                        blk = step[1]
                        act.wait_ge(onorm_ready, 2 * l + blk + 1)
                        act.wait_ge(tile_done, p.n0 + FUSED0 + C)
                        act.activation(o_hi[:, buf(3), blk, :], sub_n, ACT.Copy).then_inc(o_hi_ready, 1)
                    elif kind == "ytok":
                        _, o, blk = step
                        act.wait_ge(t_ready, T_PER * l + t_index[step] + 1)
                        ps3 = ps_t[:, 0:T].rearrange("p (k c) -> p k c", k=3)
                        act.activation(y_tok[:, :, P * blk:P * (blk + 1)], ps3, ACT.Copy).then_inc(t_free, 1)
                    elif kind == "hyout":
                        blk = step[1]
                        act.wait_ge(y_ready, 6 * l + 4 + blk + 1)
                        act.wait_ge(tile_done, p.n0 + FUSED0 + 2 * C)
                        act.activation(o_hi[:, buf(2), blk, :], hy[:, blk, :], ACT.Copy).then_inc(o_hi_ready, 1)

            def turn_t(ty, u):
                return t_index[("turn", ty, u)] if u == 0 else t_index[("turn", ty, u - 1)] + 1

            for p in PHASES:
                if p.kind == "ada":
                    for j in range(p.tiles):
                        split(p.n0 + j + AHEAD)
                        if j >= C:
                            x_square(j - C, None)
                elif p.kind == "norm":
                    norm(p)
                elif p.kind == "up":
                    up(p)
                elif p.kind == "down":
                    down(p)
                else:
                    mix(p)

        @block.vector
        def _(dve):
            order = [0]

            def link(ins):
                order[0] += 1
                ins.then_inc(dve_order, 1)
                dve.wait_ge(dve_order, order[0])

            def split(base, rep=0):
                if base >= N_TILES:
                    return
                slot = base % RING
                dve.wait_ge(hi_ready, base + 1 + 4 * rep)
                w = POOL_FROM if base in WIDE else width(base)
                dve.tensor_tensor(lo[:, slot, 0:w], raw[:, slot, 0:w], hi[:, slot, 0:w].bitcast(F32), ALU.subtract).then_inc(lo_ready, 1)

            dve.wait_ge(vecs_in, 32)
            for l in range(DEPTH):
                for i in range(2):
                    a = 128 * l + 64 * i
                    link(dve.tensor_tensor(prT[:, 0:32], lam_vecs[:, a:a + 32], lam_vecs[:, a + 32:a + 64], ALU.mult))
                    link(dve.tensor_reduce(tiny[:, 2 * l + i:2 * l + i + 1], prT[:, 0:32], AX_X, ALU.add))
            dve.memset(tiny[:, 28:29], 0.0).then_inc(lam_dot, 1)
            dve.wait_ge(cond_hi, 1)
            dve.tensor_tensor(c_parts[:, :, 2:4], c_act[:], c_parts[:, :, 0:2].bitcast(F32), ALU.subtract).then_inc(cond_lo, 1)
            dve.wait_ge(lam_exp, 1)
            for l in range(DEPTH):
                nl = tiny[:, 24 + l:25 + l]
                link(dve.tensor_tensor(nl, tiny[:, 5 + 2 * l:6 + 2 * l], tiny[:, 4 + 2 * l:5 + 2 * l], ALU.subtract))
                link(dve.tensor_scalar(nl, nl, LAM_INIT[l], None, ALU.subtract))
                link(dve.tensor_scalar(tiny[:, 26 + l:27 + l], vcol(V_SUBLN + l), 1.0 - LAM_INIT[l], None, ALU.mult))
            for n in range(AHEAD):
                split(n)

            def modulation(l, v, slot):
                dve.wait_ge(mod_done, N_MOD * C * l + C * (v + 1))
                b = vv[:, V_BADA + N_MOD * C * l + C * v:V_BADA + N_MOD * C * l + C * (v + 1)].unsqueeze(2).broadcast_to([P, C, 2])
                link(dve.tensor_tensor(modb[:, slot], mod[:, C * v:C * (v + 1), :], b, ALU.add))

            def residual_gate(l, v):
                modulation(l, v, 0)
                link(dve.tensor_scalar(coef[:, 2], modb[:, 0], 0.5, None, ALU.mult))

            def norm(p):
                k = nidx(p)
                if p.which < 3:
                    modulation(p.l, (SC1, SC2, SC3)[p.which], 0)
                    a = V_NORM + 3 * C * p.l + C * p.which
                    w = vv[:, a:a + C].unsqueeze(2).broadcast_to([P, C, 2])
                    link(dve.scalar_tensor_tensor(coef[:, 0], modb[:, 0], 1.0, w, ALU.add, ALU.mult))
                    modulation(p.l, (SH1, SH2, SH3)[p.which], 1)
                dve.wait_ge(rms_ready, k + 1)
                link(dve.reciprocal(inv_rms, rms))
                dve.tensor_tensor(diag, ident.unsqueeze(1).broadcast_to([P, TB, P]), inv_rms.unsqueeze(2).broadcast_to([P, TB, P]),
                                  ALU.mult).then_inc(diag_ready, 1)
                if p.which < 3:
                    split(p.n0 + AHEAD)
                dve.wait_ge(rstd_ready, k + 1)

                def scaled(c):
                    dve.tensor_tensor(sq[:, c, :], x[:, c, :], ps_o[:, 0:T], ALU.mult).then_inc(xn_ready, 1)

                if p.which == 3:
                    for c in range(C):
                        dve.scalar_tensor_tensor(h_f[:, c, :], x[:, c, :], vcol(V_FIN + c), ps_o[:, 0:T], ALU.mult, ALU.mult).then_inc(y_fin, 1)
                    return
                scaled(0)
                for c in range(C):
                    if 0 < c < C - 1:
                        scaled(c + 1)
                    dve.wait_ge(xn_ready, C * k + c + 1)
                    for g, (t0, t1) in enumerate(GROUPS):
                        last = dve.tensor_scalar(h_f[:, c, t0:t1], sq[:, c, t0:t1], coef[:, 0, c, g:g + 1], modb[:, 1, c, g:g + 1],
                                                 ALU.mult, ALU.add)
                    last.then_inc(h_ready, 1)
                    if c == 0:
                        scaled(1)

            def h_low(count, src, c):
                dve.wait_ge(h_hi_ready, count + 1)
                dve.tensor_tensor(h_lo[:, c, :], src, h_hi[:, c, :].bitcast(F32), ALU.subtract).then_inc(h_lo_ready, 1)

            def up(p):
                if p.first and p.ffn == 1:
                    dve.wait_ge(kv_out, 16 * 6 * (p.l + 1))
                per = 8 if p.ada else 4

                def step(j, n0, f0, m0, g0, i=0):
                    n = n0 + j
                    if n != p.n0 or not p.first:
                        split(n + AHEAD, per // 4 * i)
                    if j in ((3, 7) if p.ada else (1, 3)):
                        s = 2 * j // per
                        f = f0 + s
                        b = bank[n % RING][:, 0:T]
                        dve.wait_ge(silu_done, f + 1 + 2 * i)
                        dve.wait_ge(tile_done, n + 1 + per * i)
                        if f >= 2:
                            dve.wait_ge(g_lo_ready, f - 1 + 2 * i)
                        dve.tensor_tensor(gf[:, s, :], sil[:, s, :], b, ALU.mult).then_inc(gf_ready, 1)
                        dst = g_hi[:, bass.ds(g0 + s + 2 * i, 1), :].rearrange("p a t -> p (a t)")
                        dve.tensor_tensor(dst, sil[:, s, :], b, ALU.mult).then_inc(drained, 2)
                    if p.ada and j % 2 == 0:
                        modulation_row(n, m0 + j // 2, per // 4 * i)
                    elif p.ada:
                        modulation_column(m0 + j // 2, 4 * i)

                peeled = int(p.first)
                for j in range(per * peeled):
                    step(j, p.n0, fcount(p), p.m, p.f0)
                if p.iters > peeled:
                    with dve.Fori(0, p.iters - peeled) as i:
                        for j in range(per):
                            step(j, p.n0 + per * peeled, fcount(p) + 2 * peeled, p.m + 4 * peeled, p.f0 + 2 * peeled, i)

            def modulation_row(n, a, rep=0):
                dve.wait_ge(tile_done, n + 1 + 4 * rep)
                dve.tensor_copy(mod_row[:, a % 2, :], bank[n % RING][0:4, 0:P]).then_inc(drained, 1)

            def modulation_column(a, more=0):
                dve.wait_ge(mod_turned, a + 1 + more)
                dst = mod[:, bass.ds(a % (N_MOD * C) + more, 1), :].rearrange("p a g -> p (a g)")
                dve.tensor_copy(dst, ps_t[:, 0:2]).then_inc(mod_done, 1)

            def add_to_x(n, c, rep=0, dyn=None):
                dve.wait_ge(tile_done, n + 1 + 4 * rep)
                for g, (t0, t1) in enumerate(GROUPS):
                    if dyn is None:
                        xs, gate = x[:, c, t0:t1], coef[:, 2, c, g:g + 1]
                    else:
                        xs = x[:, bass.ds(c + 4 * dyn, 1), t0:t1].rearrange("p a t -> p (a t)")
                        gate = coef[:, 2, bass.ds(c + 4 * dyn, 1), g:g + 1].rearrange("p a g -> p (a g)")
                    last = dve.scalar_tensor_tensor(xs, bank[n % RING][:, t0:t1], gate, xs, ALU.mult, ALU.add)
                last.then_inc(drained, 1)

            def down(p):
                if p.third == 0:
                    residual_gate(p.l, (G1, G3)[p.ffn])
                if p.third == 2:
                    for j in range(C):
                        split(p.n0 + j + AHEAD)
                        add_to_x(p.n0 + j, j)
                    return
                with dve.Fori(0, 2) as i:
                    for j in range(4):
                        split(p.n0 + j + AHEAD, i)
                        add_to_x(p.n0 + j, j, i, i)

            def proj_place(k):
                if k < 2:
                    return q_na[:, k, :], 0.125
                if k < 4:
                    return kt[:, k - 2, 0:T], 1.0
                if k < 6:
                    return v_all[:, k - 4, :], 1.0
                if k < 8:
                    return q_swa[:, k - 6, :], 0.125
                if k == 8:
                    return kt[:, 2, 0:T], 1.0
                if k == 9:
                    return v_all[:, 2, :], 1.0
                if k < 12:
                    return q_df[:, k - 10, :], 32 ** -0.5
                if k < 14:
                    return kt[:, k - 9, 0:T], 1.0
                if k < 16:
                    return v_all[:, k - 11, :], 1.0
                return hy[:, k - 15, :], 1.0

            def mix(p):
                l = p.l
                if l == 0:
                    dve.wait_ge(tables_in, 16)
                for step in plan:
                    kind = step[0]
                    if kind in ("moda", "feed"):
                        of = step[1:] if kind == "feed" else step
                        if tile_of(of):
                            split(p.n0 + tile_of(of) + AHEAD)
                        if of[0:2] == ("out", 0):
                            residual_gate(l, G2)
                    elif kind == "fused" or kind in ("proj", "out") and step[-1] < PARTS - 1:
                        pass
                    elif kind == "modrow":
                        modulation_row(p.n0 + tile_of(("moda", step[1])), p.m + step[1])
                    elif kind == "modcol":
                        modulation_column(p.m + step[1])
                    elif kind == "proj":
                        k = step[1]
                        if k == 10:
                            dve.wait_ge(mlp_sin, 2 * (l + 1))
                        dve.wait_ge(tile_done, p.n0 + k + 1)
                        dst, s = proj_place(k)
                        dve.tensor_scalar(dst, bank[(p.n0 + k) % RING][:, 0:T], s, None, ALU.mult).then_inc(drained, 1)
                    elif kind == "gate":
                        _, i, n, _ = step
                        at = p.n0 + FUSED0 + C * i + n
                        dve.wait_ge(th_ready, 4 * C * l + C * i + n + 1)
                        dve.wait_ge(tile_done, at + 1)
                        a = 3 * C * l + C * (i - 1) + n
                        if i == 0:
                            dst = merged[:, n, :]
                        else:
                            dst = gated[:, n % 2, :]
                            if n >= 2 or i > 1:
                                dve.wait_ge(merged_done, a - 1)
                        dve.scalar_tensor_tensor(dst, th[:, n % 2, :], 1.0, ps_br[:, 0:T], ALU.add, ALU.mult).then_inc(drained, 1)
                    elif kind == "merged":
                        h_low(C * (4 * l + 2) + step[1], merged[:, step[1], :], step[1])
                    elif kind == "out":
                        c = step[1]
                        n = p.n0 + tile_of(step)
                        add_to_x(n, c)
                    elif kind == "sinmlp":
                        j = step[1]
                        dve.wait_ge(mlp_mm, 2 * l + j + 1)
                        if l + j:
                            dve.wait_ge(mlp_sin, 2 * l + j)
                        f, b = (vv[0:HY_HID, V_MLP + 3 * l + i:V_MLP + 3 * l + i + 1] for i in (0, 1 + j))
                        link(dve.tensor_scalar(f_arg, ps_s[0:HY_HID, 0:T], b, f, ALU.add, ALU.mult))
                        link(dve.tensor_scalar(f_turn, f_arg, 1.0 / (2 * math.pi), ROUND, ALU.mult, ALU.add))
                        link(dve.tensor_scalar(f_turn, f_turn, ROUND, None, ALU.subtract))
                        for part in (TWO_PI_A, TWO_PI_B, TWO_PI_C):
                            link(dve.scalar_tensor_tensor(f_arg, f_turn, -part, f_arg, ALU.mult, ALU.add))
                        dve.tensor_scalar(f_arg, f_arg, PI_DOWN, -PI_DOWN, ALU.min, ALU.max).then_inc(mlp_arg, 1)
                    elif kind == "taps":
                        _, o, tk = step
                        q = 6 * l + 3 * o + tk
                        dve.wait_ge(win_ready, q + 1)
                        dve.wait_ge(taps_mm, q + 1)
                        ins = dve.tensor_tensor(win, (ps_s, ps_br)[q % 2][:, :], win, ALU.mult)
                        if tk < 2:
                            link(ins)
                            ins = dve.tensor_scalar(win[:, 256:512], win[:, 256:512], kk[:, K_TM + tk:K_TM + tk + 1], None, ALU.mult)
                        ins.then_inc(taps_h, 1)
                    elif kind == "scale":
                        o = step[1]
                        dve.wait_ge(sum_mm, 6 * l + 3 * (o + 1))
                        for g, L in enumerate((T_CTX, T_DEN)):
                            order[0] += 1
                            dve.tensor_scalar(f_inv[:, g, :], ps_t[:, 256 * g:256 * (g + 1)], EPS, float(L), ALU.add, ALU.mult).then_inc(dve_order, 1)
                        dve.wait_ge(dve_order, order[0])
                        dve.reciprocal(f_inv, f_inv).then_inc(scale_ready, 1)
                    elif kind == "filter":
                        _, o, fc = step
                        q = 6 * l + 3 * o + fc
                        dve.wait_ge(filt_mm, q + 1)
                        dve.wait_ge(scale_ready, 2 * l + o + 1)
                        g = 0 if fc == 0 else 1
                        psx = (ps_o, ps_s)[q % 2][:, :].rearrange("p (s c) -> p s c", s=2)
                        inv = f_inv[:, g:g + 1, :].broadcast_to([P, 2, 256])
                        dve.tensor_tensor(filt[:, o, fc], psx, inv, ALU.mult).then_inc(filt_ready, 1)
                    elif kind == "rope":
                        j = step[1]
                        swa = j < 3
                        tgt = (q_swa[:, 0], q_swa[:, 1], kt[:, 2], q_df[:, 0], q_df[:, 1], kt[:, 3], kt[:, 4])[j][:, T_CTX:T]
                        cos, sin = (rope_t[:, 0], rope_t[:, 1]) if swa else (rope_t[:, 2], rope_t[:, 3])
                        dve.wait_ge(rot_ready, 7 * l + j + 1)
                        order[0] += 1
                        dve.tensor_tensor(spare, ps_br[:, 0:T_DEN], sin, ALU.mult).then_inc(dve_order, 1)
                        link(dve.tensor_tensor(tgt, tgt, cos, ALU.mult))
                        dve.tensor_tensor(tgt, tgt, spare, ALU.add).then_inc(rope_done, 1)
                        dve.wait_ge(rope_done, 7 * l + j + 1)
                    elif kind == "scores":
                        _, ty, u, m = step
                        blk, hh, b = unit(u)
                        r = R_PER * l + r_index[step]
                        k0, k1 = keys(b)
                        nm = tiny[:, 8 + r % 4:9 + r % 4]
                        dve.wait_ge(scores_ready, r + 1)
                        if ty == NA and b:
                            dve.wait_ge(bias_ready, l + 1)
                            link(dve.tensor_tensor(ps_s[:, 0:256], ps_s[:, 0:256], na_bias[:, b - 1, 2 * blk + hh, :], ALU.add))
                        if ty == SWA and b:
                            c0 = 128 if b == 1 else 0
                            msk = kk[:, K_SWM + P * (b - 1):K_SWM + P * b]
                            link(dve.tensor_tensor(ps_s[:, c0:c0 + P], ps_s[:, c0:c0 + P], msk, ALU.add))
                        red = dve.tensor_reduce(nm, ps_s[:, 0:k1 - k0], AX_X, ALU.max, negate=True)
                        if ty == SWA:
                            link(red)
                            head = blk + 2 * hh
                            red = dve.scalar_tensor_tensor(nm, vcol(V_SINK + 4 * l + head), -1.0, nm, ALU.mult, ALU.min)
                        red.then_inc(max_ready, 1)
                    elif kind == "probs":
                        _, ty, u = step
                        nk_ = keys(unit(u)[2])[1] - keys(unit(u)[2])[0]
                        r = R_PER * l + r_index[("scores", ty, u, 1 if ty == DF else 0)]
                        dve.wait_ge(exp_done, r + 1)
                        rs = tiny[:, 12 + r % 4:13 + r % 4]
                        rr = tiny[:, 16 + r % 4:17 + r % 4]
                        if ty == SWA:
                            link(dve.tensor_tensor(rs, rs, tiny[:, 20 + r % 4:21 + r % 4], ALU.add))
                        link(dve.reciprocal(rr, rs))
                        if ty == DF:
                            r0 = R_PER * l + r_index[("scores", ty, u, 0)]
                            rs0, rr0 = tiny[:, 12 + r0 % 4:13 + r0 % 4], tiny[:, 16 + r0 % 4:17 + r0 % 4]
                            link(dve.reciprocal(rr0, rs0))
                            link(dve.tensor_tensor(rr, rr, tiny[:, 24 + l:25 + l], ALU.mult))
                            link(dve.tensor_scalar(pr[:, 0, 0:nk_], pr[:, 0, 0:nk_], rr0, None, ALU.mult))
                            dve.scalar_tensor_tensor(pr[:, 1, 0:nk_], pr[:, 1, 0:nk_], rr, pr[:, 0, 0:nk_], ALU.mult, ALU.add).then_inc(probs_ready, 1)
                        else:
                            dst = pr[:, u % 2, 0:nk_]
                            dve.tensor_scalar(dst, dst, rr, None, ALU.mult).then_inc(probs_ready, 1)
                    elif kind == "outs":
                        _, ty, blk = step
                        br = BR_OF[ty]
                        dve.wait_ge(o_hi_ready, 8 * l + out_pair(br, blk) + 1)
                        dve.tensor_tensor(o_lo[:, buf(br), blk, :], ps_o[:, 0:T], o_hi[:, buf(br), blk, :].bitcast(F32), ALU.subtract).then_inc(o_lo_ready, 1)
                    elif kind == "subinv":
                        _, blk, b = step
                        if b == 0:
                            dve.wait_ge(t_free, T_PER * l + t_index[("subnorm", blk)] + 1)
                        link(dve.reciprocal(sub_n[:, P * b:P * (b + 1)], sub_n[:, P * b:P * (b + 1)]))
                        if b == TB - 1:
                            dve.scalar_tensor_tensor(sub_n, sub_o, tiny[:, 26 + l:27 + l], sub_n, ALU.mult, ALU.mult).then_inc(onorm_ready, 1)
                    elif kind == "subout":
                        blk = step[1]
                        dve.wait_ge(o_hi_ready, 8 * l + out_pair(3, blk) + 1)
                        dve.tensor_tensor(o_lo[:, buf(3), blk, :], sub_n, o_hi[:, buf(3), blk, :].bitcast(F32), ALU.subtract).then_inc(o_lo_ready, 1)
                    elif kind == "short":
                        j = step[1]
                        z, u = hy[:, j, :], hy[:, j + 1, :]
                        w0, w1, w2, b = (vcol(V_SHORT + 24 * l + 4 * j + i) for i in range(4))
                        dve.wait_ge(drained, p.n0 + 16 + j + 1)
                        link(dve.tensor_scalar(z, u, w1, b, ALU.mult, ALU.add))
                        for w, shift in ((w0, -1), (w2, 1)):
                            for t0, t1 in GROUPS:
                                a0, a1 = (t0 + 1, t1) if shift < 0 else (t0, t1 - 1)
                                link(dve.scalar_tensor_tensor(z[:, a0:a1], u[:, a0 + shift:a1 + shift], w, z[:, a0:a1], ALU.mult, ALU.add))
                        if j in (0, 1):
                            dve.memset(tiny[:, 28:29], 0.0).then_inc(y_ready, 1)
                    elif kind == "spectrum":
                        _, o, fc = step
                        q = 6 * l + 3 * o + fc
                        Y = (ps_s, ps_o)[q % 2][:, :].rearrange("p (s c) -> p s c", s=2)
                        Fr, Fs = (filt[:, o, fc, s:s + 1, :].broadcast_to([P, 2, 256]) for s in range(2))
                        dve.wait_ge(spec_mm, q + 1)
                        if o:
                            dve.wait_ge(conv_mm, 4 * l + 2)
                        if q:
                            dve.wait_ge(spec_ready, q)
                        dve.tensor_tensor(spec[:, fc], Y, Fr, ALU.mult)
                        dve.tensor_tensor(spec_t, Y, Fs, ALU.mult).then_inc(spec_prod, 1)
                    elif kind == "conv":
                        _, o, blk = step
                        y, gate = hy[:, blk, :], hy[:, 2 + 2 * o + blk, :]
                        dve.wait_ge(conv_mm, 4 * l + 2 * o + blk + 1)
                        link(dve.scalar_tensor_tensor(y, y, vcol(V_SKIP + 4 * l + 2 * o + blk), (ps_s, ps_o)[blk][:, 0:T], ALU.mult, ALU.add))
                        dve.tensor_tensor(y, y, gate, ALU.mult).then_inc(y_ready, 1)
                        dve.wait_ge(y_ready, 6 * l + 2 + 2 * o + blk + 1)
                    elif kind == "hyout":
                        blk = step[1]
                        dve.wait_ge(o_hi_ready, 8 * l + out_pair(2, blk) + 1)
                        dve.tensor_tensor(o_lo[:, buf(2), blk, :], hy[:, blk, :], o_hi[:, buf(2), blk, :].bitcast(F32), ALU.subtract).then_inc(o_lo_ready, 1)

            spare = areaM[:, 2816:3072]
            for p in PHASES:
                if p.kind == "ada":
                    for j in range(p.tiles):
                        n = p.n0 + j
                        split(n + AHEAD)
                        modulation_row(n, p.m + j)
                        if j:
                            modulation_column(p.m + j - 1)
                    modulation_column(p.m + p.tiles - 1)
                elif p.kind == "norm":
                    norm(p)
                elif p.kind == "up":
                    up(p)
                elif p.kind == "down":
                    down(p)
                    dve.wait_ge(drained, p.n0 + p.tiles)
                else:
                    mix(p)
                    dve.wait_ge(drained, p.n0 + p.tiles)

        @block.gpsimd
        def _(pool):
            def up(p):
                with pool.Fori(0, p.iters) as i:
                    for s in range(2):
                        f = fcount(p) + s
                        per = 8 if p.ada else 4
                        n = p.n0 + (4 * s + 3 if p.ada else 2 * s + 1)
                        pool.wait_ge(gf_ready, f + 1 + 2 * i)
                        pool.wait_ge(drained, n + 1 + per * i)
                        at = bass.ds(p.f0 + s + 2 * i, 1)
                        pool.tensor_tensor(g_lo[:, at, :].rearrange("p a t -> p (a t)"), gf[:, s, :],
                                           g_hi[:, at, :].rearrange("p a t -> p (a t)").bitcast(F32), ALU.subtract).then_inc(g_lo_ready, 1)

            def norm(p):
                if p.which == 3:
                    return
                if p.which == 1:
                    l = p.l
                    pool.wait_ge(tile_done, p.n0)
                    pool.dma_start(z_t, zt).then_inc(mlp_in, 16)
                    pool.dma_start(fw1, mlp_w[l, 0:HY_EMB, 0:64]).then_inc(mlp_in, 16)
                    pool.dma_start(fw2, mlp_w[l, 0:HY_HID, 64:128]).then_inc(mlp_in, 16)
                    pool.dma_start(rate, logdecay[l]).then_inc(mlp_in, 16)
                for c in range(C):
                    pool.wait_ge(h_hi_ready, hp8(p) + c + 1)
                    pool.tensor_tensor(h_lo[:, c, :], h_f[:, c, :], h_hi[:, c, :].bitcast(F32), ALU.subtract).then_inc(h_lo_ready, 1)

            def split(base):
                if base not in WIDE:
                    return
                pool.wait_ge(hi_ready, base + 1)
                slot = base % RING
                pool.tensor_tensor(lo[:, slot, POOL_FROM:1280], raw[:, slot, POOL_FROM:1280],
                                   hi[:, slot, POOL_FROM:1280].bitcast(F32), ALU.subtract).then_inc(lo_pool, 1)

            def layer_loads(l):
                if l:
                    pool.wait_ge(tile_done, MIX_N0[l - 1] + N_PROJ + 5 * C)
                pool.dma_start(areaE[:, 0:2048], bias[l]).then_inc(ctx_in, 16)
                pool.dma_start(areaE[:, 2048:3072], rope).then_inc(ctx_in, 16)
                pool.dma_start(kt[:, :, T:512], kctx[l]).then_inc(ctx_in, 16)
                pool.dma_start(vt[:, 3, :], vctx[l]).then_inc(ctx_in, 16)
                pool.wait_ge(ctx_in, 64 * (l + 1))
                m = kk[:, K_NAM:K_NAM + 256].unsqueeze(1).broadcast_to([P, 8, 256])
                b8 = areaE[:, 0:2048].rearrange("p (b k) -> p b k", b=8)
                if l == 0:
                    pool.wait_ge(tables_in, 16)
                pool.tensor_tensor(b8, b8, m, ALU.add).then_inc(bias_ready, 1)

            def mix(p):
                l = p.l
                pool.wait_ge(h_lo_ready, C * (4 * l + 1) + C)
                pool.dma_start(fw3, mlp_w3[l]).then_inc(filt_in, 16)
                pool.dma_start(dft_t, dft).then_inc(filt_in, 16)
                for step in plan:
                    if step[0] == "vk" and step[1] in (1, 2, 4):
                        ty = (1, 2, 4).index(step[1])
                        a, b = ((0, 2), (2, 3), (3, 5))[ty]
                        pool.wait_ge(t_free, T_PER * l + t_index[step] + 1)
                        src = k_tok[:, a:b, :].rearrange("p j t -> p (j t)").rearrange("p (h d) -> p h d", d=64)
                        pool.dma_start(nk[ty][l].rearrange("h s d -> s h d"), src).then_inc(kv_out, 16)
                        src = vt[:, 0, P * a:P * b].rearrange("p (h d) -> p h d", d=64)
                        pool.dma_start(nv[ty][l].rearrange("h s d -> s h d"), src).then_inc(kv_out, 16)
                    elif step[0] == "feed":
                        split(p.n0 + tile_of(step[1:]) + AHEAD)
                    elif step[0] == "taps":
                        _, o, tk = step
                        q = 6 * l + 3 * o + tk
                        pool.wait_ge(taps_h, q + 1)
                        if o:
                            pool.wait_ge(filt_mm, 6 * l + 3)
                        pool.tensor_tensor(taps[:, tk, 0, :], win[:, 0:256], win[:, 256:512], ALU.add)
                        pool.tensor_tensor(taps[:, tk, 1, :], win[:, 0:256], win[:, 256:512], ALU.subtract).then_inc(taps_ready, 1)
                    elif step[0] == "spectrum":
                        _, o, fc = step
                        q = 6 * l + 3 * o + fc
                        Z = spec[:, fc]
                        pool.wait_ge(spec_prod, q + 1)
                        pool.tensor_tensor(Z[:, 0, :], Z[:, 0, :], spec_t[:, 1, :], ALU.subtract)
                        pool.tensor_tensor(Z[:, 1, :], Z[:, 1, :], spec_t[:, 0, :], ALU.add).then_inc(spec_ready, 1)
                    elif step[0] == "gate" and step[1]:
                        _, i, n, _ = step
                        a = 3 * C * l + C * (i - 1) + n
                        pool.wait_ge(drained, p.n0 + FUSED0 + C * i + n + 1)
                        if a:
                            pool.wait_ge(merged_done, a)
                        pool.tensor_tensor(merged[:, n, :], merged[:, n, :], gated[:, n % 2, :], ALU.add).then_inc(merged_done, 1)

            for p in PHASES:
                if p.kind == "norm":
                    norm(p)
                elif p.kind == "up":
                    if p.first and p.ffn == 0:
                        layer_loads(p.l)
                    if p.first and p.ffn == 1:
                        pool.wait_ge(kv_out, 16 * 6 * (p.l + 1))
                    up(p)
                elif p.kind == "mix":
                    mix(p)
            pool.wait_ge(kv_out, 16 * 6 * DEPTH)

        @block.tensor
        def _(pe):
            def ready(base, rep=0):
                pe.wait_ge(lo_ready, base + 1 + 4 * rep)
                if base >= RING:
                    pe.wait_ge(drained, base - RING + 1 + 4 * rep)

            def tile(base, a_hi, a_lo, chunks, cols, before=None, off=0, out=None, count=True, only=None):
                slot = base % RING
                dst = (bank[slot] if out is None else out)[:, 0:cols]
                for c in range(chunks) if only is None else only:
                    if before is not None:
                        before(c)
                    w = slice(off + P * c, off + P * (c + 1))
                    for k, (wt, ac) in enumerate(((hi, a_hi), (hi, a_lo), (lo, a_hi))):
                        last = pe.matmul(dst, wt[:, slot, w], ac[:, c, :], start=c == 0 and k == 0, stop=c == chunks - 1 and k == 2)
                if count and c == chunks - 1:
                    last.then_inc(tile_done, 1)

            def part_of(step):
                return range(C // PARTS * step[-1], C // PARTS * (step[-1] + 1))

            def modulation_tile(base, only=range(C)):
                slot = base % RING
                for c in only:
                    for k, wt in enumerate((hi, lo)):
                        last = pe.matmul(bank[slot][0:4, 0:P], c_parts[:, c, :], wt[:, slot, P * c:P * (c + 1)],
                                         start=c + k == 0, stop=c == C - 1 and k == 1)
                if c == C - 1:
                    last.then_inc(tile_done, 1)

            def turn(a, drained_at, more=0, tiles=0):
                pe.wait_ge(drained, drained_at + tiles)
                if a:
                    pe.wait_ge(mod_done, a + more)
                pe.matmul(ps_t[:, 0:2], mod_row[:, a % 2, :], vv[0:4, V_SEL:V_SEL + 2], start=True, stop=True).then_inc(mod_turned, 1)

            def square_sum(k, c):
                pe.wait_ge(sq_ready, C * k + c + 1)
                for b in range(TB):
                    last = pe.matmul(ss[:, b:b + 1], sq[:, c, P * b:P * (b + 1)], ones[:, 0:1], start=c + b == 0,
                                     stop=c == C - 1 and b == TB - 1)
                if c == C - 1:
                    last.then_inc(ss_ready, 1)

            def norm(p):
                before_up = p.which in (0, 2)
                if before_up:
                    ready(p.n0)
                    modulation_tile(p.n0)
                square_sum(nidx(p), C - 1)
                if before_up:
                    ready(p.n0 + 2)
                    modulation_tile(p.n0 + 2, range(C - 1))
                pe.wait_ge(diag_ready, nidx(p) + 1)
                pe.matmul(ps_o[:, 0:T], ones, prT[:], start=True, stop=True).then_inc(rstd_ready, 1)

            def norms_by(p):
                return nidx(PHASES[[q is p for q in PHASES].index(True) + 1])

            def first_blocks(p):
                n, f, m = p.n0, fcount(p), p.m
                ready(n + 1)
                if f:
                    pe.wait_ge(silu_done, f)
                ready(n + 3)
                for c in range(C):
                    pe.wait_ge(h_lo_ready, hp8(p) + c + 1)
                    tile(n + 1, h_hi, h_lo, C, T, only=(c,))
                    if c == C - 2:
                        turn(m, n + 1)
                    if c == C - 1:
                        modulation_tile(n + 2, (c,))
                    if c >= BEHIND:
                        tile(n + 3, h_hi, h_lo, C, T, only=(c - BEHIND,))
                tile(n + 3, h_hi, h_lo, C, T, only=range(C - BEHIND, C))
                turn(m + 1, n + 2)

            def up(p):
                per = 8 if p.ada else 4
                n0, f0, m0, iters = p.n0, fcount(p), p.m, p.iters

                def block(j, i=0):
                    ready(n0 + j, per // 4 * i)
                    if p.ada and j in (1, 5) and f0 + j // 4 >= 1:
                        pe.wait_ge(silu_done, f0 + j // 4 + 2 * i)
                    if p.ada and j % 2 == 0:
                        modulation_tile(n0 + j)
                        return
                    tile(n0 + j, h_hi, h_lo, C, T)
                    if p.ada:
                        turn(m0 + j // 2, n0 + j - (j % 4 == 3), 4 * i, per * i)

                if p.first:
                    first_blocks(p)
                    for j in range(4, 8):
                        block(j)
                    n0, f0, m0, iters = n0 + 8, f0 + 2, m0 + 4, iters - 1
                if iters:
                    with pe.Fori(0, iters) as i:
                        for j in range(per):
                            block(j, i)

            def down(p):
                f = FB * p.q + sum(THIRDS[:p.third])

                def product(c):
                    pe.wait_ge(g_lo_ready, f + c + 1)

                pe.wait_ge(silu_done, f + THIRDS[p.third])
                if p.third == 2:
                    for j in range(C):
                        ready(p.n0 + j)
                        tile(p.n0 + j, g_hi, g_lo, THIRDS[p.third], T, product if j == 0 else None)
                        if j:
                            square_sum(norms_by(p), j - 1)
                    return
                with pe.Fori(0, 2) as i:
                    for j in range(4):
                        ready(p.n0 + j, i)
                        tile(p.n0 + j, g_hi, g_lo, THIRDS[p.third], T, product if j == 0 else None)

            def mix(p):
                l = p.l

                def have(k):
                    pe.wait_ge(drained, p.n0 + k + 1)

                if l == 0:
                    pe.wait_ge(tables_in, 16)
                for step in plan:
                    kind = step[0]
                    if kind == "moda" or kind in ("proj", "fused", "out") and step[-1] == 0:
                        ready(p.n0 + tile_of(step))
                    if kind in ("proj", "out"):
                        before = None
                        if step[1] == 0:
                            hp = 4 * l + (1 if kind == "proj" else 2)

                            def before(c, hp=hp):
                                pe.wait_ge(h_lo_ready, C * hp + c + 1)
                        tile(p.n0 + tile_of(step), h_hi, h_lo, C, T, before, only=part_of(step))
                    elif kind == "fused":
                        _, i, n, part = step
                        at = p.n0 + tile_of(step)

                        def pooled(c, m=4 * C * l + C * i + n + 1):
                            if P * (c + 1) > POOL_FROM:
                                pe.wait_ge(lo_pool, m)
                        tile(at, h_hi, h_lo, C, T, pooled, count=False, only=part_of(step))
                        if part < PARTS - 1:
                            continue
                        br = BRANCH_ORDER[i]
                        pe.wait_ge(o_lo_ready, 8 * l + 2 * i + 2)
                        pe.wait_ge(drained, at)
                        if i == 0 and n == 0:
                            pe.wait_ge(rope_done, 7 * (l + 1))
                        tile(at, o_hi[:, buf(br)], o_lo[:, buf(br)], 2, T, off=D, out=ps_br)
                    elif kind == "moda":
                        modulation_tile(p.n0 + tile_of(step))
                    elif kind == "modcol":
                        turn(p.m + step[1], p.n0 + tile_of(("moda", step[1])) + 1)
                    elif kind == "xsquare":
                        square_sum(norms_by(p), step[1])
                    elif kind == "sinmlp":
                        j = step[1]
                        if j == 0:
                            pe.wait_ge(mlp_in, 16 * 4 * (l + 1))
                            pe.matmul(ps_s[0:HY_HID, 0:T], fw1, z_t, start=True, stop=True).then_inc(mlp_mm, 1)
                        else:
                            pe.wait_ge(mlp_sin, 2 * l + 1)
                            pe.matmul(ps_s[0:HY_HID, 0:T], fw2, fg, start=True, stop=True).then_inc(mlp_mm, 1)
                    elif kind == "taps":
                        _, o, tk = step
                        q = 6 * l + 3 * o + tk
                        pe.wait_ge(mlp_sin, 2 * l + 2)
                        pe.wait_ge(mlp_arg, 2 * l + 2)
                        pe.wait_ge(filt_in, 16 * 2 * (l + 1))
                        if q >= 2:
                            pe.wait_ge(taps_h, q - 1)
                        if o:
                            pe.wait_ge(filt_ready, 6 * l + 3)
                        if l:
                            pe.wait_ge(drained, p.n0)
                        pe.matmul((ps_s, ps_br)[q % 2][:, :], fg[:, P * tk:P * (tk + 1)], fw3[:, 512 * o:512 * (o + 1)],
                                  start=True, stop=True).then_inc(taps_mm, 1)
                    elif kind == "tapsum":
                        _, o, tk = step
                        q = 6 * l + 3 * o + tk
                        pe.wait_ge(abs_ready, q + 1)
                        if o and tk == 0:
                            pe.wait_ge(scale_ready, 2 * l + 1)
                        g = 0 if tk == 0 else 1
                        for s in range(2):
                            last = pe.matmul(ps_t[:, 256 * g:256 * (g + 1)], ones, hab[:, 256 * s:256 * (s + 1)],
                                             start=s == 0 and tk < 2, stop=s == 1 and tk != 1)
                        last.then_inc(sum_mm, 1)
                    elif kind == "filter":
                        _, o, fc = step
                        q = 6 * l + 3 * o + fc
                        pe.wait_ge(taps_ready, 6 * l + 3 * (o + 1))
                        if q >= 2:
                            pe.wait_ge(filt_ready, q - 1)
                        dst = (ps_o, ps_s)[q % 2]
                        for s in range(2):
                            if fc == 0:
                                last = pe.matmul(dst[:, 256 * s:256 * (s + 1)], dft_t[:, P * s:P * (s + 1)], taps[:, 0, s, :], start=True, stop=True)
                            else:
                                for tk in range(2):
                                    a = 256 + 512 * s + 256 * tk + P * (fc - 1)
                                    last = pe.matmul(dst[:, 256 * s:256 * (s + 1)], dft_t[:, a:a + P], taps[:, 1 + tk, s, :],
                                                     start=tk == 0, stop=tk == 1)
                        last.then_inc(filt_mm, 1)
                    elif kind == "vk":
                        j, t = step[1], T_PER * l + t_index[step]
                        have((5, 5, 9, 15, 15)[j])
                        if t:
                            pe.wait_ge(t_free, t)
                        pe.wait_ge(scale_ready, 2 * (l + 1))
                        for tk in range(TB):
                            pe.transpose(ps_t[:, P * tk:P * (tk + 1)], v_all[:, j, P * tk:P * (tk + 1)], ident)
                        pe.transpose(ps_t[:, 3 * P:4 * P], kt[:, j, 0:P], ident).then_inc(t_ready, 1)
                    elif kind == "rope":
                        j = step[1]
                        src = (q_swa[:, 0], q_swa[:, 1], kt[:, 2], q_df[:, 0], q_df[:, 1], kt[:, 3], kt[:, 4])[j][:, T_CTX:T]
                        have(15)
                        pe.wait_ge(ctx_in, 64 * (l + 1))
                        pe.wait_ge(taps_ready, 6 * (l + 1))
                        if j + l:
                            pe.wait_ge(rope_done, 7 * l + j)
                        r = kk[:, K_R64:K_R64 + P] if j < 3 else kk[:, K_R32:K_R32 + P]
                        pe.matmul(ps_br[:, 0:T_DEN], r, src, start=True, stop=True).then_inc(rot_ready, 1)
                    elif kind == "scores":
                        _, ty, u, m = step
                        blk, hh, b = unit(u)
                        r = R_PER * l + r_index[step]
                        q = (q_na, q_swa, q_df)[ty]
                        kb = (blk, 2, 3 + blk)[ty]
                        if ty == NA:
                            have(5)
                        else:
                            pe.wait_ge(rope_done, 7 * (l + 1))
                        pe.wait_ge(ctx_in, 64 * (l + 1))
                        pe.wait_ge(filt_ready, 6 * (l + 1))
                        if r:
                            pe.wait_ge(exp_done, r)
                        k0, k1 = keys(b)
                        a = 64 * hh + 32 * m
                        e = a + (32 if ty == DF else 64)
                        pe.matmul(ps_s[:, 0:k1 - k0], q[a:e, blk, P * b:P * (b + 1)], kt[a:e, kb, k0:k1], start=True, stop=True).then_inc(scores_ready, 1)
                    elif kind == "turn":
                        _, ty, u = step
                        b = unit(u)[2]
                        t, g = T_PER * l + t_index[step], U_PER * l + 12 * ty + u
                        pe.wait_ge(probs_ready, g + 1)
                        pe.wait_ge(t_free, t)
                        n = (keys(b)[1] - keys(b)[0]) // P
                        for i in range(n):
                            last = pe.transpose(ps_t[:, P * i:P * (i + 1)], pr[:, 1 if ty == DF else u % 2, P * i:P * (i + 1)], ident)
                        last.then_inc(t_ready, 1)
                    elif kind == "values":
                        _, ty, u = step
                        blk, hh, b = unit(u)
                        pe.wait_ge(t_free, T_PER * l + t_index[("turn", ty, u)] + 1)
                        if u % 6 == 0:
                            if ty == DF and blk:
                                pe.wait_ge(osq_ready, 2 * l + 1)
                            else:
                                pe.wait_ge(o_lo_ready, 8 * l + 2 * ty + blk)
                            if ty == NA:
                                pe.wait_ge(filt_ready, 6 * (l + 1))
                        col = (64 * (2 * blk + hh), 256 + 64 * hh, 384 + 64 * (2 * blk + hh))[ty]
                        chunks = (0,) if b == 0 else (1, 2, 3)
                        for i, ch in enumerate(chunks):
                            last = pe.matmul(ps_o[64 * hh:64 * hh + 64, P * b:P * (b + 1)], vt[:, ch, col:col + 64], prT[:, P * i:P * (i + 1)],
                                             start=i == 0, stop=i == len(chunks) - 1)
                        last.then_inc(values_done, 1)
                    elif kind == "subnorm":
                        blk, t = step[1], T_PER * l + t_index[step]
                        pe.wait_ge(osq_ready, 2 * l + blk + 1)
                        pe.wait_ge(t_free, t)
                        pe.matmul(ps_t[:, 0:T], bones, sub_n, start=True, stop=True).then_inc(t_ready, 1)
                    elif kind == "ytok":
                        _, o, blk = step
                        pe.wait_ge(y_ready, 6 * l + 2 * o + blk + 1)
                        pe.wait_ge(t_free, T_PER * l + t_index[step])
                        for tk in range(TB):
                            last = pe.transpose(ps_t[:, P * tk:P * (tk + 1)], hy[:, blk, P * tk:P * (tk + 1)], ident)
                        last.then_inc(t_ready, 1)
                    elif kind == "spectrum":
                        _, o, fc = step
                        q = 6 * l + 3 * o + fc
                        pe.wait_ge(t_free, T_PER * l + t_index[("ytok", o, 1)] + 1)
                        pe.wait_ge(exp_done, R_PER * (l + 1))
                        pe.wait_ge(o_lo_ready, 8 * l + 6)
                        if o:
                            pe.wait_ge(y_ready, 6 * l + 4)
                        if q >= 2:
                            pe.wait_ge(spec_ready, q - 1)
                        dst = (ps_s, ps_o)[q % 2]
                        for s in range(2):
                            if fc == 0:
                                a = (K_CP, K_SP)[s]
                                last = pe.matmul(dst[:, 256 * s:256 * (s + 1)], kk[:, a:a + P], y_tok[:, 0, :], start=True, stop=True)
                            else:
                                for tk in range(2):
                                    a = (K_CS, K_SS)[s] + 256 * tk + P * (fc - 1)
                                    last = pe.matmul(dst[:, 256 * s:256 * (s + 1)], kk[:, a:a + P], y_tok[:, 1 + tk, :], start=tk == 0, stop=tk == 1)
                        last.then_inc(spec_mm, 1)
                    elif kind == "conv":
                        _, o, blk = step
                        pe.wait_ge(spec_ready, 6 * l + 3 * (o + 1))
                        dst = (ps_s, ps_o)[blk]
                        for s in range(2):
                            a = (K_CP, K_SP)[s]
                            pe.matmul(dst[:, 0:T_CTX], spec[:, 0, s, P * blk:P * (blk + 1)], kk[:, a:a + P], start=s == 0, stop=s == 1)
                        for fc in range(2):
                            for s in range(2):
                                a = (K_CS, K_SS)[s] + 256 * fc
                                last = pe.matmul(dst[:, T_CTX:T], spec[:, 1 + fc, s, P * blk:P * (blk + 1)], kk[:, a:a + T_DEN],
                                                 start=fc + s == 0, stop=fc + s == 2)
                        last.then_inc(conv_mm, 1)

            pe.wait_ge(vecs_in, 32)
            pe.wait_ge(cond_lo, 1)
            for p in PHASES:
                if p.kind == "ada":
                    for j in range(p.tiles):
                        ready(p.n0 + j)
                        modulation_tile(p.n0 + j)
                        if j:
                            turn(p.m + j - 1, p.n0 + j)
                        if j > C:
                            square_sum(0, j - 1 - C)
                    turn(p.m + p.tiles - 1, p.n0 + p.tiles)
                elif p.kind == "norm":
                    norm(p)
                elif p.kind == "up":
                    up(p)
                elif p.kind == "down":
                    down(p)
                else:
                    mix(p)


NORM_PHASES = [p for p in PHASES if p.kind == "norm"]


def nidx(p):
    return [id(q) for q in NORM_PHASES].index(id(p))


def hp8(p):
    if p.kind == "norm":
        return C * p.hp
    return C * (4 * p.l + (0 if p.ffn == 0 else 3))



def shape_constants():
    k = np.zeros((P, K_COLS), np.float64)
    i = np.arange(P)
    k[:, K_ID:K_ID + P] = np.eye(P)
    k[:, K_ONES:K_ONES + P] = 1
    k[:, K_BONES:K_BONES + P] = (i[:, None] // 64) == (i[None, :] // 64)
    for col, dh in ((K_R64, 64), (K_R32, 32)):
        nf = dh // 4
        r = np.zeros((P, P))
        for m in range(P):
            if (m // nf) % 2 == 0:
                r[m + nf, m] = -1
            else:
                r[m - nf, m] = 1
        k[:, col:col + P] = r
    qc, kc = i % GRID_W, np.arange(256) % GRID_W
    c0 = np.clip(qc - WIN_C // 2, 0, GRID_W - WIN_C)
    ok = (kc[None, :] >= c0[:, None]) & (kc[None, :] < c0[:, None] + WIN_C)
    k[:, K_NAM:K_NAM + 256] = np.where(ok, 0, NEG)
    k[:, K_SWM:K_SWM + P] = np.where(i[None, :] <= i[:, None], 0, NEG)
    k[:, K_SWM + P:K_SWM + 2 * P] = np.where(i[:, None] <= i[None, :], 0, NEG)

    def half(L, fn):
        a = np.arange(L)
        return fn(math.pi * np.outer(2 * a + 1, 2 * a + 1) / (4 * L))

    def whole(L, fn):
        a = np.arange(L)
        return fn(math.pi * np.outer(a, 2 * a + 1) / (2 * L))

    def rows(m):
        return m.reshape(2, P, 256).transpose(1, 0, 2).reshape(P, 512)

    k[:, K_CP:K_CP + P], k[:, K_SP:K_SP + P] = half(T_CTX, np.cos), half(T_CTX, np.sin)
    k[:, K_CS:K_CS + 512], k[:, K_SS:K_SS + 512] = rows(half(T_DEN, np.cos)), rows(half(T_DEN, np.sin))
    t = np.stack([i / T_CTX, i / T_DEN, (i + P) / T_DEN], 1)
    k[:, K_NTN:K_NTN + 3] = -t
    k[:, K_TM:K_TM + 3] = 1
    k[0, K_TM:K_TM + 2] = 0
    k[:, K_EPS] = EPS
    dft = np.concatenate([whole(T_CTX, np.cos), whole(T_CTX, np.sin), rows(whole(T_DEN, np.cos)), rows(whole(T_DEN, np.sin))], 1)
    tok = np.arange(T_DEN)
    rope = np.zeros((P, 4, T_DEN))
    for j, dh in ((0, 64), (2, 32)):
        nf = dh // 4
        f = (10000.0 ** (-np.arange(nf, dtype=np.float32) / nf)).astype(np.float32)
        for m in range(P):
            pos = (tok // GRID_W if (m % dh) < dh // 2 else tok % GRID_W).astype(np.float32)
            ang = (pos * f[m % nf]).astype(np.float32).astype(np.float64)
            rope[m, j], rope[m, j + 1] = np.cos(ang), np.sin(ang)
    z = []
    for L in (T_CTX, T_DEN):
        tn = (np.arange(L, dtype=np.float32) / L)
        ang = (np.float32(2.0 * math.pi) * tn[:, None] * np.arange(1, HY_FREQS + 1, dtype=np.float32)[None, :]).astype(np.float64)
        z.append(np.concatenate([tn[:, None], np.cos(ang), np.sin(ang)], 1))
    z = np.concatenate(z, 0).T
    f = lambda a: np.ascontiguousarray(a, dtype=np.float32)
    return f(k), f(dft), f(rope.reshape(P, 4 * T_DEN)), f(z)


def kernel(**inp):
    import concourse.bacc as bacc
    from concourse.bass_utils import run_bass_kernel_spmd as run

    a = {k: np.asarray(v) for k, v in inp.items()}
    f32 = np.float32

    def blocks(w):
        K, N = w.shape
        return w.reshape(K // P, P, N // P, P).transpose(2, 1, 0, 3).reshape(N // P, P, K)

    def cols(v):
        return v.reshape(-1, P).T

    n_main = N_TILES - len(WIDE)
    w_main = np.zeros((n_main, P, 1024), f32)
    w_fused = np.zeros((DEPTH * 4 * C, P, 1280), f32)
    ada = np.concatenate([blocks(a["w_ada"][l]) for l in range(DEPTH)])
    at = 0
    heads = np.r_[0:64, 128:192, 64:128, 192:256]
    for p in PHASES:
        if p.kind == "ada":
            w_main[at:at + p.tiles] = ada[p.m:p.m + p.tiles]
            at += p.tiles
        elif p.kind == "up":
            w1, w3 = (blocks(a[f"ffn{p.ffn + 1}_{w}"][p.l]) for w in ("w1", "w3"))
            fb = sum(THIRDS[:p.third]) + p.f0
            for i in range(p.iters):
                for s in range(2):
                    for w in (w1, w3):
                        if p.ada:
                            w_main[at] = ada[p.m + 4 * i + 2 * s + (w is w3)]
                            at += 1
                        w_main[at] = w[fb + 2 * i + s]
                        at += 1
        elif p.kind == "down":
            r0 = P * sum(THIRDS[:p.third])
            k = P * THIRDS[p.third]
            w_main[at:at + C, :, 0:k] = blocks(a[f"ffn{p.ffn + 1}_w2"][p.l][r0:r0 + k])
            at += C
        elif p.kind == "mix":
            w = blocks(a["w_in"][p.l])
            q = a["w_in"][p.l][:, 768:1024][:, heads]
            w[6:8] = blocks(q)
            w_main[at:at + 10] = w[0:10]
            w_main[at + 10:at + 16] = w[16:22]
            w_main[at + 16:at + 22] = w[10:16]
            at += N_PROJ
            for i, br in enumerate(BRANCH_ORDER):
                wb = a["w_branch"][p.l, br]
                if br == 1:
                    wb = wb[heads]
                dst = w_fused[4 * C * p.l + C * i:4 * C * p.l + C * (i + 1)]
                dst[:, :, 0:1024] = w[22 + C * br:22 + C * (br + 1)]
                dst[:, :, 1024:] = blocks(wb)
            wo = blocks(a["w_out"][p.l])
            done = set()
            for step in mix_plan():
                if step[0] in ("moda", "out") and step[:2] not in done:
                    done.add(step[:2])
                    w_main[at] = wo[step[1]] if step[0] == "out" else ada[p.m + step[1]]
                    at += 1
    assert at == n_main

    consts, dft, rope, zt = shape_constants()
    v = np.zeros((P, V_COLS), f32)
    v[:, V_COND:V_COND + 2 * C] = np.stack([cols(a["c_ctx"]), cols(a["c"][0])], 2).reshape(P, 2 * C)
    lam = np.zeros((P, DEPTH * 128), f32)
    mlp_w = np.zeros((DEPTH, 64, 128), f32)
    d_row = np.arange(4)[None, :] - np.arange(4)[:, None] + WIN_R - 1
    d_col = np.clip(np.arange(GRID_W)[None, :] - np.arange(GRID_W)[:, None] + WIN_C - 1, 0, 2 * WIN_C - 2)
    bias = np.zeros((DEPTH, P, 2, 4, 256), f32)
    kctx = np.zeros((DEPTH, P, 5, P), f32)
    vctx = np.zeros((DEPTH, P, 640), f32)
    for l in range(DEPTH):
        v[:, V_BADA + 72 * l:V_BADA + 72 * (l + 1)] = cols(a["b_ada"][l])
        for i, nm in enumerate(("norm_ffn1", "norm_mix", "norm_ffn2")):
            v[:, V_NORM + 24 * l + 8 * i:V_NORM + 24 * l + 8 * (i + 1)] = cols(a[nm][l])
        short = np.stack([cols(a["hy_short_w"][l, i]) for i in range(3)] + [cols(a["hy_short_b"][l])], 2)
        v[:, V_SHORT + 24 * l:V_SHORT + 24 * (l + 1)] = short.reshape(P, 24)
        v[:, V_SKIP + 4 * l:V_SKIP + 4 * (l + 1)] = np.concatenate([cols(a["hy_skip"][l, o]) for o in range(2)], 1)
        for i, nm in enumerate(("hy_sin_freq", "hy_b1", "hy_b2")):
            v[0:64, V_MLP + 3 * l + i] = a[nm][l]
        v[:, V_SUBLN + l] = np.tile(a["diff_subln"][l], 2)
        v[:, V_SINK + 4 * l:V_SINK + 4 * (l + 1)] = a["swa_sink"][l][None, :]
        lam[:, 128 * l:128 * (l + 1)] = a["diff_lambda"][l].reshape(1, 128)
        mlp_w[l, 0:HY_EMB, 0:64], mlp_w[l, :, 64:128] = a["hy_w1"][l], a["hy_w2"][l]
        e = a["na_rpb"][l][:, d_row[:, None, :, None], d_col[None, :, None, :]]
        bias[l] = e.reshape(4, 2, P, 256).transpose(2, 1, 0, 3)
        kc = [a[f"cache_{nm}_k"][0, l].transpose(0, 2, 1).reshape(-1, P, PAST) for nm in ("na", "swa", "diff")]
        kctx[l] = np.concatenate(kc).transpose(1, 0, 2)
        vc = [a[f"cache_{nm}_v"][0, l].transpose(1, 0, 2).reshape(PAST, -1) for nm in ("na", "swa", "diff")]
        vctx[l] = np.concatenate(vc, 1)
    v[:, V_FIN:V_FIN + C] = cols(a["final_norm"])
    v[0, V_SEL] = v[1, V_SEL + 1] = v[2, V_SEL] = v[3, V_SEL + 1] = 1
    xs = np.concatenate([a["x_prompt"][0], a["x_sample"][0]], 0)
    x_in = xs.T.reshape(C, P, T).transpose(1, 0, 2).reshape(P, C * T)
    logdecay = np.broadcast_to(a["hy_log_decay"][:, None, :], (DEPTH, P, 1024))

    arrays = dict(w_main=w_main, w_fused=w_fused, consts=consts, vecs=v, lam=lam, x_in=x_in, rope=rope,
                  bias=bias.reshape(DEPTH, P, 2048), logdecay=logdecay, kctx=kctx, vctx=vctx,
                  mlp_w=mlp_w, mlp_w3=a["hy_w3"], zt=zt, dft=dft)
    arrays = {k: np.ascontiguousarray(w) for k, w in arrays.items()}
    nc = bacc.Bacc("TRN2", target_bir_lowering=False, num_devices=1)
    ins = [nc.dram_tensor(k, w.shape, mybir.dt.from_np(w.dtype), kind="ExternalInput").ap() for k, w in arrays.items()]
    y_out = nc.dram_tensor("y_out", (P, C * T), F32, kind="ExternalOutput").ap()
    kv = {}
    for nm, h in (("na", 4), ("swa", 2), ("diff", 4)):
        for w in "kv":
            kv[nm + w] = nc.dram_tensor(f"new_{nm}_{w}", (DEPTH, h, T_CTX, 64), F32, kind="ExternalOutput").ap()
    build(nc, *ins, y_out, [kv["nak"], kv["swak"], kv["diffk"]], [kv["nav"], kv["swav"], kv["diffv"]])
    r = run(nc, [arrays], core_ids=[0]).results[0]
    y = r["y_out"].reshape(P, C, T).transpose(2, 1, 0).reshape(T, D)
    return (y[None, 0:T_CTX], y[None, T_CTX:T], r["new_na_k"][None], r["new_na_v"][None], r["new_swa_k"][None],
            r["new_swa_v"][None], r["new_diff_k"][None], r["new_diff_v"][None])
```
